# Optimizing a Trainium2 kernel written in Bass

```python
import math
import jax
import jax.numpy as jnp
from jax import lax
import numpy as np

D_MODEL = 1024
BATCH = 1
SEQ = 256
DEPTH = 2

N_MIXERS = 4
N_CONV = (DEPTH + 3) // N_MIXERS
N_SGU = (DEPTH + 2) // N_MIXERS
N_GDN = (DEPTH + 1) // N_MIXERS
N_MLA = DEPTH // N_MIXERS
N_DENSE = (DEPTH + 1) // 2
N_MOE = DEPTH // 2

DEEPNORM_ALPHA = (2 * DEPTH) ** 0.25
DEEPNORM_BETA = (8 * DEPTH) ** -0.25

CONV_WIDTH = 31
SGU_CHUNK = 128
SGU_GROUPS = 8
SGU_HALF = 2 * D_MODEL
GDN_HEADS = 8
GDN_DK = 128
GDN_DV = 128
GDN_CONV = 4
GDN_CHUNK = 64
GDN_QKV = 2 * GDN_HEADS * GDN_DK + GDN_HEADS * GDN_DV
GDN_PROJ = GDN_QKV + GDN_HEADS * GDN_DV + 2 * GDN_HEADS
MLA_HEADS = 8
MLA_Q_RANK = 512
MLA_KV_RANK = 256
MLA_NOPE = 128
MLA_ROPE = 64
MLA_V = 128
ROPE_THETA = 10000.0
Q_BLOCK = 128
FFN_HIDDEN = 7 * D_MODEL // 2
N_EXPERTS = 8
TOP_K = 2
MOE_BLOCK = 256

kernel_name = "hybrid_conv_sgu_gdn_mla_moe_deepnorm_adaln"

def _layernorm(x, g, b, eps=1e-5):
    xf = x.astype(jnp.float32)
    mu = jnp.mean(xf, -1, keepdims=True)
    var = jnp.mean(jnp.square(xf - mu), -1, keepdims=True)
    return ((xf - mu) * lax.rsqrt(var + eps)).astype(x.dtype) * g + b

def _rmsnorm(x, g, eps=1e-6):
    xf = x.astype(jnp.float32)
    return (xf * lax.rsqrt(jnp.mean(xf * xf, -1, keepdims=True) + eps)).astype(x.dtype) * g

def _l2norm(x, eps=1e-6):
    xf = x.astype(jnp.float32)
    return xf * lax.rsqrt(jnp.sum(xf * xf, -1, keepdims=True) + eps)

def _causal_dwconv(x, w):
    k, ch = w.shape
    return lax.conv_general_dilated(
        x, w[:, None, :].astype(x.dtype), window_strides=(1,), padding=((k - 1, 0),),
        dimension_numbers=("NWC", "WIO", "NWC"), feature_group_count=ch)

def _rope(x, positions):
    half = x.shape[-1] // 2
    inv_freq = ROPE_THETA ** (-jnp.arange(half, dtype=jnp.float32) / half)
    ang = positions.astype(jnp.float32)[..., None, None] * inv_freq
    cos, sin = jnp.cos(ang).astype(x.dtype), jnp.sin(ang).astype(x.dtype)
    x1, x2 = x[..., :half], x[..., half:]
    return jnp.concatenate([x1 * cos - x2 * sin, x2 * cos + x1 * sin], -1)

def conformer_conv(h, w_in, dw, dw_b, ln_g, ln_b, w_out):
    a, g = jnp.split(h @ w_in, 2, -1)
    y = a * jax.nn.sigmoid(g)
    y = _causal_dwconv(y, dw) + dw_b
    y = jax.nn.silu(_layernorm(y, ln_g, ln_b))
    return y @ w_out

def chunked_spatial_gating(h, w_in, b_in, ln_g, ln_b, w_s, b_s, w_out):
    bsz, s, _ = h.shape
    z = jax.nn.gelu(h @ w_in + b_in, approximate=False)
    u, v = jnp.split(z, 2, -1)
    v = _layernorm(v, ln_g, ln_b)
    v = v.reshape(bsz, s // SGU_CHUNK, SGU_CHUNK, SGU_GROUPS, SGU_HALF // SGU_GROUPS)
    causal = jnp.tril(jnp.ones((SGU_CHUNK, SGU_CHUNK), dtype=bool))
    ws = jnp.where(causal, w_s, jnp.zeros((), w_s.dtype))
    sv = jnp.einsum("gts,bnsgd->bntgd", ws, v) + b_s.T[None, None, :, :, None]
    return (u * sv.reshape(bsz, s, SGU_HALF)) @ w_out

def _chunk_gated_delta(q, k, v, g, beta):
    bsz, s, nh, dk = q.shape
    dv = v.shape[-1]
    c = GDN_CHUNK
    n = s // c
    f32 = jnp.float32

    def chunks(t):
        t = t.astype(f32).reshape(bsz, n, c, nh, *t.shape[3:])
        return jnp.moveaxis(t, 3, 1)

    q, k, v, g, beta = (chunks(t) for t in (q, k, v, g, beta))
    gc = jnp.cumsum(g, -1)
    causal = jnp.tril(jnp.ones((c, c), dtype=bool))
    strict = jnp.tril(jnp.ones((c, c), dtype=bool), -1)
    diff = gc[..., :, None] - gc[..., None, :]
    decay = jnp.where(causal, jnp.exp(jnp.where(causal, diff, 0.0)), 0.0)
    kk = jnp.einsum("bhncd,bhnsd->bhncs", k, k)
    a = jnp.where(strict, beta[..., None] * kk * decay, 0.0)
    rhs = jnp.concatenate([v * beta[..., None], k * (beta * jnp.exp(gc))[..., None]], -1)
    sol = lax.linalg.triangular_solve(a + jnp.eye(c, dtype=f32), rhs, left_side=True,
                                      lower=True, unit_diagonal=True)
    u, w = jnp.split(sol, [dv], -1)
    qk = jnp.where(causal, jnp.einsum("bhncd,bhnsd->bhncs", q, k) * decay, 0.0)
    q_dec = q * jnp.exp(gc)[..., None]
    k_dec = k * jnp.exp(gc[..., -1:] - gc)[..., None]
    last = jnp.exp(gc[..., -1])

    def step(state, inp):
        q_i, k_i, u_i, w_i, qk_i, last_i = inp
        v_new = u_i - jnp.einsum("bhcd,bhde->bhce", w_i, state)
        o_i = jnp.einsum("bhcd,bhde->bhce", q_i, state) + jnp.einsum("bhcs,bhse->bhce", qk_i, v_new)
        state = state * last_i[..., None, None] + jnp.einsum("bhcd,bhce->bhde", k_i, v_new)
        return state, o_i

    xs = tuple(jnp.moveaxis(t, 2, 0) for t in (q_dec, k_dec, u, w, qk, last))
    _, o = lax.scan(step, jnp.zeros((bsz, nh, dk, dv), f32), xs)
    return jnp.transpose(o, (1, 0, 3, 2, 4)).reshape(bsz, s, nh, dv)

def gated_deltanet(h, w_in, conv_w, a_log, dt_bias, norm_g, w_out):
    bsz, s, _ = h.shape
    nh = GDN_HEADS
    qkv, z, b_raw, a_raw = jnp.split(
        h @ w_in, [GDN_QKV, GDN_QKV + nh * GDN_DV, GDN_QKV + nh * GDN_DV + nh], -1)
    qkv = jax.nn.silu(_causal_dwconv(qkv, conv_w))
    q, k, v = jnp.split(qkv, [nh * GDN_DK, 2 * nh * GDN_DK], -1)
    q = _l2norm(q.reshape(bsz, s, nh, GDN_DK)) * (GDN_DK ** -0.5)
    k = _l2norm(k.reshape(bsz, s, nh, GDN_DK))
    v = v.reshape(bsz, s, nh, GDN_DV)
    beta = jax.nn.sigmoid(b_raw.astype(jnp.float32))
    g = -jnp.exp(a_log.astype(jnp.float32)) * jax.nn.softplus(
        a_raw.astype(jnp.float32) + dt_bias.astype(jnp.float32))
    o = _chunk_gated_delta(q, k, v, g, beta).astype(h.dtype)
    o = _rmsnorm(o, norm_g) * jax.nn.silu(z.reshape(bsz, s, nh, GDN_DV))
    return o.reshape(bsz, s, nh * GDN_DV) @ w_out

def latent_attention(h, positions, w_in, q_norm_g, kv_norm_g, w_uq, w_ukv, w_out):
    bsz, s, _ = h.shape
    nh = MLA_HEADS
    c_q, c_kv, k_rope = jnp.split(h @ w_in, [MLA_Q_RANK, MLA_Q_RANK + MLA_KV_RANK], -1)
    q = (_rmsnorm(c_q, q_norm_g) @ w_uq).reshape(bsz, s, nh, MLA_NOPE + MLA_ROPE)
    kv = (_rmsnorm(c_kv, kv_norm_g) @ w_ukv).reshape(bsz, s, nh, MLA_NOPE + MLA_V)
    q_nope, q_rope = jnp.split(q, [MLA_NOPE], -1)
    k_nope, v = jnp.split(kv, [MLA_NOPE], -1)
    q_rope = _rope(q_rope, positions)
    k_rope = _rope(k_rope[:, :, None, :], positions)[:, :, 0]
    scale = (MLA_NOPE + MLA_ROPE) ** -0.5
    nb = s // Q_BLOCK
    qn_b = jnp.moveaxis(q_nope.reshape(bsz, nb, Q_BLOCK, nh, MLA_NOPE), 1, 0)
    qr_b = jnp.moveaxis(q_rope.reshape(bsz, nb, Q_BLOCK, nh, MLA_ROPE), 1, 0)
    key_idx = jnp.arange(s)

    def block(args):
        i, qn, qr = args
        sc = (jnp.einsum("bqhd,bkhd->bhqk", qn, k_nope)
              + jnp.einsum("bqhd,bkd->bhqk", qr, k_rope)).astype(jnp.float32) * scale
        q_idx = i * Q_BLOCK + jnp.arange(Q_BLOCK)
        sc = jnp.where(key_idx[None, :] <= q_idx[:, None], sc, -jnp.inf)
        p = jax.nn.softmax(sc, -1).astype(v.dtype)
        return jnp.einsum("bhqk,bkhd->bqhd", p, v)

    o = lax.map(block, (jnp.arange(nb), qn_b, qr_b))
    return jnp.moveaxis(o, 0, 1).reshape(bsz, s, nh * MLA_V) @ w_out

def swiglu(h, w_in, w_out):
    a, b = jnp.split(h @ w_in, 2, -1)
    return (jax.nn.silu(a) * b) @ w_out

def moe_swiglu(h, router, w_in, w_out):
    bsz, s, d = h.shape
    t = h.reshape(-1, d)
    n = t.shape[0]
    nk = n * TOP_K
    logits = (t @ router).astype(jnp.float32)
    top_logit, top_e = lax.top_k(logits, TOP_K)
    gate = jax.nn.softmax(top_logit, -1)
    flat_e = top_e.reshape(-1)
    flat_tok = jnp.repeat(jnp.arange(n, dtype=jnp.int32), TOP_K)
    flat_gate = gate.reshape(-1)
    order = jnp.argsort(flat_e)
    se, stok, sgate = flat_e[order], flat_tok[order], flat_gate[order]
    counts = jnp.bincount(flat_e, length=N_EXPERTS)
    start = jnp.cumsum(counts) - counts
    padded = (counts + MOE_BLOCK - 1) // MOE_BLOCK * MOE_BLOCK
    pend = jnp.cumsum(padded)
    pstart = pend - padded
    dest = pstart[se] + (jnp.arange(nk, dtype=jnp.int32) - start[se])
    n_blocks = (nk + N_EXPERTS * (MOE_BLOCK - 1) + MOE_BLOCK - 1) // MOE_BLOCK
    cap = n_blocks * MOE_BLOCK
    buf_tok = jnp.zeros((cap,), jnp.int32).at[dest].set(stok)
    buf_gate = jnp.zeros((cap,), jnp.float32).at[dest].set(sgate)
    block_e = jnp.clip(jnp.searchsorted(pend, jnp.arange(n_blocks) * MOE_BLOCK, side="right"),
                       0, N_EXPERTS - 1)
    xb = t[buf_tok].reshape(n_blocks, MOE_BLOCK, d)

    def expert_block(args):
        xe, e = args
        a, b = jnp.split(xe @ w_in[e], 2, -1)
        return (jax.nn.silu(a) * b) @ w_out[e]

    yb = lax.map(expert_block, (xb, block_e)).reshape(cap, d)
    y = jnp.zeros_like(t).at[buf_tok].add(yb * buf_gate[:, None].astype(yb.dtype))
    return y.reshape(bsz, s, d)

def _normal(key, shape, fan_in, scale=1.0):
    return jax.random.normal(key, shape, jnp.float32) * (scale * fan_in ** -0.5)

def _gain(key, shape):
    return 1.0 + 0.02 * jax.random.normal(key, shape, jnp.float32)

def _bias(key, shape, scale=0.02):
    return scale * jax.random.normal(key, shape, jnp.float32)

def setup_inputs(seed: int = 0) -> dict:
    key = jax.random.key(seed)
    ks = iter(jax.random.split(key, 64))
    D = D_MODEL
    beta = DEEPNORM_BETA
    dt = jnp.exp(jax.random.uniform(next(ks), (N_GDN, GDN_HEADS), jnp.float32,
                                    math.log(1e-3), math.log(1e-1)))
    return {
        "x": jax.random.normal(next(ks), (BATCH, SEQ, D), jnp.float32),
        "c": jax.random.normal(next(ks), (BATCH, D), jnp.float32),
        "positions": jnp.arange(SEQ, dtype=jnp.int32)[None, :]
        + jax.random.randint(next(ks), (BATCH, 1), 0, 1024, dtype=jnp.int32),
        "ada_w": _normal(next(ks), (DEPTH, D, 6 * D), D, 0.1),
        "ada_b": _bias(next(ks), (DEPTH, 6 * D), 0.01),
        "ln_g": _gain(next(ks), (DEPTH, 2, D)),
        "ln_b": _bias(next(ks), (DEPTH, 2, D)),
        "conv_w_in": _normal(next(ks), (N_CONV, D, 2 * D), D),
        "conv_dw": _normal(next(ks), (N_CONV, CONV_WIDTH, D), CONV_WIDTH),
        "conv_dw_b": _bias(next(ks), (N_CONV, D)),
        "conv_ln_g": _gain(next(ks), (N_CONV, D)),
        "conv_ln_b": _bias(next(ks), (N_CONV, D)),
        "conv_w_out": _normal(next(ks), (N_CONV, D, D), D, beta),
        "sgu_w_in": _normal(next(ks), (N_SGU, D, 2 * SGU_HALF), D),
        "sgu_b_in": _bias(next(ks), (N_SGU, 2 * SGU_HALF)),
        "sgu_ln_g": _gain(next(ks), (N_SGU, SGU_HALF)),
        "sgu_ln_b": _bias(next(ks), (N_SGU, SGU_HALF)),
        "sgu_w_s": _normal(next(ks), (N_SGU, SGU_GROUPS, SGU_CHUNK, SGU_CHUNK), SGU_CHUNK),
        "sgu_b_s": _gain(next(ks), (N_SGU, SGU_GROUPS, SGU_CHUNK)),
        "sgu_w_out": _normal(next(ks), (N_SGU, SGU_HALF, D), SGU_HALF, beta),
        "gdn_w_in": _normal(next(ks), (N_GDN, D, GDN_PROJ), D),
        "gdn_conv": _normal(next(ks), (N_GDN, GDN_CONV, GDN_QKV), GDN_CONV),
        "gdn_a_log": jnp.log(jax.random.uniform(next(ks), (N_GDN, GDN_HEADS), jnp.float32, 1.0, 16.0)),
        "gdn_dt_bias": dt + jnp.log(-jnp.expm1(-dt)),
        "gdn_norm_g": _gain(next(ks), (N_GDN, GDN_DV)),
        "gdn_w_out": _normal(next(ks), (N_GDN, GDN_HEADS * GDN_DV, D), GDN_HEADS * GDN_DV, beta),
        "mla_w_in": _normal(next(ks), (N_MLA, D, MLA_Q_RANK + MLA_KV_RANK + MLA_ROPE), D),
        "mla_q_norm_g": _gain(next(ks), (N_MLA, MLA_Q_RANK)),
        "mla_kv_norm_g": _gain(next(ks), (N_MLA, MLA_KV_RANK)),
        "mla_w_uq": _normal(next(ks), (N_MLA, MLA_Q_RANK, MLA_HEADS * (MLA_NOPE + MLA_ROPE)), MLA_Q_RANK),
        "mla_w_ukv": _normal(next(ks), (N_MLA, MLA_KV_RANK, MLA_HEADS * (MLA_NOPE + MLA_V)), MLA_KV_RANK),
        "mla_w_out": _normal(next(ks), (N_MLA, MLA_HEADS * MLA_V, D), MLA_HEADS * MLA_V, beta),
        "ffn_w_in": _normal(next(ks), (N_DENSE, D, 2 * FFN_HIDDEN), D),
        "ffn_w_out": _normal(next(ks), (N_DENSE, FFN_HIDDEN, D), FFN_HIDDEN, beta),
        "moe_router": _normal(next(ks), (N_MOE, D, N_EXPERTS), D),
        "moe_w_in": _normal(next(ks), (N_MOE, N_EXPERTS, D, 2 * FFN_HIDDEN), D),
        "moe_w_out": _normal(next(ks), (N_MOE, N_EXPERTS, FFN_HIDDEN, D), FFN_HIDDEN, beta),
    }

def reference(x, c, positions, ada_w, ada_b, ln_g, ln_b,
              conv_w_in, conv_dw, conv_dw_b, conv_ln_g, conv_ln_b, conv_w_out,
              sgu_w_in, sgu_b_in, sgu_ln_g, sgu_ln_b, sgu_w_s, sgu_b_s, sgu_w_out,
              gdn_w_in, gdn_conv, gdn_a_log, gdn_dt_bias, gdn_norm_g, gdn_w_out,
              mla_w_in, mla_q_norm_g, mla_kv_norm_g, mla_w_uq, mla_w_ukv, mla_w_out,
              ffn_w_in, ffn_w_out, moe_router, moe_w_in, moe_w_out):
    cond = jax.nn.silu(c)
    for i in range(DEPTH):
        mod = (cond @ ada_w[i] + ada_b[i])[:, None, :]
        sh1, sc1, g1, sh2, sc2, g2 = jnp.split(mod, 6, -1)
        h = x * (1 + sc1) + sh1
        j = i // N_MIXERS
        mixer = i % N_MIXERS
        if mixer == 0:
            y = conformer_conv(h, conv_w_in[j], conv_dw[j], conv_dw_b[j], conv_ln_g[j],
                               conv_ln_b[j], conv_w_out[j])
        elif mixer == 1:
            y = chunked_spatial_gating(h, sgu_w_in[j], sgu_b_in[j], sgu_ln_g[j], sgu_ln_b[j],
                                       sgu_w_s[j], sgu_b_s[j], sgu_w_out[j])
        elif mixer == 2:
            y = gated_deltanet(h, gdn_w_in[j], gdn_conv[j], gdn_a_log[j], gdn_dt_bias[j],
                               gdn_norm_g[j], gdn_w_out[j])
        else:
            y = latent_attention(h, positions, mla_w_in[j], mla_q_norm_g[j], mla_kv_norm_g[j],
                                 mla_w_uq[j], mla_w_ukv[j], mla_w_out[j])
        x = _layernorm(DEEPNORM_ALPHA * x + (1 + g1) * y, ln_g[i, 0], ln_b[i, 0])
        h = x * (1 + sc2) + sh2
        if i % 2 == 0:
            y = swiglu(h, ffn_w_in[i // 2], ffn_w_out[i // 2])
        else:
            y = moe_swiglu(h, moe_router[i // 2], moe_w_in[i // 2], moe_w_out[i // 2])
        x = _layernorm(DEEPNORM_ALPHA * x + (1 + g2) * y, ln_g[i, 1], ln_b[i, 1])
    return x


_drawn_inputs = setup_inputs


def setup_inputs(seed=0):
    import zlib

    import numpy as np

    out = dict(_drawn_inputs(seed))
    spreads = {}
    factors = {'ada_b': 3.651,
     'conv_dw_b': 3.441,
     'conv_ln_g': 4.042,
     'conv_ln_b': 8.0,
     'sgu_b_in': 5.098,
     'sgu_ln_g': 6.448,
     'sgu_ln_b': 4.722,
     'sgu_b_s': 4.817}
    for name, (base, spread) in spreads.items():
        noise = np.random.default_rng([zlib.crc32(name.encode()), seed]).standard_normal(out[name].shape)
        drawn = base * np.exp(spread * noise) if base else spread * noise
        out[name] = jnp.asarray(drawn.astype(out[name].dtype))
    for name, factor in factors.items():
        out[name] = (out[name] * factor).astype(out[name].dtype)
    return out
```

```python
from contextlib import ExitStack

import concourse.bass as bass
from concourse import mybir

ALU = mybir.AluOpType
ACT = mybir.ActivationFunctionType
F32 = mybir.dt.float32
F32R = mybir.dt.float32r
I32 = mybir.dt.int32
U32 = mybir.dt.uint32

P = 128
BANK = 512
SLOTS = 7
UNIT = 2048
HALF = UNIT // 2


def hybrid_trunk(nc, x, c, ada_w, ada_b, ln_g, ln_b, conv_w_in, conv_dw, conv_dw_b, conv_ln_g,
                 conv_ln_b, conv_w_out, sgu_w_in, sgu_b_in, sgu_ln_g, sgu_ln_b, sgu_w_s, sgu_b_s,
                 sgu_w_out, ffn_w_in, ffn_w_out, moe_router, moe_w_in, moe_w_out, out):
    _, S, D = x.shape
    NT = S // P
    KC = D // P
    F = ffn_w_out.shape[1]
    NJ = F // BANK
    FC = F // P
    E = moe_router.shape[2]
    TAPS = conv_dw.shape[1]
    PADL = TAPS - 1
    HS = sgu_w_out.shape[1]
    HC = HS // P
    G = sgu_w_s.shape[1]
    GW = HS // G
    DEPTH = ada_w.shape[0]
    ALPHA = (2 * DEPTH) ** 0.25
    SEG = 6
    ADB = SEG * D // BANK
    NCOL = E + 4
    INU = 4 * NJ
    OUTU = FC // 2
    FFU = INU + OUTU
    DVE_CH = KC // 2
    assert NT == 2 and KC == 8 and FC % 4 == 0 and FFU % SLOTS == 0 and SEG * D // P == 48

    def in_unit(w, col, kh):
        return w.rearrange("(k p) n -> p k n", p=P)[:, 4 * kh:4 * kh + 4, col:col + BANK]

    def out_unit(w, m):
        return w.rearrange("(k p) n -> p k n", p=P)[:, 2 * m:2 * m + 2, :]

    units, ada_at, split_at = [], [], []

    def add_ada(layer, b):
        for kh in range(2):
            ada_at.append(len(units))
            units.append(("ada", len(ada_at) - 1, in_unit(ada_w[layer], b * BANK, kh)))

    def add_split(ap):
        split_at.append(len(units))
        units.append(("split", len(split_at) - 1, ap))

    for b in range(4):
        add_ada(0, b)
    for blk in range(2):
        for col in (D, 0):
            for kh in range(2):
                add_split(in_unit(conv_w_in[0], col + blk * BANK, kh))
    for b in range(4, ADB):
        add_ada(0, b)
    CONV_OUT = len(split_at)
    for m in range(KC // 2):
        add_split(out_unit(conv_w_out[0], m))
    FFN = len(split_at)
    for u in range(INU):
        j, part, kh = u // 4, (u % 4) // 2, u % 2
        add_split(in_unit(ffn_w_in[0], part * F + j * BANK, kh))
        if u % 2 and u // 2 < ADB:
            add_ada(1, u // 2)
    for m in range(OUTU):
        add_split(out_unit(ffn_w_out[0], m))
    SGU = len(split_at)
    for q in range(8):
        for kh in range(2):
            add_split(in_unit(sgu_w_in[0], (HS + q * BANK) if q < 4 else (q - 4) * BANK, kh))
    SGU_OUT = len(split_at)
    for m in range(HC // 2):
        add_split(out_unit(sgu_w_out[0], m))
    MOE = len(split_at)
    MOE_AT = len(units)
    assert MOE_AT % SLOTS == 0 and MOE % 2 == 0

    with ExitStack() as ctx:
        def sem(name):
            return ctx.enter_context(nc.semaphore(name))

        def sb(name, shape, dt=F32):
            return ctx.enter_context(nc.sbuf_tensor(name, shape, dt))

        ring = sb("ring", [P, SLOTS, UNIT])
        w_hi = sb("w_hi", [P, 4, HALF], F32R)
        w_lo = sb("w_lo", [P, 4, HALF], F32R)
        xs = sb("xs", [P, NT, D])
        g1row = sb("g1row", [P, D])
        g2row = sb("g2row", [P, 2, D])
        lng = sb("lng", [P, D])
        lnb = sb("lnb", [P, D])
        ident = sb("ident", [P, P])
        ones = sb("ones", [P, P])
        sel4 = sb("sel4", [P, P])
        tri = sb("tri", [P, P])
        iota = sb("iota", [P, P])
        vcols = sb("vcols", [P, P])
        modb = sb("modb", [P, 96])
        mods = sb("mods", [P, 2, SEG, KC])
        csil = sb("csil", [P, KC, 32])
        modrow = sb("modrow", [P, BANK])
        wsT = sb("wsT", [P, G, P])
        bsT = sb("bsT", [P, G])
        router = sb("router", [P, KC, E])
        stats = sb("stats", [P, NT, 4, 6])
        mv = sb("mv", [P, NT, 2])
        var = sb("var", [P, NT])
        dev = sb("dev", [P, NT])
        rstd = sb("rstd", [P, NT])
        ps = ctx.enter_context(nc.psum_tensor("ps", [P, 8, BANK], F32))

        ARENA = 80
        sb("arena", [P, ARENA * 256])
        base = nc.sbuf_base - ARENA * 1024

        def at(kib, name, shape, dt=F32):
            return nc.alloc_sbuf_tensor_at(name, shape, dt, offset=int(base + kib * 1024))

        hT_hi = at(0, "hT_hi", [P, KC, S], F32R)
        hT_lo = at(8, "hT_lo", [P, KC, S], F32R)
        ztmp = at(16, "ztmp", [P, D])
        h32 = at(16, "h32", [P, KC, S])
        ypad = at(24, "ypad", [P, KC, PADL + S])
        ycv = at(34, "ycv", [P, KC, S])
        ysq = at(42, "ysq", [P, KC, S])
        y_hi = at(50, "y_hi", [P, KC, S], F32R)
        y_lo = at(58, "y_lo", [P, KC, S], F32R)
        sig = at(66, "sig", [P, 4, S])
        dwT = at(70, "dwT", [P, KC, TAPS])
        diag = at(71, "diag", [P, 8, P])
        cst = at(75, "cst", [P, 4, S])
        vecs = at(42, "vecs", [P, P])
        iota_i = at(42.5, "iota_i", [P, P], I32)
        dwrow = at(43, "dwrow", [TAPS, D])
        bsrow = at(47, "bsrow", [G, P])
        wsr = at(50, "wsr", [P, G, P])
        wsm = at(54, "wsm", [P, G, P])
        f_sil = at(16, "f_sil", [P, NT, BANK])
        f_hid = at(20, "f_hid", [P, NT, BANK])
        hid_hi = at(24, "hid_hi", [P, FC, S], F32R)
        hid_lo = at(52, "hid_lo", [P, FC, S], F32R)
        vv = at(24, "vv", [P, NT, HS])
        uu = at(40, "uu", [P, NT, HS])
        s_lng = at(56, "s_lng", [P, HS])
        s_lnb = at(64, "s_lnb", [P, HS])
        brow = at(72, "brow", [P, 2, BANK])
        uT_hi = at(0, "uT_hi", [P, HC, S], F32R)
        uT_lo = at(56, "uT_lo", [P, HC, S], F32R)
        acc = at(0, "acc", [P, NT, D])
        oneh = at(8, "oneh", [P, NT, P])
        ggate = at(9, "ggate", [P, NT, P])
        ggT = at(10, "ggT", [P, NT, P])
        xe32 = at(24, "xe32", [P, KC, P])
        xe_hi = at(28, "xe_hi", [P, KC, P], F32R)
        xe_lo = at(32, "xe_lo", [P, KC, P], F32R)
        eh_hi = at(36, "eh_hi", [P, FC, P], F32R)
        eh_lo = at(50, "eh_lo", [P, FC, P], F32R)
        ye = at(64, "ye", [P, D])
        e_sil = at(68, "e_sil", [P, 1, BANK])
        e_hid = at(70, "e_hid", [P, 1, BANK])
        small_at = [11 * 1024]

        def small(name, cols, dt=F32):
            t = nc.alloc_sbuf_tensor_at(name, [P, *cols], dt, offset=base + small_at[0])
            n = 4
            for d in cols:
                n *= d
            small_at[0] += (n + 31) // 32 * 32
            assert small_at[0] <= 16 * 1024
            return t

        lgt = small("lgt", [NT, E])
        top = small("top", [NT, 8])
        topi = small("topi", [NT, 8], U32)
        topf = small("topf", [NT, 8])
        tdif = small("tdif", [NT, 1])
        tgate = small("tgate", [NT, 2])
        mask1 = small("mask1", [NT, E])
        mask2 = small("mask2", [NT, E])
        mask = small("mask", [NT, E])
        gate1 = small("gate1", [NT, E])
        gate = small("gate", [NT, E])
        rank1 = small("rank1", [NT, E])
        excess = small("excess", [NT, E])
        over = small("over", [4, 2 * E])
        before = small("before", [E])
        oh = small("oh", [4, E])
        junk = small("junk", [E])
        dest = small("dest", [NT, NCOL])
        gcol = small("gcol", [NT, NCOL])
        meta = small("meta", [8])
        metai = small("metai", [8], I32)

        landed = [sem(f"landed{i}") for i in range(SLOTS)]
        x_landed, vec_landed, misc_landed = sem("x_landed"), sem("vec_landed"), sem("misc_landed")
        rows_landed, gb_landed = sem("rows_landed"), sem("gb_landed")
        sln_landed = sem("sln_landed")
        brow_landed = [sem("brow_landed0"), sem("brow_landed1")]
        stored = sem("stored")
        consts, pool_step, ws_masked = sem("consts"), sem("pool_step"), sem("ws_masked")
        hi_ready, lo_ready, half_used = sem("hi_ready"), sem("lo_ready"), sem("half_used")
        ada_used, ada_copied, ada_sums, ada_out = sem("ada_used"), sem("ada_copied"), sem("ada_sums"), sem("ada_out")
        vec_ps, vec_out, ws_ps, ws_out = sem("vec_ps"), sem("vec_out"), sem("ws_ps"), sem("ws_out")
        csil_ready, modb_ready, iota_ready = sem("csil_ready"), sem("modb_ready"), sem("iota_ready")
        pad_zero = sem("pad_zero")
        xT_ps, h32_out, h_ready = sem("xT_ps"), sem("h32_out"), sem("h_ready")
        sig_out, glu_out, diag_ready, diag_used = sem("sig_out"), sem("glu_out"), sem("diag_ready"), sem("diag_used")
        taps_out, dconv_out = sem("taps_out"), sem("dconv_out")
        mean_ps, centred, squared, var_ps, cvar, cdev, normed, cact, y_ready = (
            sem(n) for n in ("mean_ps", "centred", "squared", "var_ps", "cvar", "cdev", "normed", "cact", "y_ready"))
        var_ready, dev_ready, x_ready = sem("var_ready"), sem("dev_ready"), sem("x_ready")
        silu_out, hid_out, hidT_ps, hidT_hi, hidT_lo = (
            sem(n) for n in ("silu_out", "hid_out", "hidT_ps", "hidT_hi", "hidT_lo"))
        zb_out, gelu_out, vvar, vdev, v_ready, sv_ps, gated, uT_ps, uT_hi_out, uT_lo_out = (
            sem(n) for n in ("zb_out", "gelu_out", "vvar", "vdev", "v_ready", "sv_ps", "gated", "uT_ps",
                             "uT_hi_out", "uT_lo_out"))
        logit_ps, mdif, mgate, mask_ready, rank_ps, meta_ready = (
            sem(n) for n in ("logit_ps", "mdif", "mgate", "mask_ready", "rank_ps", "meta_ready"))
        pick_ready, picked_ps, xe32_out, xe_ready = (
            sem(n) for n in ("pick_ready", "picked_ps", "xe32_out", "xe_ready"))
        ggT_ps, ggT_out, ye_ready, spread_ps, acc_out = (
            sem(n) for n in ("ggT_ps", "ggT_out", "ye_ready", "spread_ps", "acc_out"))
        dve_step, dve_turn, dve_last = sem("dve_step"), sem("dve_turn"), sem("dve_last")

        XB = (4, 2)
        YB = (6, 0)

        def flat(t):
            return t.rearrange("p a b -> p (a b)")

        def tok(t):
            return slice(t * P, (t + 1) * P)

        def wait_landed(eng, pos):
            eng.wait_ge(landed[pos % SLOTS], 16 * (pos // SLOTS + 1))

        block = ctx.enter_context(nc.Block())

        @block.sync
        def _(sp):
            for pos, (kind, n, src) in enumerate(units):
                if pos >= SLOTS:
                    k0, n0, _ = units[pos - SLOTS]
                    if k0 == "ada":
                        sp.wait_ge(ada_used, n0 + 1)
                    else:
                        sp.wait_ge(lo_ready, 2 * n0 + 2)
                dst = ring[:, pos % SLOTS, :].rearrange("p (k n) -> p k n", k=src.shape[1])
                sp.dma_start(dst, src).then_inc(landed[pos % SLOTS], 16)

            w_in = moe_w_in[0].rearrange("e (k p) n -> e p k n", p=P)
            w_out = moe_w_out[0].rearrange("e (k p) n -> e p k n", p=P)

            def expert(e, i):
                for u in range(FFU):
                    sp.wait_ge(lo_ready, i * (2 * FFU) + (2 * (MOE + u - SLOTS) + 2))
                    if u < INU:
                        j, part, kh = u // 4, (u % 4) // 2, u % 2
                        src = w_in[bass.ds(e, 1), :, 4 * kh:4 * kh + 4, part * F + j * BANK:part * F + (j + 1) * BANK]
                    else:
                        src = w_out[bass.ds(e, 1), :, 2 * (u - INU):2 * (u - INU) + 2, :]
                    k = src.shape[2]
                    src = src.rearrange("e p k n -> (e p) k n")
                    dst = ring[:, u % SLOTS, :].rearrange("p (k n) -> p k n", k=k)
                    sp.dma_start(dst, src).then_inc(landed[u % SLOTS], 16)

            with sp.Fori(0, E) as i:
                expert(i, i)
            sp.wait_ge(meta_ready, 1)
            items = sp.value_load(metai[0:1, 4:5], min_val=E, max_val=NCOL - 1)
            with sp.If(items > E):
                with sp.Fori(E, items) as i:
                    e = sp.value_load(metai[0:1, bass.ds(i - E, 1)], min_val=0, max_val=E - 1)
                    expert(e, i)
                sp.nop()
            for t in range(NT):
                sp.wait_ge(x_ready, 2 * 3 + t + 1)
                sp.dma_start(out[0, tok(t), :], xs[:, t, :]).then_inc(stored, 16)
            sp.wait_ge(stored, 16 * NT)

        @block.gpsimd
        def _(pool):
            flatrow = lambda v, n: v.rearrange("(j p) -> j p", p=P)
            pool.dma_start(dwrow[:, :], conv_dw[0]).then_inc(misc_landed, 16)
            pool.dma_start(bsrow[:, :], sgu_b_s[0]).then_inc(misc_landed, 16)
            pool.dma_start(wsr[:, :, :], sgu_w_s[0].rearrange("g t s -> t g s")).then_inc(misc_landed, 16)
            pool.dma_start(router[:, :, :], moe_router[0].rearrange("(k p) e -> p k e", p=P)).then_inc(misc_landed, 16)
            pool.memset(ident[:, :], 0.0).then_inc(pool_step, 1)
            pool.memset(ones[:, :], 1.0).then_inc(pool_step, 1)
            pool.memset(tri[:, :], 0.0).then_inc(pool_step, 1)
            pool.memset(sel4[:, :], 0.0).then_inc(pool_step, 1)
            pool.iota(iota_i[:, :], pattern=[[1, P]], base=0, channel_multiplier=0).then_inc(pool_step, 1)
            pool.wait_ge(pool_step, 5)
            pool.affine_select(out=ident[:, :], in_=ident[:, :], compare_op=ALU.not_equal, fill=1.0, base=0,
                               pattern=[[-1, P]], channel_multiplier=1).then_inc(consts, 1)
            pool.affine_select(out=tri[:, :], in_=tri[:, :], compare_op=ALU.is_ge, fill=1.0, base=0,
                               pattern=[[-1, P]], channel_multiplier=1).then_inc(consts, 1)
            for row, seg, layer in ((g1row[:, :], 2, 0), (g2row[:, 0, :], 5, 0), (g2row[:, 1, :], 5, 1)):
                pool.dma_start(row, ada_b[layer, seg * D:(seg + 1) * D].partition_broadcast(P)).then_inc(gb_landed, 16)
            pool.dma_start(lng[:, :], ln_g[0, 0].partition_broadcast(P)).then_inc(rows_landed, 16)
            pool.dma_start(lnb[:, :], ln_b[0, 0].partition_broadcast(P)).then_inc(rows_landed, 16)
            pool.wait_ge(misc_landed, 64)
            pool.affine_select(out=wsm[:, :, :], in_=wsr[:, :, :], compare_op=ALU.is_ge, fill=0.0, base=0,
                               pattern=[[0, G], [-1, P]], channel_multiplier=1).then_inc(ws_masked, 1)
            pool.wait_ge(vec_out, 2)
            for n in range((KC - DVE_CH) * TAPS):
                ch, k = DVE_CH + n // TAPS, n % TAPS
                if n >= 8:
                    pool.wait_ge(diag_used, n - 7)
                pool.tensor_scalar(diag[:, n % 8, :], ident[:, :], dwT[:, ch, k:k + 1], None,
                                   ALU.mult).then_inc(diag_ready, 1)

            def norm_rows(q):
                pool.wait_ge(x_ready, 2 * q)
                pool.dma_start(lng[:, :], ln_g[q // 2, q % 2].partition_broadcast(P)).then_inc(rows_landed, 16)
                pool.dma_start(lnb[:, :], ln_b[q // 2, q % 2].partition_broadcast(P)).then_inc(rows_landed, 16)

            norm_rows(1)
            pool.dma_start(g1row[:, :], ada_b[1, 2 * D:3 * D].partition_broadcast(P)).then_inc(gb_landed, 16)
            norm_rows(2)
            pool.dma_start(s_lng[:, :], sgu_ln_g[0].partition_broadcast(P)).then_inc(sln_landed, 16)
            pool.dma_start(s_lnb[:, :], sgu_ln_b[0].partition_broadcast(P)).then_inc(sln_landed, 16)
            for q in range(8):
                if q >= 2:
                    pool.wait_ge(zb_out, q - 1)
                col = HS + q * BANK if q < 4 else (q - 4) * BANK
                pool.dma_start(brow[:, q % 2, :], sgu_b_in[0, col:col + BANK].partition_broadcast(P))\
                    .then_inc(brow_landed[q % 2], 16)
            norm_rows(3)

        @block.tensor
        def _(pe):
            def three(o, a_hi, a_lo, b_hi, b_lo, start, stop):
                nc.tensor.matmul(o, a_hi, b_hi, start=start, stop=False)
                nc.tensor.matmul(o, a_hi, b_lo, start=False, stop=False)
                return nc.tensor.matmul(o, a_lo, b_hi, start=False, stop=stop)

            def ada_rows(n, bank):
                if n:
                    pe.wait_ge(ada_copied, n)
                for kh in range(2):
                    pos = ada_at[2 * n + kh]
                    wait_landed(pe, pos)
                    for g in range(4):
                        mm = nc.tensor.matmul(ps[32 * g:32 * g + 32, bank, :], csil[:, 4 * kh + g, :],
                                              ring[:, pos % SLOTS, g * BANK:(g + 1) * BANK],
                                              start=(kh == 0), stop=(kh == 1), skip_group_check=True)
                    mm.then_inc(ada_used, 1)

            def ada_finish(n, bank):
                b = n % ADB
                pe.wait_ge(ada_copied, n + 1)
                if b // 2 in (2, 5):
                    mm = nc.tensor.matmul(ps[:, bank, :], sel4[:, :], modrow[:, :], start=True, stop=True)
                else:
                    for j in range(4):
                        mm = nc.tensor.matmul(ps[:, bank, 4 * b + j:4 * b + j + 1], modrow[:, tok(j)],
                                              sel4[:, 0:1], start=True, stop=True)
                mm.then_inc(ada_sums, 1)

            def turn_x(q, t):
                if q:
                    pe.wait_ge(x_ready, 2 * (q - 1) + t + 1)
                for k in range(KC):
                    mm = nc.tensor.transpose(ps[:, XB[t] + k // 4, (k % 4) * P:(k % 4 + 1) * P],
                                             xs[:, t, tok(k)], ident[:, :])
                mm.then_inc(xT_ps, 1)

            def out_unit_rows(h, hb, a_hi, a_lo, kc, nt, first, last):
                pe.wait_ge(lo_ready, h + 1)
                for t in range(nt):
                    for dh in range(2):
                        mm = three(ps[:, YB[t] + dh, :], a_hi[:, kc, tok(t)], a_lo[:, kc, tok(t)],
                                   w_hi[:, hb, dh * BANK:(dh + 1) * BANK], w_lo[:, hb, dh * BANK:(dh + 1) * BANK],
                                   first, last)
                mm.then_inc(half_used, 1)

            def in_unit_rows(h, hb, a_hi, a_lo, k0, nt, bank):
                pe.wait_ge(lo_ready, h + 1)
                for t in range(nt):
                    for kk in range(2):
                        k = k0 + kk
                        mm = three(ps[:, bank + t, :], a_hi[:, k, tok(t)], a_lo[:, k, tok(t)],
                                   w_hi[:, hb, kk * BANK:(kk + 1) * BANK], w_lo[:, hb, kk * BANK:(kk + 1) * BANK],
                                   k == 0, k == KC - 1)
                mm.then_inc(half_used, 1)

            def swiglu(h0, c0, nt, a_hi, a_lo, hid, e_hi, e_lo, after):
                for u in range(FFU):
                    j, b_part, kh = u // 4, (u % 4) // 2, u % 2
                    if u < INU:
                        if kh == 0:
                            pe.wait_ge(hid_out if b_part else silu_out, c0 + j)
                        for s in range(2):
                            in_unit_rows(h0 + (2 * u + s), (2 * u + s) % 4, a_hi, a_lo, 4 * kh + 2 * s, nt,
                                         2 * b_part)
                    else:
                        for s in range(2):
                            kc = 2 * (u - INU) + s
                            if kc % 4 == 0:
                                pe.wait_ge(hidT_lo, c0 + (kc // 4 + 1))
                            if u == INU and s == 0:
                                pe.wait_ge(silu_out, c0 + NJ)
                            out_unit_rows(h0 + (2 * u + s), (2 * u + s) % 4, e_hi, e_lo, kc, nt,
                                          kc == 0, kc == FC - 1)
                    if u % 4 == 1 and 5 <= u <= INU + 1:
                        j = (u - 5) // 4
                        pe.wait_ge(hid_out, c0 + (j + 1))
                        pe.wait_ge(hidT_lo, c0 + j)
                        for t in range(nt):
                            for f in range(4):
                                mm = nc.tensor.transpose(ps[:, 4 + t, f * P:(f + 1) * P], hid[:, t, tok(f)],
                                                         ident[:, :])
                        mm.then_inc(hidT_ps, 1)
                    after(u)

            pe.wait_ge(consts, 6)
            pe.wait_ge(vec_landed, 96)
            nc.tensor.transpose(ps[:, 6, 0:P], vecs[:, :], ident[:, :]).then_inc(vec_ps, 1)
            pe.wait_ge(misc_landed, 64)
            for k in range(KC):
                nc.tensor.transpose(ps[:, 5, TAPS * k:TAPS * (k + 1)], dwrow[:, tok(k)], ident[0:TAPS, 0:TAPS])
            nc.tensor.transpose(ps[:, 5, 256:256 + G], bsrow[:, :], ident[0:G, 0:G]).then_inc(vec_ps, 1)
            pe.wait_ge(ws_masked, 1)
            for g in range(G):
                mm = nc.tensor.transpose(ps[:, g // 4, (g % 4) * P:(g % 4 + 1) * P], wsm[:, g, :], ident[:, :])
            mm.then_inc(ws_ps, 1)
            pe.wait_ge(csil_ready, 1)
            pe.wait_ge(vec_out, 3)
            ada_rows(0, 6)
            pe.wait_ge(x_landed, 16)
            for t in range(NT):
                turn_x(0, t)
            for n in range(4):
                if n:
                    pe.wait_ge(ada_out, n)
                ada_finish(n, 7)
                if n < 3:
                    ada_rows(n + 1, 6)

            pe.wait_ge(h_ready, 2)
            pe.wait_ge(ws_out, 1)
            pe.wait_ge(ada_out, 4)
            for i in range(8):
                blk, part, kh = i // 4, (i % 4) // 2, i % 2
                if blk and kh == 0:
                    pe.wait_ge(glu_out if part else sig_out, 1)
                for s in range(2):
                    h = 2 * i + s
                    pe.wait_ge(lo_ready, h + 1)
                    for ch in range(4):
                        for kk in range(2):
                            k = 4 * kh + 2 * s + kk
                            w = slice(kk * BANK + ch * P, kk * BANK + (ch + 1) * P)
                            mm = three(ps[:, 4 * part + ch, 0:S], w_hi[:, h % 4, w], w_lo[:, h % 4, w],
                                       hT_hi[:, k, :], hT_lo[:, k, :], k == 0, k == KC - 1)
                    mm.then_inc(half_used, 1)
            pe.wait_ge(glu_out, 2)
            for ch in range(DVE_CH, KC):
                for half in range(2):
                    n = 4 + 2 * (ch - DVE_CH) + half
                    ada_rows(n, 0)
                    for k in (range(16) if half == 0 else range(16, TAPS)):
                        m = (ch - DVE_CH) * TAPS + k
                        pe.wait_ge(diag_ready, m + 1)
                        nc.tensor.matmul(ps[:, ch, 0:S], diag[:, m % 8, :], ypad[:, ch, k:k + S],
                                         start=(k == 0), stop=(k == TAPS - 1)).then_inc(diag_used, 1)
                    pe.wait_ge(ada_out, n - 2)
                    ada_finish(n, 1 + n % 3)
            pe.wait_ge(taps_out, DVE_CH)
            pe.wait_ge(dconv_out, KC - DVE_CH)
            for ch in range(KC):
                mm = nc.tensor.matmul(ps[:, 4, 0:S], ones[:, :], ycv[:, ch, :], start=(ch == 0), stop=(ch == KC - 1))
            mm.then_inc(mean_ps, 1)
            for ch in range(KC):
                if ch % 4 == 0:
                    pe.wait_ge(squared, ch // 4 + 1)
                mm = nc.tensor.matmul(ps[:, 5, 0:S], ones[:, :], ysq[:, ch, :], start=(ch == 0), stop=(ch == KC - 1))
            mm.then_inc(var_ps, 1)
            pe.wait_ge(ada_out, ADB)
            for m in range(KC // 2):
                for s in range(2):
                    kc = 2 * m + s
                    if kc % 4 == 0:
                        pe.wait_ge(y_ready, kc // 4 + 1)
                    h = 2 * (CONV_OUT + m) + s
                    out_unit_rows(h, h % 4, y_hi, y_lo, kc, NT, kc == 0, kc == KC - 1)

            for t in range(NT):
                turn_x(1, t)
            pe.wait_ge(h_ready, 4)

            def ada_between(u):
                if u < INU and u % 2 and u // 2 < ADB:
                    ada_rows(ADB + u // 2, 6)
                if u < INU and u % 2 == 0 and 1 <= u // 2 <= ADB:
                    n = ADB + u // 2 - 1
                    pe.wait_ge(ada_out, n)
                    ada_finish(n, 7)
                if u == INU - 1:
                    pe.wait_ge(ada_out, 2 * ADB)

            swiglu(2 * FFN, 0, NT, hT_hi, hT_lo, f_hid, hid_hi, hid_lo, ada_between)

            for t in range(NT):
                turn_x(2, t)
            pe.wait_ge(h_ready, 6)
            for i in range(16):
                q, kh = i // 2, i % 2
                if kh == 0 and q >= 2:
                    pe.wait_ge(zb_out, q - 1)
                for s in range(2):
                    h = 2 * (SGU + i) + s
                    in_unit_rows(h, h % 4, hT_hi, hT_lo, 4 * kh + 2 * s, NT, 2 * (q % 2))
            for t in range(NT):
                pe.wait_ge(v_ready, t + 1)
                if t:
                    pe.wait_ge(zb_out, 8)
                for g in range(G):
                    mm = nc.tensor.matmul(ps[:, (0 if t else 4) + g // 2, (g % 2) * GW:(g % 2 + 1) * GW],
                                          wsT[:, g, :], vv[:, t, g * GW:(g + 1) * GW], start=True, stop=True)
                mm.then_inc(sv_ps, 1)
            for r in range(2 * NT * 2):
                t, m = r % 2, r // 2
                pe.wait_ge(gated, NT if r else NT)
                if r >= 4:
                    pe.wait_ge(uT_lo_out, r - 3)
                for f in range(4):
                    mm = nc.tensor.transpose(ps[:, XB[t] + m % 2, f * P:(f + 1) * P],
                                             uu[:, t, tok(4 * m + f)], ident[:, :])
                mm.then_inc(uT_ps, 1)
            for m in range(HC // 2):
                for s in range(2):
                    kc = 2 * m + s
                    if kc % 4 == 0:
                        pe.wait_ge(uT_lo_out, 2 * (kc // 4 + 1))
                    h = 2 * (SGU_OUT + m) + s
                    out_unit_rows(h, h % 4, uT_hi, uT_lo, kc, NT, kc == 0, kc == HC - 1)

            for t in range(NT):
                turn_x(3, t)
            for t in range(NT):
                pe.wait_ge(h32_out, 6 + t + 1)
                for k in range(KC):
                    mm = nc.tensor.matmul(ps[:, 6, t * E:(t + 1) * E], h32[:, k, tok(t)], router[:, k, :],
                                          start=(k == 0), stop=(k == KC - 1))
                mm.then_inc(logit_ps, 1)
            pe.wait_ge(mask_ready, 1)
            nc.tensor.matmul(ps[:, 7, 0:E], tri[:, :], mask[:, 0, :], start=True, stop=True)
            nc.tensor.matmul(ps[:, 7, E:2 * E], ones[:, :], mask[:, 0, :], start=True, stop=False)
            nc.tensor.matmul(ps[:, 7, E:2 * E], tri[:, :], mask[:, 1, :], start=False, stop=True)
            nc.tensor.matmul(ps[:, 7, 2 * E:3 * E], ones[:, :], mask[:, 0, :], start=True, stop=False)
            nc.tensor.matmul(ps[:, 7, 2 * E:3 * E], ones[:, :], mask[:, 1, :], start=False, stop=True)\
                .then_inc(rank_ps, 1)

            def pick():
                for k in range(KC):
                    for t in range(NT):
                        mm = nc.tensor.matmul(ps[:, 1 + 2 * (k // 4), (k % 4) * P:(k % 4 + 1) * P],
                                              xs[:, t, tok(k)], oneh[:, t, :], start=(t == 0), stop=(t == NT - 1))
                mm.then_inc(picked_ps, 1)

            def spread():
                for t in range(NT):
                    for dh in range(2):
                        mm = nc.tensor.matmul(ps[:, (1, 3, 4, 5)[2 * t + dh], :], ggT[:, t, :],
                                              ye[:, dh * BANK:(dh + 1) * BANK], start=True, stop=True)
                mm.then_inc(spread_ps, 1)

            pe.wait_ge(meta_ready, 1)
            items = pe.value_load(metai[0:1, 4:5], min_val=E, max_val=NCOL - 1)
            pe.wait_ge(pick_ready, 1)
            pick()
            with pe.Fori(0, items) as i:
                def between(u):
                    if u == 1:
                        pe.wait_ge(ye_ready, i + 1)
                        spread()
                    if u == 3:
                        for t in range(NT):
                            mm = nc.tensor.transpose(ps[:, 6, tok(t)], ggate[:, t, :], ident[:, :])
                        mm.then_inc(ggT_ps, 1)
                    if u == INU + 3:
                        pe.wait_ge(pick_ready, i + 2)
                        pick()
                    if u == INU - 1:
                        pe.wait_ge(ggT_out, i + 1)

                pe.wait_ge(xe_ready, i + 1)
                swiglu(i * (2 * FFU) + 2 * MOE, i * NJ + NJ, 1, xe_hi, xe_lo, e_hid, eh_hi, eh_lo, between)
            pe.wait_ge(ye_ready, items + 1)
            spread()

        @block.scalar
        def _(act):
            def split(pos_slot, landed_count, h, hb, first):
                if first:
                    act.wait_ge(landed[pos_slot], landed_count)
                return nc.scalar.activation(w_hi[:, hb, :], ring[:, pos_slot, (hb % 2) * HALF:(hb % 2 + 1) * HALF],
                                            ACT.Copy).then_inc(hi_ready, 1)

            def split_unit(n):
                pos = split_at[n]
                for s in range(2):
                    h = 2 * n + s
                    if h >= 4:
                        act.wait_ge(half_used, h - 3)
                    split(pos % SLOTS, 16 * (pos // SLOTS + 1), h, h % 4, s == 0)

            def ada_copy(n, bank):
                act.wait_ge(ada_used, 2 * n + 2)
                if n:
                    act.wait_ge(ada_sums, n)
                nc.scalar.activation(modrow[:, :], ps[:, bank, :], ACT.Copy).then_inc(ada_copied, 1)

            def modulate(q, layer, sh, sc):
                for t in range(NT):
                    act.wait_ge(xT_ps, 2 * q + t + 1)
                    if t == 0:
                        act.wait_ge(ada_out, (4, 10, 16, 22)[q])
                    for k in range(KC):
                        op = nc.scalar.activation(h32[:, k, tok(t)], ps[:, XB[t] + k // 4, (k % 4) * P:(k % 4 + 1) * P],
                                                  ACT.Identity, bias=mods[:, layer, sh, k:k + 1],
                                                  scale=mods[:, layer, sc, k:k + 1])
                    op.then_inc(h32_out, 1)

            def deviations(q):
                for t in range(NT):
                    act.wait_ge(var_ready, 2 * q + t + 1)
                    nc.scalar.activation(dev[:, t:t + 1], var[:, t:t + 1], ACT.Sqrt).then_inc(dev_ready, 1)

            def swiglu(h0, c0, nt, unit, sil, e_hi, after):
                for u in range(FFU):
                    unit(u)
                    if u % 4 == 3 and u < INU:
                        j = (u - 3) // 4
                        act.wait_ge(half_used, h0 + 2 * (4 * j + 2))
                        act.wait_ge(hid_out, c0 + j)
                        nc.scalar.activation(sil[:, 0:nt, :], ps[:, 0:nt, :], ACT.Silu).then_inc(silu_out, 1)
                    if u % 4 == 3 and 7 <= u <= INU + 3:
                        j = (u - 7) // 4
                        act.wait_ge(hidT_ps, c0 + (j + 1))
                        for t in range(nt):
                            op = nc.scalar.activation(e_hi[:, 4 * j:4 * j + 4, tok(t)],
                                                      ps[:, 4 + t, :].rearrange("p (k n) -> p k n", k=4), ACT.Copy)
                        op.then_inc(hidT_hi, 1)
                    after(u)

            for j, (vec, n) in enumerate(((ada_b[0], 48), (ada_b[1], 48), (c[0], 8), (conv_dw_b[0], 8),
                                          (conv_ln_g[0], 8), (conv_ln_b[0], 8))):
                r0 = (0, 48, 96, 104, 112, 120)[j]
                act.dma_start(vecs[r0:r0 + n, :], vec.rearrange("(j p) -> j p", p=P)).then_inc(vec_landed, 16)
            act.dma_start(xs[:, :, :], x[0].rearrange("(t p) d -> p t d", p=P)).then_inc(x_landed, 16)
            act.wait_ge(vec_out, 1)
            nc.scalar.activation(csil[:, :, :], vcols[:, 96:104].unsqueeze(2).broadcast_to([P, KC, 32]), ACT.Silu)\
                .then_inc(csil_ready, 1)
            act.wait_ge(ws_ps, 1)
            nc.scalar.activation(wsT[:, :, :], ps[:, 0:2, :].rearrange("p b (g n) -> p (b g) n", g=4), ACT.Copy)\
                .then_inc(ws_out, 1)
            for n in range(4):
                ada_copy(n, 6)
                if n < 2:
                    split_unit(n)
            modulate(0, 0, 0, 1)

            for i in range(2, 8):
                split_unit(i)
                if i % 4 == 3:
                    blk = i // 4
                    act.wait_ge(half_used, 8 * blk + 4)
                    if blk:
                        act.wait_ge(glu_out, 1)
                    nc.scalar.activation(sig[:, :, :], ps[:, 0:4, 0:S], ACT.Sigmoid).then_inc(sig_out, 1)
            for ch in range(DVE_CH, KC):
                for half in range(2):
                    ada_copy(4 + 2 * (ch - DVE_CH) + half, 0)
                act.wait_ge(diag_used, (ch - DVE_CH + 1) * TAPS)
                nc.scalar.activation(ycv[:, ch, :], ps[:, ch, 0:S], ACT.Identity, bias=vcols[:, 104 + ch:105 + ch])\
                    .then_inc(dconv_out, 1)
            for hf in range(2):
                act.wait_ge(centred, hf + 1)
                nc.scalar.activation(ysq[:, 4 * hf:4 * hf + 4, :], ycv[:, 4 * hf:4 * hf + 4, :], ACT.Square)\
                    .then_inc(squared, 1)
            act.wait_ge(cvar, 1)
            nc.scalar.activation(cst[:, 2, :], cst[:, 1, :], ACT.Sqrt).then_inc(cdev, 1)
            for i in range(2):
                split_unit(CONV_OUT + i)
            for hf in range(2):
                act.wait_ge(normed, hf + 1)
                for ch in range(4 * hf, 4 * hf + 4):
                    op = nc.scalar.activation(ysq[:, ch, :], ycv[:, ch, :], ACT.Silu,
                                              bias=vcols[:, 120 + ch:121 + ch], scale=vcols[:, 112 + ch:113 + ch])
                op.then_inc(cact, 1)
            for i in range(2, 4):
                split_unit(CONV_OUT + i)
            for i in range(2):
                split_unit(FFN + i)
            deviations(0)
            modulate(1, 0, 3, 4)

            def ffn_unit(u):
                if u >= 2:
                    split_unit(FFN + u)

            def ada_between(u):
                if u % 2 and 0 <= (u - 3) // 2 < ADB and u >= 3:
                    ada_copy(ADB + (u - 3) // 2, 6)

            swiglu(2 * FFN, 0, NT, ffn_unit, f_sil, hid_hi, ada_between)
            for i in range(2):
                split_unit(SGU + i)
            deviations(1)
            modulate(2, 1, 0, 1)

            def gelu(q):
                act.wait_ge(zb_out, q + 1)
                z = vv if q < 4 else uu
                nc.scalar.activation(z[:, :, (q % 4) * BANK:(q % 4 + 1) * BANK],
                                     z[:, :, (q % 4) * BANK:(q % 4 + 1) * BANK], ACT.Gelu).then_inc(gelu_out, 1)

            for i in range(2, 18):
                split_unit(SGU + i)
                if i % 2:
                    gelu((i - 3) // 2)
                if i in (10, 12):
                    t = (i - 10) // 2
                    act.wait_ge(vvar, t + 1)
                    nc.scalar.activation(dev[:, t:t + 1], var[:, t:t + 1], ACT.Sqrt).then_inc(vdev, 1)
            for r in range(8):
                t, m = r % 2, r // 2
                act.wait_ge(uT_ps, r + 1)
                nc.scalar.activation(uT_hi[:, 4 * m:4 * m + 4, tok(t)],
                                     ps[:, XB[t] + m % 2, :].rearrange("p (k n) -> p k n", k=4), ACT.Copy)\
                    .then_inc(uT_hi_out, 1)
            for m in range(2, HC // 2):
                split_unit(SGU_OUT + m)

            def moe_unit(i):
                def unit(u):
                    for s in range(2):
                        act.wait_ge(half_used, i * (2 * FFU) + (2 * (MOE + u) + s - 3))
                        split(u % SLOTS, i * (16 * FFU // SLOTS) + 16 * ((MOE_AT + u) // SLOTS + 1), None,
                              (2 * u + s) % 4, s == 0)
                return unit

            deviations(2)
            modulate(3, 1, 3, 4)
            act.wait_ge(mdif, 1)
            nc.scalar.activation(tgate[:, :, 0:1], tdif[:, :, :], ACT.Sigmoid, scale=-1.0).then_inc(mgate, 1)
            nc.scalar.activation(tgate[:, :, 1:2], tdif[:, :, :], ACT.Sigmoid).then_inc(mgate, 1)

            def modulate_item():
                for k in range(KC):
                    op = nc.scalar.activation(xe32[:, k, :], ps[:, 1 + 2 * (k // 4), (k % 4) * P:(k % 4 + 1) * P],
                                              ACT.Identity, bias=mods[:, 1, 3, k:k + 1], scale=mods[:, 1, 4, k:k + 1])
                op.then_inc(xe32_out, 1)

            act.wait_ge(meta_ready, 1)
            items = act.value_load(metai[0:1, 4:5], min_val=E, max_val=NCOL - 1)
            act.wait_ge(picked_ps, 1)
            modulate_item()
            with act.Fori(0, items) as i:
                def between(u):
                    if u == 5:
                        act.wait_ge(ggT_ps, i + 1)
                        nc.scalar.activation(ggT[:, :, :], ps[:, 6, 0:NT * P].rearrange("p (t n) -> p t n", t=NT),
                                             ACT.Copy).then_inc(ggT_out, 1)
                    if u == INU + 5:
                        act.wait_ge(picked_ps, i + 2)
                        modulate_item()

                swiglu(i * (2 * FFU) + 2 * MOE, i * NJ + NJ, 1, moe_unit(i), e_sil, eh_hi, between)
            act.wait_ge(var_ready, 7)
            nc.scalar.activation(dev[:, 0:1], var[:, 0:1], ACT.Sqrt).then_inc(dev_ready, 1)
            act.wait_ge(var_ready, 8)
            nc.scalar.activation(dev[:, 1:2], var[:, 1:2], ACT.Sqrt).then_inc(dev_ready, 1)

        @block.vector
        def _(dve):
            steps = [0]

            def link(ins):
                steps[0] += 1
                ins.then_inc(dve_step, 1)
                dve.wait_ge(dve_step, steps[0])

            def split_unit(n):
                for s in range(2):
                    h = 2 * n + s
                    dve.wait_ge(hi_ready, h + 1)
                    if h >= 4:
                        dve.wait_ge(half_used, h - 3)
                    nc.vector.tensor_tensor(w_lo[:, h % 4, :],
                                            ring[:, split_at[n] % SLOTS, s * HALF:(s + 1) * HALF],
                                            w_hi[:, h % 4, :].bitcast(F32), ALU.subtract).then_inc(lo_ready, 1)

            def ada_take(n, bank):
                layer, b = n // ADB, n % ADB
                dve.wait_ge(ada_sums, n + 1)
                if b // 2 in (2, 5):
                    row = g1row[:, :] if b // 2 == 2 else g2row[:, layer, :]
                    row = row[:, (b % 2) * BANK:(b % 2 + 1) * BANK]
                    dve.wait_ge(gb_landed, 64 if layer else 48)
                    op = nc.vector.scalar_tensor_tensor(out=row, in0=ps[:, bank, :], scalar=1.0, in1=row,
                                                        op0=ALU.add, op1=ALU.add)
                else:
                    op = nc.vector.tensor_tensor(mods[:, layer, b // 2, 4 * (b % 2):4 * (b % 2) + 4],
                                                 ps[:, bank, 4 * b:4 * b + 4],
                                                 modb[:, 48 * layer + 4 * b:48 * layer + 4 * b + 4], ALU.add)
                op.then_inc(ada_out, 1)

            def split_h(q):
                for t in range(NT):
                    dve.wait_ge(h32_out, 2 * q + t + 1)
                    link(nc.vector.tensor_copy(hT_hi[:, :, tok(t)], h32[:, :, tok(t)]))
                    nc.vector.tensor_tensor(hT_lo[:, :, tok(t)], h32[:, :, tok(t)],
                                            hT_hi[:, :, tok(t)].bitcast(F32), ALU.subtract).then_inc(h_ready, 1)

            def variance(t, row, width, ready):
                n = width // BANK
                for k in range(n):
                    op = nc.vector.bn_stats(stats[:, t, k, :], row[:, k * BANK:(k + 1) * BANK])
                link(op)
                link(nc.vector.bn_aggr(mv[:, t, :], stats[:, t, 0:n, :].rearrange("p a b -> p (a b)")))
                nc.vector.tensor_scalar(var[:, t:t + 1], mv[:, t, 1:2], 1e-5, None, ALU.add).then_inc(ready, 1)

            def standardise(t, row, out_row, ready, count, gain, bias):
                dve.wait_ge(ready, count)
                link(nc.vector.reciprocal(rstd[:, t:t + 1], dev[:, t:t + 1]))
                link(nc.vector.tensor_scalar(out_row, row, mv[:, t, 0:1], rstd[:, t:t + 1], ALU.subtract, ALU.mult))
                link(nc.vector.tensor_tensor(out_row, out_row, gain, ALU.mult))
                return nc.vector.tensor_tensor(out_row, out_row, bias, ALU.add)

            def post_norm(q, h_end, grow):
                dve.wait_ge(half_used, h_end)
                for t in range(NT):
                    y = ps[:, YB[t]:YB[t] + 2, :].rearrange("p a b -> p (a b)")
                    link(nc.vector.tensor_tensor(ztmp[:, :], y, grow, ALU.mult))
                    link(nc.vector.scalar_tensor_tensor(out=xs[:, t, :], in0=xs[:, t, :], scalar=ALPHA,
                                                        in1=ztmp[:, :], op0=ALU.mult, op1=ALU.add))
                    variance(t, xs[:, t, :], D, var_ready)
                dve.wait_ge(rows_landed, 32 * (q + 1))
                for t in range(NT):
                    standardise(t, xs[:, t, :], xs[:, t, :], dev_ready, 2 * q + t + 1, lng[:, :], lnb[:, :])\
                        .then_inc(x_ready, 1)

            def swiglu(h0, c0, nt, unit, sil, hid, e_hi, e_lo, after):
                for u in range(FFU):
                    unit(u)
                    if u % 4 == 1 and 5 <= u <= INU + 1:
                        j = (u - 5) // 4
                        dve.wait_ge(half_used, h0 + 2 * (4 * j + 4))
                        dve.wait_ge(silu_out, c0 + (j + 1))
                        dve.wait_ge(hidT_ps, c0 + j)
                        nc.vector.tensor_tensor(hid[:, 0:nt, :], ps[:, 2:2 + nt, :], sil[:, 0:nt, :], ALU.mult)\
                            .then_inc(hid_out, 1)
                    if u % 4 == 3 and 7 <= u <= INU + 3:
                        j = (u - 7) // 4
                        dve.wait_ge(hidT_hi, c0 + (j + 1))
                        for t in range(nt):
                            op = nc.vector.tensor_tensor(e_lo[:, 4 * j:4 * j + 4, tok(t)],
                                                         ps[:, 4 + t, :].rearrange("p (k n) -> p k n", k=4),
                                                         e_hi[:, 4 * j:4 * j + 4, tok(t)].bitcast(F32), ALU.subtract)
                        op.then_inc(hidT_lo, 1)
                    after(u)

            nc.vector.memset(ypad[:, :, 0:PADL], 0.0).then_inc(pad_zero, 1)
            dve.wait_ge(pool_step, 5)
            nc.vector.tensor_copy(iota[:, :], iota_i[:, :]).then_inc(iota_ready, 1)
            for r in range(0, P, 32):
                nc.vector.memset(sel4[r:r + 1, :], 1.0).then_inc(consts, 1)
            dve.wait_ge(vec_ps, 1)
            nc.vector.tensor_copy(vcols[:, :], ps[:, 6, 0:P]).then_inc(vec_out, 1)
            dve.wait_ge(vec_ps, 2)
            nc.vector.tensor_copy(dwT[:, :, :], ps[:, 5, 0:KC * TAPS].rearrange("p (c k) -> p c k", c=KC))\
                .then_inc(vec_out, 1)
            nc.vector.tensor_copy(bsT[:, :], ps[:, 5, 256:256 + G]).then_inc(vec_out, 1)
            dve.wait_ge(vec_out, 3)
            link(nc.vector.tensor_copy(modb[:, :], vcols[:, 0:96]))
            for layer in range(2):
                for seg in (1, 4):
                    col = modb[:, 48 * layer + 8 * seg:48 * layer + 8 * seg + 8]
                    op = nc.vector.tensor_scalar(col, col, 1.0, None, ALU.add)
            link(op)
            for n in range(4):
                ada_take(n, 7)
            split_unit(0)
            split_unit(1)
            split_h(0)

            def glu(blk):
                dve.wait_ge(sig_out, blk + 1)
                dve.wait_ge(half_used, 8 * blk + 8)
                nc.vector.tensor_tensor(ypad[:, 4 * blk:4 * blk + 4, PADL:], ps[:, 4:8, 0:S], sig[:, :, :],
                                        ALU.mult).then_inc(glu_out, 1)

            for i in range(2, 6):
                split_unit(i)
            glu(0)
            for i in range(6, 8):
                split_unit(i)
            glu(1)
            dve.wait_ge(glu_out, 2)
            dve.wait_ge(pad_zero, 1)
            for ch in range(DVE_CH):
                for k in range(TAPS):
                    src, w = ypad[:, ch, k:k + S], dwT[:, ch, k:k + 1]
                    if k == 0:
                        op = nc.vector.tensor_scalar(ycv[:, ch, :], src, w, vcols[:, 104 + ch:105 + ch],
                                                     ALU.mult, ALU.add)
                    else:
                        op = nc.vector.scalar_tensor_tensor(out=ycv[:, ch, :], in0=src, scalar=w, in1=ycv[:, ch, :],
                                                            op0=ALU.mult, op1=ALU.add)
                    if k < TAPS - 1:
                        link(op)
                op.then_inc(taps_out, 1)
                for half in range(2):
                    n = 4 + 2 * ch + half
                    ada_take(n, 1 + n % 3)
            dve.wait_ge(mean_ps, 1)
            link(nc.vector.tensor_scalar(cst[:, 0, :], ps[:, 4, 0:S], 1.0 / D, None, ALU.mult))
            for hf in range(2):
                part = ycv[:, 4 * hf:4 * hf + 4, :]
                nc.vector.tensor_tensor(part, part, cst[:, 0:1, :].broadcast_to([P, 4, S]), ALU.subtract)\
                    .then_inc(centred, 1)
            dve.wait_ge(var_ps, 1)
            nc.vector.tensor_scalar(cst[:, 1, :], ps[:, 5, 0:S], 1.0 / D, 1e-5, ALU.mult, ALU.add).then_inc(cvar, 1)
            dve.wait_ge(cdev, 1)
            dve.wait_ge(centred, 2)
            link(nc.vector.reciprocal(cst[:, 3, :], cst[:, 2, :]))
            for hf in range(2):
                part = ycv[:, 4 * hf:4 * hf + 4, :]
                nc.vector.tensor_tensor(part, part, cst[:, 3:4, :].broadcast_to([P, 4, S]), ALU.mult)\
                    .then_inc(normed, 1)
            for i in range(2):
                split_unit(CONV_OUT + i)
            for hf in range(2):
                part = slice(4 * hf, 4 * hf + 4)
                dve.wait_ge(cact, hf + 1)
                link(nc.vector.tensor_copy(y_hi[:, part, :], ysq[:, part, :]))
                nc.vector.tensor_tensor(y_lo[:, part, :], ysq[:, part, :], y_hi[:, part, :].bitcast(F32),
                                        ALU.subtract).then_inc(y_ready, 1)
            for i in range(2, 4):
                split_unit(CONV_OUT + i)
            for i in range(2):
                split_unit(FFN + i)
            post_norm(0, 2 * FFN, g1row[:, :])
            split_h(1)

            def ffn_unit(u):
                if u >= 2:
                    split_unit(FFN + u)

            def ada_between(u):
                if u % 2 == 0 and u >= 4 and (u - 4) // 2 < ADB:
                    ada_take(ADB + (u - 4) // 2, 7)

            swiglu(2 * FFN, 0, NT, ffn_unit, f_sil, f_hid, hid_hi, hid_lo, ada_between)
            for i in range(2):
                split_unit(SGU + i)
            post_norm(1, 2 * SGU, g2row[:, 0, :])
            split_h(2)

            def add_bias(q):
                dve.wait_ge(half_used, 2 * (SGU + 2 * q + 2))
                dve.wait_ge(brow_landed[q % 2], 16 * (q // 2 + 1))
                z = vv if q < 4 else uu
                for t in range(NT):
                    op = nc.vector.tensor_tensor(z[:, t, (q % 4) * BANK:(q % 4 + 1) * BANK],
                                                 ps[:, 2 * (q % 2) + t, :], brow[:, q % 2, :], ALU.add)
                op.then_inc(zb_out, 1)

            for i in range(2, 18):
                split_unit(SGU + i)
                if i % 2:
                    add_bias((i - 3) // 2)
                if i in (10, 12):
                    t = (i - 10) // 2
                    dve.wait_ge(gelu_out, 4)
                    dve.wait_ge(sln_landed, 32)
                    variance(t, vv[:, t, :], HS, vvar)
                    standardise(t, vv[:, t, :], vv[:, t, :], vdev, t + 1, s_lng[:, :], s_lnb[:, :])\
                        .then_inc(v_ready, 1)
            for t in range(NT):
                dve.wait_ge(sv_ps, t + 1)
                dve.wait_ge(gelu_out, 8)
                for g in range(G):
                    u_g = uu[:, t, g * GW:(g + 1) * GW]
                    op = nc.vector.scalar_tensor_tensor(
                        out=u_g, in0=ps[:, (0 if t else 4) + g // 2, (g % 2) * GW:(g % 2 + 1) * GW],
                        scalar=bsT[:, g:g + 1], in1=u_g, op0=ALU.add, op1=ALU.mult)
                op.then_inc(gated, 1)
            for r in range(8):
                t, m = r % 2, r // 2
                dve.wait_ge(uT_hi_out, r + 1)
                nc.vector.tensor_tensor(uT_lo[:, 4 * m:4 * m + 4, tok(t)],
                                        ps[:, XB[t] + m % 2, :].rearrange("p (k n) -> p k n", k=4),
                                        uT_hi[:, 4 * m:4 * m + 4, tok(t)].bitcast(F32), ALU.subtract)\
                    .then_inc(uT_lo_out, 1)
            for m in range(2, HC // 2):
                split_unit(SGU_OUT + m)

            post_norm(2, 2 * MOE, g1row[:, :])

            dve.wait_ge(logit_ps, 2)
            dve.wait_ge(iota_ready, 1)
            link(nc.vector.tensor_copy(lgt[:, :, :], ps[:, 6, 0:NT * E].rearrange("p (t e) -> p t e", t=NT)))
            for t in range(NT):
                op = nc.vector.max(top[:, t, :], lgt[:, t, :])
            link(op)
            nc.vector.tensor_tensor(tdif[:, :, :], top[:, :, 1:2], top[:, :, 0:1], ALU.subtract).then_inc(mdif, 1)
            for t in range(NT):
                op = nc.vector.max_index(topi[:, t, :], top[:, t, :], lgt[:, t, :])
            link(op)
            link(nc.vector.tensor_copy(topf[:, :, :], topi[:, :, :]))
            for t in range(NT):
                nc.vector.tensor_scalar(mask1[:, t, :], iota[:, 0:E], topf[:, t, 0:1], None, ALU.is_equal)
                op = nc.vector.tensor_scalar(mask2[:, t, :], iota[:, 0:E], topf[:, t, 1:2], None, ALU.is_equal)
            link(op)
            nc.vector.tensor_tensor(mask[:, :, :], mask1[:, :, :], mask2[:, :, :], ALU.add).then_inc(mask_ready, 1)
            dve.wait_ge(mgate, 2)
            for t in range(NT):
                op = nc.vector.tensor_scalar(gate1[:, t, :], mask1[:, t, :], tgate[:, t, 0:1], None, ALU.mult)
            link(op)
            for t in range(NT):
                op = nc.vector.scalar_tensor_tensor(out=gate[:, t, :], in0=mask2[:, t, :], scalar=tgate[:, t, 1:2],
                                                    in1=gate1[:, t, :], op0=ALU.mult, op1=ALU.add)
            nc.vector.memset(over[:, :, :], 0.0)
            nc.vector.memset(dest[:, :, :], -1.0)
            nc.vector.memset(meta[:, :], 0.0)
            link(nc.vector.memset(gcol[:, :, :], 0.0))
            dve.wait_ge(rank_ps, 1)
            dve.wait_ge(mask_ready, 1)
            for t in range(NT):
                op = nc.vector.scalar_tensor_tensor(out=rank1[:, t, :], in0=ps[:, 7, t * E:(t + 1) * E], scalar=1.0,
                                                    in1=mask[:, t, :], op0=ALU.add, op1=ALU.mult)
            link(op)
            nc.vector.tensor_scalar(dest[:, :, 0:E], rank1[:, :, :], 1.0, None, ALU.subtract)
            nc.vector.tensor_copy(gcol[:, :, 0:E], gate[:, :, :])
            nc.vector.tensor_scalar(excess[:, :, :], rank1[:, :, :], float(P), 0.0, ALU.subtract, ALU.max)
            link(nc.vector.tensor_scalar(over[:, 0, E:], ps[:, 7, 2 * E:3 * E], float(P), None, ALU.is_gt))
            for s in range(3):
                link(nc.vector.tensor_tensor(over[:, s + 1, E:], over[:, s, E:], over[:, s, E - 2 ** s:2 * E - 2 ** s],
                                             ALU.add))
            link(nc.vector.tensor_tensor(before[:, :], over[:, 3, E:], over[:, 0, E:], ALU.subtract))
            for m in range(3):
                link(nc.vector.scalar_tensor_tensor(out=oh[:, m, :], in0=before[:, :], scalar=float(m),
                                                    in1=over[:, 0, E:], op0=ALU.is_equal, op1=ALU.mult))
                link(nc.vector.tensor_tensor_reduce(junk[:, :], oh[:, m, :], iota[:, 0:E], 1.0, 0.0, ALU.mult,
                                                    ALU.add, meta[:, m:m + 1]))
                for t in range(NT):
                    link(nc.vector.tensor_tensor_reduce(junk[:, :], oh[:, m, :], excess[:, t, :], 1.0, -1.0,
                                                        ALU.mult, ALU.add, dest[:, t, E + m:E + m + 1]))
                    link(nc.vector.tensor_tensor_reduce(junk[:, :], oh[:, m, :], gate[:, t, :], 1.0, 0.0,
                                                        ALU.mult, ALU.add, gcol[:, t, E + m:E + m + 1]))
            link(nc.vector.tensor_scalar(meta[:, 4:5], over[:, 3, 2 * E - 1:2 * E], float(E), None, ALU.add))
            nc.vector.tensor_copy(metai[:, :], meta[:, :]).then_inc(meta_ready, 1)
            nc.vector.memset(ye[:, :], 0.0)
            nc.vector.memset(ggT[:, :, :], 0.0)
            link(nc.vector.tensor_scalar(flat(acc[:, :, :]), flat(xs[:, :, :]), ALPHA, None, ALU.mult))

            def choose(item):
                for t in range(NT):
                    d = dest[:, t, item]
                    nc.vector.tensor_scalar(oneh[:, t, :], iota[:, :], d, None, ALU.is_equal)
                    op = nc.vector.tensor_scalar(ggate[:, t, :], iota[:, :], d, gcol[:, t, item],
                                                 ALU.is_equal, ALU.mult)
                op.then_inc(pick_ready, 1)

            def split_item(step):
                step(nc.vector.tensor_copy(xe_hi[:, :, :], xe32[:, :, :]))
                nc.vector.tensor_tensor(xe_lo[:, :, :], xe32[:, :, :], xe_hi[:, :, :].bitcast(F32), ALU.subtract)\
                    .then_inc(xe_ready, 1)

            def take_rows():
                nc.vector.tensor_tensor(ye[:, :], ps[:, 6:8, :].rearrange("p a b -> p (a b)"), g2row[:, 1, :],
                                        ALU.mult).then_inc(ye_ready, 1)

            def add_rows():
                for t in range(NT):
                    for dh in range(2):
                        a = acc[:, t, dh * BANK:(dh + 1) * BANK]
                        op = nc.vector.tensor_tensor(a, ps[:, (1, 3, 4, 5)[2 * t + dh], :], a, ALU.add)
                op.then_inc(acc_out, 1)

            dve.wait_ge(meta_ready, 1)
            items = dve.value_load(metai[0:1, 4:5], min_val=E, max_val=NCOL - 1)
            choose(slice(0, 1))
            dve.wait_ge(xe32_out, 1)
            split_item(link)
            TURN = 1
            with dve.Fori(0, items) as i:
                turn = [0]

                def step(ins):
                    turn[0] += 1
                    ins.then_inc(dve_turn, 1)
                    dve.wait_ge(dve_turn, i * TURN + turn[0])

                def unit(u):
                    for s in range(2):
                        hb = (2 * u + s) % 4
                        dve.wait_ge(hi_ready, i * (2 * FFU) + (2 * (MOE + u) + s + 1))
                        dve.wait_ge(half_used, i * (2 * FFU) + (2 * (MOE + u) + s - 3))
                        nc.vector.tensor_tensor(w_lo[:, hb, :], ring[:, u % SLOTS, s * HALF:(s + 1) * HALF],
                                                w_hi[:, hb, :].bitcast(F32), ALU.subtract).then_inc(lo_ready, 1)

                def between(u):
                    if u == 0:
                        dve.wait_ge(half_used, i * (2 * FFU) + 2 * MOE)
                        take_rows()
                    if u == 3:
                        dve.wait_ge(spread_ps, i + 1)
                        add_rows()
                    if u == INU - 1:
                        dve.wait_ge(ggT_ps, i + 1)
                        choose(bass.ds(i + 1, 1))
                    if u == INU + 5:
                        dve.wait_ge(xe32_out, i + 2)
                        split_item(step)

                swiglu(i * (2 * FFU) + 2 * MOE, i * NJ + NJ, 1, unit, e_sil, e_hid, eh_hi, eh_lo, between)
                assert turn[0] == TURN
            dve.wait_ge(half_used, items * (2 * FFU) + 2 * MOE)
            take_rows()
            dve.wait_ge(spread_ps, items + 1)
            add_rows()
            dve.wait_ge(acc_out, items + 1)
            for t in range(NT):
                variance(t, acc[:, t, :], D, var_ready)
            dve.wait_ge(rows_landed, 128)
            for t in range(NT):
                standardise(t, acc[:, t, :], xs[:, t, :], dev_ready, 6 + t + 1, lng[:, :], lnb[:, :])\
                    .then_inc(x_ready, 1)


_INS = ["x", "c", "ada_w", "ada_b", "ln_g", "ln_b", "conv_w_in", "conv_dw", "conv_dw_b", "conv_ln_g", "conv_ln_b",
        "conv_w_out", "sgu_w_in", "sgu_b_in", "sgu_ln_g", "sgu_ln_b", "sgu_w_s", "sgu_b_s", "sgu_w_out",
        "ffn_w_in", "ffn_w_out", "moe_router", "moe_w_in", "moe_w_out"]


def kernel(**inputs):
    import numpy as _np
    import concourse.bacc as _bacc
    from concourse import mybir as _mybir
    from concourse.bass_utils import run_bass_kernel_spmd as _run

    nc = _bacc.Bacc("TRN2", target_bir_lowering=False, num_devices=1)
    arrays, args = {}, []
    for name in _INS:
        a = _np.ascontiguousarray(inputs[name])
        arrays[f"in_{name}"] = a
        args.append(nc.dram_tensor(f"in_{name}", a.shape, _mybir.dt.from_np(a.dtype), kind="ExternalInput").ap())
    shape = inputs["x"].shape
    out = nc.dram_tensor("out_x", shape, _mybir.dt.float32, kind="ExternalOutput").ap()
    hybrid_trunk(nc, *args, out)
    r = _run(nc, [arrays], core_ids=[0])
    return r.results[0]["out_x"]
```

```python
from contextlib import ExitStack

import concourse.bass as bass
from concourse import mybir

ALU = mybir.AluOpType
ACT = mybir.ActivationFunctionType
F32 = mybir.dt.float32
F32R = mybir.dt.float32r
I32 = mybir.dt.int32
U32 = mybir.dt.uint32

P = 128
BANK = 512
SLOTS = 7
UNIT = 2048
HALF = UNIT // 2


def hybrid_trunk(nc, x, c, ada_w, ada_b, ln_g, ln_b, conv_w_in, conv_dw, conv_dw_b, conv_ln_g,
                 conv_ln_b, conv_w_out, sgu_w_in, sgu_b_in, sgu_ln_g, sgu_ln_b, sgu_w_s, sgu_b_s,
                 sgu_w_out, ffn_w_in, ffn_w_out, moe_router, moe_w_in, moe_w_out, out):
    _, S, D = x.shape
    NT = S // P
    KC = D // P
    F = ffn_w_out.shape[1]
    NJ = F // BANK
    FC = F // P
    E = moe_router.shape[2]
    TAPS = conv_dw.shape[1]
    PADL = TAPS - 1
    HS = sgu_w_out.shape[1]
    HC = HS // P
    G = sgu_w_s.shape[1]
    GW = HS // G
    DEPTH = ada_w.shape[0]
    ALPHA = (2 * DEPTH) ** 0.25
    SEG = 6
    ADB = SEG * D // BANK
    XS = 32
    CAP = P + XS
    NCOL = E + 4
    INU = 4 * NJ
    OUTU = FC // 2
    FFU = INU + OUTU
    DVE_CH = 5
    DIAGS = (KC - DVE_CH) * TAPS
    assert S <= 2 * CAP and E * CAP >= S and 4 * (CAP + 1) > 2 * S
    assert NT == 2 and KC == 8 and FC % 4 == 0 and FFU % SLOTS == 0 and SEG * D // P == 48

    def in_unit(w, col, kh):
        return w.rearrange("(k p) n -> p k n", p=P)[:, 4 * kh:4 * kh + 4, col:col + BANK]

    def out_unit(w, m):
        return w.rearrange("(k p) n -> p k n", p=P)[:, 2 * m:2 * m + 2, :]

    units, ada_at, split_at = [], [], []

    def add_ada(layer, b):
        for kh in range(2):
            ada_at.append(len(units))
            units.append(("ada", len(ada_at) - 1, in_unit(ada_w[layer], b * BANK, kh)))

    def add_split(ap):
        split_at.append(len(units))
        units.append(("split", len(split_at) - 1, ap))

    for b in range(4):
        add_ada(0, b)
    for blk in range(2):
        for col in (D, 0):
            for kh in range(2):
                add_split(in_unit(conv_w_in[0], col + blk * BANK, kh))
    for b in range(4, ADB):
        add_ada(0, b)
    CONV_OUT = len(split_at)
    for m in range(KC // 2):
        add_split(out_unit(conv_w_out[0], m))
    FFN = len(split_at)
    for u in range(INU):
        j, part, kh = u // 4, (u % 4) // 2, u % 2
        add_split(in_unit(ffn_w_in[0], part * F + j * BANK, kh))
        if u % 2 and u // 2 < ADB:
            add_ada(1, u // 2)
    for m in range(OUTU):
        add_split(out_unit(ffn_w_out[0], m))
    SGU = len(split_at)
    for q in range(8):
        for kh in range(2):
            add_split(in_unit(sgu_w_in[0], (HS + q * BANK) if q < 4 else (q - 4) * BANK, kh))
    SGU_OUT = len(split_at)
    for m in range(HC // 2):
        add_split(out_unit(sgu_w_out[0], m))
    MOE = len(split_at)
    MOE_AT = len(units)
    assert MOE_AT % SLOTS == 0 and MOE % 2 == 0

    with ExitStack() as ctx:
        def sem(name):
            return ctx.enter_context(nc.semaphore(name))

        def sb(name, shape, dt=F32):
            return ctx.enter_context(nc.sbuf_tensor(name, shape, dt))

        ring = sb("ring", [P, SLOTS, UNIT])
        w_hi = sb("w_hi", [P, 4, HALF], F32R)
        w_lo = sb("w_lo", [P, 4, HALF], F32R)
        xs = sb("xs", [P, NT, D])
        g1row = sb("g1row", [P, D])
        g2row = sb("g2row", [P, 2, D])
        lng = sb("lng", [P, D])
        lnb = sb("lnb", [P, D])
        ident = sb("ident", [P, P])
        ones = sb("ones", [P, P])
        sel4 = sb("sel4", [P, P])
        tri = sb("tri", [P, P])
        iota = sb("iota", [P, P])
        vcols = sb("vcols", [P, P])
        modb = sb("modb", [P, 96])
        mods = sb("mods", [P, 2, SEG, KC])
        lncols = sb("lncols", [P, 2, 3, KC])
        ab = sb("ab", [P, 3, 2, KC])
        csil = sb("csil", [P, KC, 32])
        modrow = sb("modrow", [P, BANK])
        wsT = sb("wsT", [P, G, P])
        bsT = sb("bsT", [P, G])
        router = sb("router", [P, KC, E])
        stats = sb("stats", [P, NT, 4, 6])
        mv = sb("mv", [P, NT, 2])
        var = sb("var", [P, NT])
        dev = sb("dev", [P, NT])
        rstd = sb("rstd", [P, NT])
        ps = ctx.enter_context(nc.psum_tensor("ps", [P, 8, BANK], F32))

        ARENA = 80
        sb("arena", [P, ARENA * 256])
        base = nc.sbuf_base - ARENA * 1024

        def at(kib, name, shape, dt=F32):
            return nc.alloc_sbuf_tensor_at(name, shape, dt, offset=int(base + kib * 1024))

        hT_hi = at(0, "hT_hi", [P, KC, S], F32R)
        hT_lo = at(8, "hT_lo", [P, KC, S], F32R)
        ztmp_early = at(8, "ztmp_early", [P, NT, D])
        ztmp_late = at(24, "ztmp_late", [P, NT, D])
        h32 = at(16, "h32", [P, KC, S])
        ypad = at(24, "ypad", [P, KC, PADL + S])
        ycv = at(34, "ycv", [P, KC, S])
        ysq = at(42, "ysq", [P, KC, S])
        y_hi = at(50, "y_hi", [P, KC, S], F32R)
        y_lo = at(58, "y_lo", [P, KC, S], F32R)
        sig = at(66, "sig", [P, 4, S])
        dwT = at(70, "dwT", [P, KC, TAPS])
        diag = at(71, "diag", [P, 8, P])
        cst = at(75, "cst", [P, 4, S])
        vecs = at(42, "vecs", [P, P])
        vecs2 = at(42.5, "vecs2", [48, P])
        iota_i = at(58, "iota_i", [P, P], I32)
        dwrow = at(43, "dwrow", [TAPS, D])
        bsrow = at(47, "bsrow", [G, P])
        wsr = at(50, "wsr", [P, G, P])
        wsm = at(54, "wsm", [P, G, P])
        f_sil = at(16, "f_sil", [P, NT, BANK])
        f_hid = at(20, "f_hid", [P, NT, BANK])
        hid_hi = at(24, "hid_hi", [P, FC, S], F32R)
        hid_lo = at(52, "hid_lo", [P, FC, S], F32R)
        vv = at(24, "vv", [P, NT, HS])
        uu = at(40, "uu", [P, NT, HS])
        s_lng = at(56, "s_lng", [P, HS])
        s_lnb = at(64, "s_lnb", [P, HS])
        brow = at(72, "brow", [P, 2, BANK])
        uT_hi = at(0, "uT_hi", [P, HC, S], F32R)
        uT_lo = at(56, "uT_lo", [P, HC, S], F32R)
        acc = at(0, "acc", [P, NT, D])
        oneh = at(22, "oneh", [P, NT, CAP])
        ggate = at(9, "ggate", [P, NT, P])
        ggT = at(10, "ggT", [P, 2 * NT, P])
        xe32 = at(24, "xe32", [P, KC, P])
        xe_hi = at(28, "xe_hi", [P, KC, P], F32R)
        xe_lo = at(32, "xe_lo", [P, KC, P], F32R)
        eh_hi = at(36, "eh_hi", [P, FC, P], F32R)
        eh_lo = at(50, "eh_lo", [P, FC, P], F32R)
        ye = at(64, "ye", [P, D])
        e_sil = at(68, "e_sil", [P, 1, BANK])
        e_hid = at(70, "e_hid", [P, 1, BANK])
        hidx_T = at(16, "hidx_T", [P, FC, XS])
        xx = at(20, "xx", [P, KC, XS])
        ggx = at(21, "ggx", [P, NT, P])
        yex = at(72, "yex", [P, D])
        silx = at(76, "silx", [P, P])
        hidx = at(76.5, "hidx", [P, P])
        iotax = at(77.5, "iotax", [P, P])
        small_at = [12 * 1024]

        def small(name, cols, dt=F32):
            t = nc.alloc_sbuf_tensor_at(name, [P, *cols], dt, offset=base + small_at[0])
            n = 4
            for d in cols:
                n *= d
            small_at[0] += (n + 31) // 32 * 32
            assert small_at[0] <= 16 * 1024
            return t

        lgt = small("lgt", [NT, E])
        top = small("top", [NT, 8])
        topi = small("topi", [NT, 8], U32)
        topf = small("topf", [NT, 8])
        tdif = small("tdif", [NT, 1])
        tgate = small("tgate", [NT, 2])
        mask1 = small("mask1", [NT, E])
        mask2 = small("mask2", [NT, E])
        mask = small("mask", [NT, E])
        gate1 = small("gate1", [NT, E])
        gate = small("gate", [NT, E])
        rank1 = small("rank1", [NT, E])
        excess = small("excess", [NT, E])
        over = small("over", [4, 2 * E])
        before = small("before", [E])
        oh = small("oh", [4, E])
        junk = small("junk", [15, E])
        dest = small("dest", [NT, NCOL])
        gcol = small("gcol", [NT, NCOL])
        XF = 8
        meta = small("meta", [XF + 1 + NCOL])
        metai = small("metai", [XF + 1 + NCOL], I32)

        landed = [sem(f"landed{i}") for i in range(SLOTS)]
        x_landed, vec_landed, misc_landed = sem("x_landed"), sem("vec_landed"), sem("misc_landed")
        rows_landed, gb_landed = sem("rows_landed"), sem("gb_landed")
        sln_landed = sem("sln_landed")
        brow_landed = [sem("brow_landed0"), sem("brow_landed1")]
        stored = sem("stored")
        lo_seen = sem("lo_seen")
        consts, pool_step, ws_masked = sem("consts"), sem("pool_step"), sem("ws_masked")
        hi_ready, lo_ready, half_used = sem("hi_ready"), sem("lo_ready"), sem("half_used")
        ada_used, ada_copied, ada_sums, ada_out = sem("ada_used"), sem("ada_copied"), sem("ada_sums"), sem("ada_out")
        vec_ps, vec_out, ws_ps, ws_out = sem("vec_ps"), sem("vec_out"), sem("ws_ps"), sem("ws_out")
        csil_ready, modb_ready, iota_ready = sem("csil_ready"), sem("modb_ready"), sem("iota_ready")
        pad_zero = sem("pad_zero")
        xT_ps, h32_out, h_ready = sem("xT_ps"), sem("h32_out"), sem("h_ready")
        sig_out, glu_out, diag_ready, diag_used = sem("sig_out"), sem("glu_out"), sem("diag_ready"), sem("diag_used")
        taps_out, dconv_out = sem("taps_out"), sem("dconv_out")
        mean_ps, centred, squared, var_ps, cvar, cdev, normed, cact, y_ready = (
            sem(n) for n in ("mean_ps", "centred", "squared", "var_ps", "cvar", "cdev", "normed", "cact", "y_ready"))
        var_ready, dev_ready, x_ready = sem("var_ready"), sem("dev_ready"), sem("x_ready")
        y_done, ab_ready, rows_used = sem("y_done"), sem("ab_ready"), sem("rows_used")
        silu_out, hid_out, hidT_ps, hidT_hi, hidT_lo = (
            sem(n) for n in ("silu_out", "hid_out", "hidT_ps", "hidT_hi", "hidT_lo"))
        zb_out, gelu_out, vvar, vdev, v_ready, sv_ps, gated, uT_ps, uT_hi_out, uT_lo_out = (
            sem(n) for n in ("zb_out", "gelu_out", "vvar", "vdev", "v_ready", "sv_ps", "gated", "uT_ps",
                             "uT_hi_out", "uT_lo_out"))
        logit_ps, mdif, mgate, mask_ready, rank_ps, meta_ready = (
            sem(n) for n in ("logit_ps", "mdif", "mgate", "mask_ready", "rank_ps", "meta_ready"))
        pick_ready, picked_ps, xe32_out, xe_ready = (
            sem(n) for n in ("pick_ready", "picked_ps", "xe32_out", "xe_ready"))
        ggT_ps, ggT_out, ye_ready, spread_ps, acc_out = (
            sem(n) for n in ("ggT_ps", "ggT_out", "ye_ready", "spread_ps", "acc_out"))
        dve_step, dve_turn, dve_last = sem("dve_step"), sem("dve_turn"), sem("dve_last")

        SB = ((6, 7), (4, 5))
        XB = (4, 2)
        PB = (0, 2, 3)
        YB = (6, 0)

        def flat(t):
            return t.rearrange("p a b -> p (a b)")

        def tok(t):
            return slice(t * P, (t + 1) * P)

        def wait_landed(eng, pos):
            eng.wait_ge(landed[pos % SLOTS], 16 * (pos // SLOTS + 1))

        block = ctx.enter_context(nc.Block())

        @block.sync
        def _(sp):
            for r0, n, vec in ((0, 48, ada_b[0]), (48, 48, ada_b[1]), (96, 8, c[0]), (104, 8, conv_dw_b[0]),
                               (112, 8, conv_ln_g[0]), (120, 8, conv_ln_b[0])):
                sp.dma_start(vecs[r0:r0 + n, :], vec.rearrange("(j p) -> j p", p=P)).then_inc(vec_landed, 16)
            sp.dma_start(vecs2[0:24, :], ln_g.rearrange("l n (j p) -> (l n j) p", p=P)[0:24, :]).then_inc(vec_landed, 16)
            sp.dma_start(vecs2[24:48, :], ln_b.rearrange("l n (j p) -> (l n j) p", p=P)[0:24, :]).then_inc(vec_landed, 16)
            for pos, (kind, n, src) in enumerate(units):
                if pos >= SLOTS:
                    k0, n0, _ = units[pos - SLOTS]
                    if k0 == "ada":
                        sp.wait_ge(ada_used, n0 + 1)
                    else:
                        sp.wait_ge(lo_ready, 2 * n0 + 2)
                dst = ring[:, pos % SLOTS, :].rearrange("p (k n) -> p k n", k=src.shape[1])
                sp.dma_start(dst, src).then_inc(landed[pos % SLOTS], 16)
                if pos == 1:
                    sp.dma_start(xs[:, :, :], x[0].rearrange("(t p) d -> p t d", p=P)).then_inc(x_landed, 16)

            w_in = moe_w_in[0].rearrange("e (k p) n -> e p k n", p=P)
            w_out = moe_w_out[0].rearrange("e (k p) n -> e p k n", p=P)

            def expert(e, i, wholly):
                for u in range(FFU):
                    h = 2 * (MOE + u - SLOTS) + 2
                    if wholly is None:
                        sp.wait_ge(half_used, i * (2 * FFU) + h)
                    else:
                        sp.wait_ge(lo_ready, i * (2 * FFU) + h)
                        sp.sem_inc(lo_seen, 1)
                        sp.wait_ge(half_used, (i * (2 * FFU) + wholly[u >= SLOTS]) + (h - 4))
                    if u < INU:
                        j, part, kh = u // 4, (u % 4) // 2, u % 2
                        src = w_in[bass.ds(e, 1), :, 4 * kh:4 * kh + 4, part * F + j * BANK:part * F + (j + 1) * BANK]
                    else:
                        src = w_out[bass.ds(e, 1), :, 2 * (u - INU):2 * (u - INU) + 2, :]
                    k = src.shape[2]
                    src = src.rearrange("e p k n -> (e p) k n")
                    dst = ring[:, u % SLOTS, :].rearrange("p (k n) -> p k n", k=k)
                    sp.dma_start(dst, src).then_inc(landed[u % SLOTS], 16)

            def freed(i):
                return [sp.value_load(metai[0:1, bass.ds(i + (XF + v), 1)], min_val=0, max_val=1) * 4
                        for v in range(2)]

            expert(0, 0, None)
            sp.wait_ge(meta_ready, 1)
            with sp.Fori(1, E) as i:
                expert(i, i, freed(i))
            items = sp.value_load(metai[0:1, 4:5], min_val=E, max_val=NCOL - 1)
            with sp.If(items > E):
                with sp.Fori(E, items) as i:
                    e = sp.value_load(metai[0:1, bass.ds(i - E, 1)], min_val=0, max_val=E - 1)
                    expert(e, i, freed(i))
                sp.nop()
            for t in range(NT):
                sp.wait_ge(x_ready, 2 * 3 + t + 1)
                sp.dma_start(out[0, tok(t), :], xs[:, t, :]).then_inc(stored, 16)
            sp.wait_ge(stored, 16 * NT)

        @block.gpsimd
        def _(pool):
            pool.memset(ident[:, :], 0.0).then_inc(pool_step, 1)
            pool.memset(ones[:, :], 1.0).then_inc(pool_step, 1)
            pool.memset(tri[:, :], 0.0).then_inc(pool_step, 1)
            pool.memset(sel4[:, :], 0.0).then_inc(pool_step, 1)
            pool.iota(iota_i[:, :], pattern=[[1, P]], base=0, channel_multiplier=0).then_inc(pool_step, 1)
            pool.wait_ge(pool_step, 5)
            pool.affine_select(out=ident[:, :], in_=ident[:, :], compare_op=ALU.not_equal, fill=1.0, base=0,
                               pattern=[[-1, P]], channel_multiplier=1).then_inc(consts, 1)
            pool.affine_select(out=tri[:, :], in_=tri[:, :], compare_op=ALU.is_ge, fill=1.0, base=0,
                               pattern=[[-1, P]], channel_multiplier=1).then_inc(consts, 1)
            for row, seg, layer in ((g1row[:, :], 2, 0), (g2row[:, 0, :], 5, 0), (g2row[:, 1, :], 5, 1)):
                pool.dma_start(row, ada_b[layer, seg * D:(seg + 1) * D].partition_broadcast(P)).then_inc(gb_landed, 16)
            pool.dma_start(lng[:, :], ln_g[0, 0].partition_broadcast(P)).then_inc(rows_landed, 16)
            pool.dma_start(lnb[:, :], ln_b[0, 0].partition_broadcast(P)).then_inc(rows_landed, 16)
            pool.wait_ge(misc_landed, 64)
            pool.affine_select(out=wsm[:, :, :], in_=wsr[:, :, :], compare_op=ALU.is_ge, fill=0.0, base=0,
                               pattern=[[0, G], [-1, P]], channel_multiplier=1).then_inc(ws_masked, 1)
            pool.wait_ge(vec_out, 2)
            for n in range(DIAGS):
                ch, k = DVE_CH + n // TAPS, n % TAPS
                if n >= 8:
                    pool.wait_ge(diag_used, n - 7)
                pool.tensor_scalar(diag[:, n % 8, :], ident[:, :], dwT[:, ch, k:k + 1], None,
                                   ALU.mult).then_inc(diag_ready, 1)

            def norm_rows(q):
                pool.wait_ge(rows_used, q)
                pool.dma_start(lng[:, :], ln_g[q // 2, q % 2].partition_broadcast(P)).then_inc(rows_landed, 16)
                pool.dma_start(lnb[:, :], ln_b[q // 2, q % 2].partition_broadcast(P)).then_inc(rows_landed, 16)

            norm_rows(1)
            pool.dma_start(g1row[:, :], ada_b[1, 2 * D:3 * D].partition_broadcast(P)).then_inc(gb_landed, 16)
            pool.wait_ge(x_ready, 4)
            pool.dma_start(s_lng[:, :], sgu_ln_g[0].partition_broadcast(P)).then_inc(sln_landed, 16)
            pool.dma_start(s_lnb[:, :], sgu_ln_b[0].partition_broadcast(P)).then_inc(sln_landed, 16)
            for q in range(8):
                if q >= 2:
                    pool.wait_ge(zb_out, q - 1)
                col = HS + q * BANK if q < 4 else (q - 4) * BANK
                pool.dma_start(brow[:, q % 2, :], sgu_b_in[0, col:col + BANK].partition_broadcast(P))\
                    .then_inc(brow_landed[q % 2], 16)
            norm_rows(2)
            norm_rows(3)

        @block.tensor
        def _(pe):
            def three(o, a_hi, a_lo, b_hi, b_lo, start, stop):
                nc.tensor.matmul(o, a_hi, b_hi, start=start, stop=False)
                nc.tensor.matmul(o, a_hi, b_lo, start=False, stop=False)
                return nc.tensor.matmul(o, a_lo, b_hi, start=False, stop=stop)

            def ada_rows(n, bank):
                if n:
                    pe.wait_ge(ada_copied, n)
                for kh in range(2):
                    pos = ada_at[2 * n + kh]
                    wait_landed(pe, pos)
                    for g in range(4):
                        mm = nc.tensor.matmul(ps[32 * g:32 * g + 32, bank, :], csil[:, 4 * kh + g, :],
                                              ring[:, pos % SLOTS, g * BANK:(g + 1) * BANK],
                                              start=(kh == 0), stop=(kh == 1), skip_group_check=True)
                    mm.then_inc(ada_used, 1)

            def ada_finish(n, bank):
                b = n % ADB
                pe.wait_ge(ada_copied, n + 1)
                if b // 2 in (2, 5):
                    mm = nc.tensor.matmul(ps[:, bank, :], sel4[:, :], modrow[:, :], start=True, stop=True)
                else:
                    for j in range(4):
                        mm = nc.tensor.matmul(ps[:, bank, 4 * b + j:4 * b + j + 1], modrow[:, tok(j)],
                                              sel4[:, 0:1], start=True, stop=True)
                mm.then_inc(ada_sums, 1)

            def turn_x(q, t):
                if q:
                    pe.wait_ge(x_ready, 2 * (q - 1) + t + 1)
                for k in range(KC):
                    mm = nc.tensor.transpose(ps[:, XB[t] + k // 4, (k % 4) * P:(k % 4 + 1) * P],
                                             xs[:, t, tok(k)], ident[:, :])
                mm.then_inc(xT_ps, 1)

            def out_unit_rows(h, hb, a_hi, a_lo, kc, nt, first, last, extra=None):
                pe.wait_ge(lo_ready, h + 1)
                for t in range(nt):
                    for dh in range(2):
                        mm = three(ps[:, YB[t] + dh, :], a_hi[:, kc, tok(t)], a_lo[:, kc, tok(t)],
                                   w_hi[:, hb, dh * BANK:(dh + 1) * BANK], w_lo[:, hb, dh * BANK:(dh + 1) * BANK],
                                   first, last)
                if extra is not None:
                    mm = extra_out(extra, hb % 2, kc)
                mm.then_inc(half_used, 1)

            def in_half_rows(hb, a_hi, a_lo, k0, t, bank):
                for kk in range(2):
                    k = k0 + kk
                    mm = three(ps[:, bank + t, :], a_hi[:, k, tok(t)], a_lo[:, k, tok(t)],
                               w_hi[:, hb, kk * BANK:(kk + 1) * BANK], w_lo[:, hb, kk * BANK:(kk + 1) * BANK],
                               k == 0, k == KC - 1)
                return mm

            def in_unit_rows(h, hb, a_hi, a_lo, k0, nt, bank, extra=None):
                pe.wait_ge(lo_ready, h + 1)
                for t in range(nt):
                    mm = in_half_rows(hb, a_hi, a_lo, k0, t, bank)
                if extra is not None:
                    mm = extra_in(extra, hb % 2, k0, bank + 1)
                mm.then_inc(half_used, 1)

            def first_block(h0, q):
                for t in range(NT):
                    pe.wait_ge(h_ready, 2 * q + t + 1)
                    for s in range(4):
                        if t == 0:
                            pe.wait_ge(lo_ready, h0 + s + 1)
                        if t == 0 and s == 1:
                            turn_x(q, 1)
                        mm = in_half_rows((h0 + s) % 4, hT_hi, hT_lo, 2 * s, t, 0)
                        if t:
                            mm.then_inc(half_used, 1)

            def last_rows(h0, a_hi, a_lo, n):
                for t in range(NT):
                    for s in range(4):
                        kc = n - 4 + s
                        if t == 0:
                            pe.wait_ge(lo_ready, h0 + s + 1)
                        for dh in range(2):
                            mm = three(ps[:, YB[t] + dh, :], a_hi[:, kc, tok(t)], a_lo[:, kc, tok(t)],
                                       w_hi[:, (h0 + s) % 4, dh * BANK:(dh + 1) * BANK],
                                       w_lo[:, (h0 + s) % 4, dh * BANK:(dh + 1) * BANK], False, kc == n - 1)
                        if s == 3 and t == 0:
                            mm.then_inc(y_done, 1)
                        if t:
                            mm.then_inc(half_used, 1)

            def extra_in(slot, s, k0, bank):
                for kk in range(2):
                    for g in range(4):
                        w0 = s * HALF + kk * BANK + g * P
                        mm = nc.tensor.matmul(ps[32 * g:32 * g + 32, bank, 0:P], xx[:, k0 + kk, :],
                                              ring[:, slot, w0:w0 + P], start=(k0 + kk == 0),
                                              stop=(k0 + kk == KC - 1), skip_group_check=True)
                return mm

            def extra_out(slot, s, kc):
                for g in range(4):
                    w0 = s * HALF + g * (D // 4)
                    mm = nc.tensor.matmul(ps[32 * g:32 * g + 32, 1, 0:D // 4], hidx_T[:, kc, :],
                                          ring[:, slot, w0:w0 + D // 4], start=(kc == 0), stop=(kc == FC - 1),
                                          skip_group_check=True)
                return mm

            def swiglu(h0, c0, nt, a_hi, a_lo, hid, e_hi, e_lo, after, extra=False):
                for u in range(FFU):
                    j, b_part, kh = u // 4, (u % 4) // 2, u % 2
                    if nt == NT and u < 2:
                        if u == 0:
                            first_block(h0, 1)
                    elif nt == NT and u >= FFU - 2:
                        if u == FFU - 2:
                            last_rows(h0 + (2 * FFU - 4), e_hi, e_lo, FC)
                    elif u < INU:
                        if kh == 0:
                            pe.wait_ge(hid_out if b_part else silu_out, c0 + j)
                        for s in range(2):
                            in_unit_rows(h0 + (2 * u + s), (2 * u + s) % 4, a_hi, a_lo, 4 * kh + 2 * s, nt,
                                         2 * b_part, u % SLOTS if extra else None)
                    else:
                        for s in range(2):
                            kc = 2 * (u - INU) + s
                            if kc % 4 == 0:
                                pe.wait_ge(hidT_lo, c0 + (kc // 4 + 1))
                            if u == INU and s == 0:
                                pe.wait_ge(silu_out, c0 + NJ)
                            out_unit_rows(h0 + (2 * u + s), (2 * u + s) % 4, e_hi, e_lo, kc, nt,
                                          kc == 0, kc == FC - 1, u % SLOTS if extra else None)
                    if u % 4 == 1 and 5 <= u <= INU + 1:
                        j = (u - 5) // 4
                        pe.wait_ge(hid_out, c0 + (j + 1))
                        pe.wait_ge(hidT_lo, c0 + j)
                        for t in range(nt):
                            for f in range(4):
                                mm = nc.tensor.transpose(ps[:, 4 + t, f * P:(f + 1) * P], hid[:, t, tok(f)],
                                                         ident[:, :])
                        if nt == 1:
                            mm = nc.tensor.transpose(ps[:, 5, 0:P], hidx[:, :], ident[:, :])
                        mm.then_inc(hidT_ps, 1)
                    after(u)

            pe.wait_ge(consts, 6)
            pe.wait_ge(vec_landed, 16 * 8)
            nc.tensor.transpose(ps[:, 6, 0:P], vecs[:, :], ident[:, :])
            nc.tensor.transpose(ps[:, 6, P:P + 48], vecs2[:, :], ident[0:48, 0:48]).then_inc(vec_ps, 1)
            pe.wait_ge(misc_landed, 64)
            for k in range(KC):
                nc.tensor.transpose(ps[:, 5, TAPS * k:TAPS * (k + 1)], dwrow[:, tok(k)], ident[0:TAPS, 0:TAPS])
            nc.tensor.transpose(ps[:, 5, 256:256 + G], bsrow[:, :], ident[0:G, 0:G]).then_inc(vec_ps, 1)
            pe.wait_ge(csil_ready, 1)
            pe.wait_ge(vec_out, 3)
            ada_rows(0, 6)
            pe.wait_ge(x_landed, 16)
            for t in range(NT):
                turn_x(0, t)
            for n in range(4):
                if n:
                    pe.wait_ge(ada_out, n)
                ada_finish(n, 7)
                if n < 3:
                    ada_rows(n + 1, 6)
                if n == 0:
                    pe.wait_ge(ws_masked, 1)
                    for g in range(G):
                        mm = nc.tensor.transpose(ps[:, g // 4, (g % 4) * P:(g % 4 + 1) * P], wsm[:, g, :], ident[:, :])
                    mm.then_inc(ws_ps, 1)

            pe.wait_ge(h_ready, 2)
            pe.wait_ge(ws_out, 1)
            pe.wait_ge(ada_out, 4)
            for i in range(8):
                blk, part, kh = i // 4, (i % 4) // 2, i % 2
                if blk and kh == 0:
                    pe.wait_ge(glu_out if part else sig_out, 1)
                for s in range(2):
                    h = 2 * i + s
                    pe.wait_ge(lo_ready, h + 1)
                    for ch in range(4):
                        for kk in range(2):
                            k = 4 * kh + 2 * s + kk
                            w = slice(kk * BANK + ch * P, kk * BANK + (ch + 1) * P)
                            mm = three(ps[:, 4 * part + ch, 0:S], w_hi[:, h % 4, w], w_lo[:, h % 4, w],
                                       hT_hi[:, k, :], hT_lo[:, k, :], k == 0, k == KC - 1)
                    mm.then_inc(half_used, 1)
            pe.wait_ge(glu_out, 2)
            for n in range(4, ADB):
                ada_rows(n, 0)
                for m in range(DIAGS * (n - 4) // 8, DIAGS * (n - 3) // 8):
                    ch, k = DVE_CH + m // TAPS, m % TAPS
                    pe.wait_ge(diag_ready, m + 1)
                    nc.tensor.matmul(ps[:, ch, 0:S], diag[:, m % 8, :], ypad[:, ch, k:k + S],
                                     start=(k == 0), stop=(k == TAPS - 1)).then_inc(diag_used, 1)
                pe.wait_ge(ada_out, n - 2)
                ada_finish(n, 1 + n % 3)
            order = (0, 1, 5, 6, 7, 2, 3, 4)
            for n, ch in enumerate(order):
                if n in (0, 5):
                    pe.wait_ge(taps_out, 2 if n == 0 else 5)
                if n == 2:
                    pe.wait_ge(dconv_out, KC - DVE_CH)
                mm = nc.tensor.matmul(ps[:, 4, 0:S], ones[:, :], ycv[:, ch, :], start=(n == 0), stop=(n == KC - 1))
            mm.then_inc(mean_ps, 1)
            for ch in range(KC):
                if ch % 4 == 0:
                    pe.wait_ge(squared, ch // 4 + 1)
                mm = nc.tensor.matmul(ps[:, 5, 0:S], ones[:, :], ysq[:, ch, :], start=(ch == 0), stop=(ch == KC - 1))
            mm.then_inc(var_ps, 1)
            pe.wait_ge(ada_out, ADB)
            pe.wait_ge(y_ready, 1)
            for kc in range(KC - 4):
                h = 2 * CONV_OUT + kc
                out_unit_rows(h, h % 4, y_hi, y_lo, kc, NT, kc == 0, False)
            pe.wait_ge(y_ready, 2)
            last_rows(2 * FFN - 4, y_hi, y_lo, KC)

            turn_x(1, 0)

            def ada_between(u):
                if u < INU and u % 2 and u // 2 < ADB:
                    ada_rows(ADB + u // 2, 6)
                if u < INU and u % 2 == 0 and 1 <= u // 2 <= ADB:
                    n = ADB + u // 2 - 1
                    pe.wait_ge(ada_out, n)
                    ada_finish(n, 7)
                if u == INU - 1:
                    pe.wait_ge(ada_out, 2 * ADB)

            swiglu(2 * FFN, 0, NT, hT_hi, hT_lo, f_hid, hid_hi, hid_lo, ada_between)

            turn_x(2, 0)
            first_block(2 * SGU, 2)
            for i in range(2, 16):
                q, kh = i // 2, i % 2
                if kh == 0 and q >= 2:
                    pe.wait_ge(zb_out, q - 1)
                for s in range(2):
                    h = 2 * (SGU + i) + s
                    in_unit_rows(h, h % 4, hT_hi, hT_lo, 4 * kh + 2 * s, NT, 2 * (q % 2))
            for t in range(NT):
                pe.wait_ge(v_ready, t + 1)
                if t:
                    pe.wait_ge(zb_out, 8)
                for g in range(G):
                    mm = nc.tensor.matmul(ps[:, (0 if t else 4) + g // 2, (g % 2) * GW:(g % 2 + 1) * GW],
                                          wsT[:, g, :], vv[:, t, g * GW:(g + 1) * GW], start=True, stop=True)
                mm.then_inc(sv_ps, 1)
            for r in range(2 * NT * 2):
                t, m = r % 2, r // 2
                pe.wait_ge(gated, NT if r else NT)
                if r >= 4:
                    pe.wait_ge(uT_lo_out, r - 3)
                for f in range(4):
                    mm = nc.tensor.transpose(ps[:, XB[t] + m % 2, f * P:(f + 1) * P],
                                             uu[:, t, tok(4 * m + f)], ident[:, :])
                mm.then_inc(uT_ps, 1)
            for m in range(HC // 2 - 2):
                for s in range(2):
                    kc = 2 * m + s
                    if kc % 4 == 0:
                        pe.wait_ge(uT_lo_out, 2 * (kc // 4 + 1))
                    h = 2 * (SGU_OUT + m) + s
                    out_unit_rows(h, h % 4, uT_hi, uT_lo, kc, NT, kc == 0, False)
            last_rows(2 * MOE - 4, uT_hi, uT_lo, HC)

            for t in range(NT):
                turn_x(3, t)
            for t in range(NT):
                pe.wait_ge(h32_out, 6 + t + 1)
                for k in range(KC):
                    mm = nc.tensor.matmul(ps[:, 6, t * E:(t + 1) * E], h32[:, k, tok(t)], router[:, k, :],
                                          start=(k == 0), stop=(k == KC - 1))
                mm.then_inc(logit_ps, 1)
            pe.wait_ge(mask_ready, 1)
            nc.tensor.matmul(ps[:, 7, 0:E], tri[:, :], mask[:, 0, :], start=True, stop=True)
            nc.tensor.matmul(ps[:, 7, E:2 * E], ones[:, :], mask[:, 0, :], start=True, stop=False)
            nc.tensor.matmul(ps[:, 7, E:2 * E], tri[:, :], mask[:, 1, :], start=False, stop=True)
            nc.tensor.matmul(ps[:, 7, 2 * E:3 * E], ones[:, :], mask[:, 0, :], start=True, stop=False)
            nc.tensor.matmul(ps[:, 7, 2 * E:3 * E], ones[:, :], mask[:, 1, :], start=False, stop=True)\
                .then_inc(rank_ps, 1)

            def pick():
                for k in range(KC):
                    for t in range(NT):
                        mm = nc.tensor.matmul(ps[:, PB[k // 3], (k % 3) * CAP:(k % 3 + 1) * CAP],
                                              xs[:, t, tok(k)], oneh[:, t, :], start=(t == 0), stop=(t == NT - 1))
                mm.then_inc(picked_ps, 1)

            def spread(extra):
                for t in range(NT):
                    for dh in range(2):
                        cols = slice(dh * BANK, (dh + 1) * BANK)
                        mm = nc.tensor.matmul(ps[:, SB[t][dh], :], ggT[:, t, :], ye[:, cols], start=True,
                                              stop=not extra)
                        if extra:
                            mm = nc.tensor.matmul(ps[:, SB[t][dh], :], ggT[:, NT + t, :], yex[:, cols],
                                                  start=False, stop=True)
                mm.then_inc(spread_ps, 1)

            def spread_last(flag):
                with pe.If(flag > 0):
                    spread(True)
                with pe.Else():
                    spread(False)
                pe.nop()

            pe.wait_ge(pick_ready, 1)
            pick()
            pe.wait_ge(meta_ready, 1)
            items = pe.value_load(metai[0:1, 4:5], min_val=E, max_val=NCOL - 1)
            with pe.Fori(0, items) as i:
                was_extra = pe.value_load(metai[0:1, bass.ds(i + XF, 1)], min_val=0, max_val=1)
                is_extra = pe.value_load(metai[0:1, bass.ds(i + (XF + 1), 1)], min_val=0, max_val=1)

                def between(u):
                    if u == 1:
                        pe.wait_ge(ye_ready, i + 1)
                        spread_last(was_extra)
                    if u == 4:
                        pe.wait_ge(acc_out, i + 1)
                        for t in range(NT):
                            nc.tensor.transpose(ps[:, 6, tok(t)], ggate[:, t, :], ident[:, :])
                        for t in range(NT):
                            mm = nc.tensor.transpose(ps[:, 6, tok(NT + t)], ggx[:, t, :], ident[:, :])
                        mm.then_inc(ggT_ps, 1)
                    if u == INU + 3:
                        pe.wait_ge(pick_ready, i + 2)
                        pick()
                    if u == INU - 1:
                        pe.wait_ge(ggT_out, i + 1)

                pe.wait_ge(xe_ready, i + 1)
                h0, c0 = i * (2 * FFU) + 2 * MOE, i * NJ + NJ
                with pe.If(is_extra > 0):
                    pe.wait_ge(ye_ready, i + 1)
                    swiglu(h0, c0, 1, xe_hi, xe_lo, e_hid, eh_hi, eh_lo, between, True)
                with pe.Else():
                    swiglu(h0, c0, 1, xe_hi, xe_lo, e_hid, eh_hi, eh_lo, between)
                pe.nop()
            pe.wait_ge(ye_ready, items + 1)
            spread_last(pe.value_load(metai[0:1, bass.ds(items + XF, 1)], min_val=0, max_val=1))

        @block.scalar
        def _(act):
            def split(pos_slot, landed_count, h, hb, first):
                if first:
                    act.wait_ge(landed[pos_slot], landed_count)
                return nc.scalar.activation(w_hi[:, hb, :], ring[:, pos_slot, (hb % 2) * HALF:(hb % 2 + 1) * HALF],
                                            ACT.Copy).then_inc(hi_ready, 1)

            def split_unit(n):
                pos = split_at[n]
                for s in range(2):
                    h = 2 * n + s
                    if h >= 4:
                        act.wait_ge(half_used, h - 3)
                    split(pos % SLOTS, 16 * (pos // SLOTS + 1), h, h % 4, s == 0)

            def ada_copy(n, bank):
                act.wait_ge(ada_used, 2 * n + 2)
                if n:
                    act.wait_ge(ada_sums, n)
                nc.scalar.activation(modrow[:, :], ps[:, bank, :], ACT.Copy).then_inc(ada_copied, 1)

            def modulate(q, gain, shift, tiles=(0, 1)):
                for t in tiles:
                    act.wait_ge(xT_ps, 2 * q + t + 1)
                    if t == 0 and q == 0:
                        act.wait_ge(ada_out, 4)
                    elif t == 0:
                        act.wait_ge(ab_ready, q)
                    for k in range(KC):
                        op = nc.scalar.activation(h32[:, k, tok(t)], ps[:, XB[t] + k // 4, (k % 4) * P:(k % 4 + 1) * P],
                                                  ACT.Identity, bias=shift[:, k:k + 1], scale=gain[:, k:k + 1])
                    op.then_inc(h32_out, 1)

            def deviation(q, t):
                act.wait_ge(var_ready, 2 * q + t + 1)
                nc.scalar.activation(dev[:, t:t + 1], var[:, t:t + 1], ACT.Sqrt).then_inc(dev_ready, 1)

            def next_stage(q, n):
                split_unit(n)
                deviation(q, 0)
                split_unit(n + 1)
                modulate(q + 1, ab[:, q, 0, :], ab[:, q, 1, :], (0,))
                deviation(q, 1)
                modulate(q + 1, ab[:, q, 0, :], ab[:, q, 1, :], (1,))

            def swiglu(h0, c0, nt, unit, sil, e_hi, after):
                for u in range(FFU):
                    unit(u)
                    if u % 4 == 3 and u < INU:
                        j = (u - 3) // 4
                        act.wait_ge(half_used, h0 + 2 * (4 * j + 2))
                        act.wait_ge(hid_out, c0 + j)
                        op = nc.scalar.activation(sil[:, 0:nt, :], ps[:, 0:nt, :], ACT.Silu)
                        if nt == 1:
                            op = nc.scalar.activation(silx[:, :], ps[:, 1, 0:P], ACT.Silu)
                        op.then_inc(silu_out, 1)
                    if u % 4 == 3 and 7 <= u <= INU + 3:
                        j = (u - 7) // 4
                        act.wait_ge(hidT_ps, c0 + (j + 1))
                        if nt == 1:
                            nc.scalar.activation(hidx_T[:, 4 * j:4 * j + 4, :],
                                                 ps[:, 5, 0:P].rearrange("p (k n) -> p k n", k=4), ACT.Copy)
                        for t in range(nt):
                            op = nc.scalar.activation(e_hi[:, 4 * j:4 * j + 4, tok(t)],
                                                      ps[:, 4 + t, :].rearrange("p (k n) -> p k n", k=4), ACT.Copy)
                        op.then_inc(hidT_hi, 1)
                    after(u)

            act.dma_start(dwrow[:, :], conv_dw[0]).then_inc(misc_landed, 16)
            act.dma_start(bsrow[:, :], sgu_b_s[0]).then_inc(misc_landed, 16)
            act.dma_start(wsr[:, :, :], sgu_w_s[0].rearrange("g t s -> t g s")).then_inc(misc_landed, 16)
            act.dma_start(router[:, :, :], moe_router[0].rearrange("(k p) e -> p k e", p=P)).then_inc(misc_landed, 16)
            act.wait_ge(vec_out, 1)
            nc.scalar.activation(csil[:, :, :], vcols[:, 96:104].unsqueeze(2).broadcast_to([P, KC, 32]), ACT.Silu)\
                .then_inc(csil_ready, 1)
            for n in range(4):
                ada_copy(n, 6)
                if n == 1:
                    act.wait_ge(ws_ps, 1)
                    nc.scalar.activation(wsT[:, :, :], ps[:, 0:2, :].rearrange("p b (g n) -> p (b g) n", g=4), ACT.Copy)\
                        .then_inc(ws_out, 1)
            modulate(0, mods[:, 0, 1, :], mods[:, 0, 0, :])
            split_unit(0)
            split_unit(1)

            for i in range(2, 8):
                split_unit(i)
                if i % 4 == 3:
                    blk = i // 4
                    act.wait_ge(half_used, 8 * blk + 4)
                    if blk:
                        act.wait_ge(glu_out, 1)
                    nc.scalar.activation(sig[:, :, :], ps[:, 0:4, 0:S], ACT.Sigmoid).then_inc(sig_out, 1)
            done = 0
            for n in range(4, ADB + 1):
                if n < ADB:
                    ada_copy(n, 0)
                while (done + 1) * TAPS <= DIAGS * (n - 4) // 8:
                    ch = DVE_CH + done
                    done += 1
                    act.wait_ge(diag_used, done * TAPS)
                    nc.scalar.activation(ycv[:, ch, :], ps[:, ch, 0:S], ACT.Identity, bias=vcols[:, 104 + ch:105 + ch])\
                        .then_inc(dconv_out, 1)
            for hf in range(2):
                act.wait_ge(centred, hf + 1)
                nc.scalar.activation(ysq[:, 4 * hf:4 * hf + 4, :], ycv[:, 4 * hf:4 * hf + 4, :], ACT.Square)\
                    .then_inc(squared, 1)
            act.wait_ge(cvar, 1)
            nc.scalar.activation(cst[:, 2, :], cst[:, 1, :], ACT.Sqrt).then_inc(cdev, 1)
            for i in range(2):
                split_unit(CONV_OUT + i)
            for hf in range(2):
                act.wait_ge(normed, hf + 1)
                for ch in range(4 * hf, 4 * hf + 4):
                    op = nc.scalar.activation(ysq[:, ch, :], ycv[:, ch, :], ACT.Silu,
                                              bias=vcols[:, 120 + ch:121 + ch], scale=vcols[:, 112 + ch:113 + ch])
                op.then_inc(cact, 1)
            for i in range(2, 4):
                split_unit(CONV_OUT + i)
            next_stage(0, FFN)

            def ffn_unit(u):
                if u >= 2:
                    split_unit(FFN + u)

            def ada_between(u):
                if u % 2 and 0 <= (u - 3) // 2 < ADB and u >= 3:
                    ada_copy(ADB + (u - 3) // 2, 6)

            swiglu(2 * FFN, 0, NT, ffn_unit, f_sil, hid_hi, ada_between)
            next_stage(1, SGU)

            def gelu(q):
                act.wait_ge(zb_out, q + 1)
                z = vv if q < 4 else uu
                nc.scalar.activation(z[:, :, (q % 4) * BANK:(q % 4 + 1) * BANK],
                                     z[:, :, (q % 4) * BANK:(q % 4 + 1) * BANK], ACT.Gelu).then_inc(gelu_out, 1)

            for i in range(2, 18):
                split_unit(SGU + i)
                if i % 2:
                    gelu((i - 3) // 2)
                if i in (10, 12):
                    t = (i - 10) // 2
                    act.wait_ge(vvar, t + 1)
                    nc.scalar.activation(dev[:, t:t + 1], var[:, t:t + 1], ACT.Sqrt).then_inc(vdev, 1)
            for r in range(8):
                t, m = r % 2, r // 2
                act.wait_ge(uT_ps, r + 1)
                nc.scalar.activation(uT_hi[:, 4 * m:4 * m + 4, tok(t)],
                                     ps[:, XB[t] + m % 2, :].rearrange("p (k n) -> p k n", k=4), ACT.Copy)\
                    .then_inc(uT_hi_out, 1)
            for m in range(2, HC // 2):
                split_unit(SGU_OUT + m)

            def moe_unit(i):
                def unit(u):
                    for s in range(2):
                        act.wait_ge(half_used, i * (2 * FFU) + (2 * (MOE + u) + s - 3))
                        split(u % SLOTS, i * (16 * FFU // SLOTS) + 16 * ((MOE_AT + u) // SLOTS + 1), None,
                              (2 * u + s) % 4, s == 0)
                return unit

            deviation(2, 0)
            modulate(3, ab[:, 2, 0, :], ab[:, 2, 1, :], (0,))
            deviation(2, 1)
            modulate(3, ab[:, 2, 0, :], ab[:, 2, 1, :], (1,))
            act.wait_ge(mdif, 1)
            nc.scalar.activation(tgate[:, :, 0:1], tdif[:, :, :], ACT.Sigmoid, scale=-1.0).then_inc(mgate, 1)
            nc.scalar.activation(tgate[:, :, 1:2], tdif[:, :, :], ACT.Sigmoid).then_inc(mgate, 1)

            def modulate_item():
                for k in range(KC):
                    op = nc.scalar.activation(xe32[:, k, :], ps[:, PB[k // 3], (k % 3) * CAP:(k % 3) * CAP + P],
                                              ACT.Identity, bias=ab[:, 2, 1, k:k + 1], scale=ab[:, 2, 0, k:k + 1])
                op.then_inc(xe32_out, 1)

            act.wait_ge(picked_ps, 1)
            modulate_item()
            act.wait_ge(meta_ready, 1)
            items = act.value_load(metai[0:1, 4:5], min_val=E, max_val=NCOL - 1)
            with act.Fori(0, items) as i:
                def between(u):
                    if u == 6:
                        act.wait_ge(ggT_ps, i + 1)
                        nc.scalar.activation(ggT[:, :, :], ps[:, 6, :].rearrange("p (t n) -> p t n", t=2 * NT),
                                             ACT.Copy).then_inc(ggT_out, 1)
                    if u == INU + 5:
                        act.wait_ge(picked_ps, i + 2)
                        modulate_item()

                swiglu(i * (2 * FFU) + 2 * MOE, i * NJ + NJ, 1, moe_unit(i), e_sil, eh_hi, between)
            act.wait_ge(var_ready, 7)
            nc.scalar.activation(dev[:, 0:1], var[:, 0:1], ACT.Sqrt).then_inc(dev_ready, 1)
            act.wait_ge(var_ready, 8)
            nc.scalar.activation(dev[:, 1:2], var[:, 1:2], ACT.Sqrt).then_inc(dev_ready, 1)

        @block.vector
        def _(dve):
            steps = [0]

            def link(ins):
                steps[0] += 1
                ins.then_inc(dve_step, 1)
                dve.wait_ge(dve_step, steps[0])

            def split_unit(n):
                for s in range(2):
                    h = 2 * n + s
                    dve.wait_ge(hi_ready, h + 1)
                    if h >= 4:
                        dve.wait_ge(half_used, h - 3)
                    nc.vector.tensor_tensor(w_lo[:, h % 4, :],
                                            ring[:, split_at[n] % SLOTS, s * HALF:(s + 1) * HALF],
                                            w_hi[:, h % 4, :].bitcast(F32), ALU.subtract).then_inc(lo_ready, 1)

            def ada_take(n, bank):
                layer, b = n // ADB, n % ADB
                dve.wait_ge(ada_sums, n + 1)
                if b // 2 in (2, 5):
                    row = g1row[:, :] if b // 2 == 2 else g2row[:, layer, :]
                    row = row[:, (b % 2) * BANK:(b % 2 + 1) * BANK]
                    dve.wait_ge(gb_landed, 64 if layer else 48)
                    op = nc.vector.scalar_tensor_tensor(out=row, in0=ps[:, bank, :], scalar=1.0, in1=row,
                                                        op0=ALU.add, op1=ALU.add)
                else:
                    op = nc.vector.tensor_tensor(mods[:, layer, b // 2, 4 * (b % 2):4 * (b % 2) + 4],
                                                 ps[:, bank, 4 * b:4 * b + 4],
                                                 modb[:, 48 * layer + 4 * b:48 * layer + 4 * b + 4], ALU.add)
                op.then_inc(ada_out, 1)

            def split_h(q, t):
                dve.wait_ge(h32_out, 2 * q + t + 1)
                link(nc.vector.tensor_copy(hT_hi[:, :, tok(t)], h32[:, :, tok(t)]))
                nc.vector.tensor_tensor(hT_lo[:, :, tok(t)], h32[:, :, tok(t)],
                                        hT_hi[:, :, tok(t)].bitcast(F32), ALU.subtract).then_inc(h_ready, 1)

            def merge(q, layer, sh, sc):
                link(nc.vector.tensor_tensor(ab[:, q, 0, :], lncols[:, 0, q, :], mods[:, layer, sc, :], ALU.mult))
                link(nc.vector.tensor_tensor(ab[:, q, 1, :], lncols[:, 1, q, :], mods[:, layer, sc, :], ALU.mult))
                nc.vector.tensor_tensor(ab[:, q, 1, :], ab[:, q, 1, :], mods[:, layer, sh, :], ALU.add)\
                    .then_inc(ab_ready, 1)

            def variance(t, row, width, ready):
                n = width // BANK
                for k in range(n):
                    op = nc.vector.bn_stats(stats[:, t, k, :], row[:, k * BANK:(k + 1) * BANK])
                link(op)
                link(nc.vector.bn_aggr(mv[:, t, :], stats[:, t, 0:n, :].rearrange("p a b -> p (a b)")))
                nc.vector.tensor_scalar(var[:, t:t + 1], mv[:, t, 1:2], 1e-5, None, ALU.add).then_inc(ready, 1)

            def standardise(t, row, out_row, ready, count):
                dve.wait_ge(ready, count)
                link(nc.vector.reciprocal(rstd[:, t:t + 1], dev[:, t:t + 1]))
                return nc.vector.tensor_scalar(out_row, row, mv[:, t, 0:1], rstd[:, t:t + 1], ALU.subtract, ALU.mult)

            def residual(q, t, grow):
                if t == 0:
                    dve.wait_ge(y_done, q + 1)
                else:
                    dve.wait_ge(half_used, 2 * (FFN, SGU, MOE)[q])
                ztmp = ztmp_late if q == 2 else ztmp_early
                y = ps[:, YB[t]:YB[t] + 2, :].rearrange("p a b -> p (a b)")
                link(nc.vector.tensor_tensor(ztmp[:, t, :], y, grow, ALU.mult))
                link(nc.vector.scalar_tensor_tensor(out=xs[:, t, :], in0=xs[:, t, :], scalar=ALPHA,
                                                    in1=ztmp[:, t, :], op0=ALU.mult, op1=ALU.add))
                variance(t, xs[:, t, :], D, var_ready)

            def next_stage(q, grow, n):
                residual(q, 0, grow)
                split_unit(n)
                standardise(0, xs[:, 0, :], xs[:, 0, :], dev_ready, 2 * q + 1).then_inc(x_ready, 1)
                residual(q, 1, grow)
                split_h(q + 1, 0)
                standardise(1, xs[:, 1, :], xs[:, 1, :], dev_ready, 2 * q + 2).then_inc(x_ready, 1)
                split_unit(n + 1)
                split_h(q + 1, 1)

            def gain_and_bias(q):
                dve.wait_ge(rows_landed, 32 * (q + 1))
                dve.wait_ge(xT_ps, 2 * (q + 1) + 2)
                for t in range(NT):
                    link(nc.vector.tensor_tensor(xs[:, t, :], xs[:, t, :], lng[:, :], ALU.mult))
                    op = nc.vector.tensor_tensor(xs[:, t, :], xs[:, t, :], lnb[:, :], ALU.add)
                op.then_inc(rows_used, 1)
                dve.wait_ge(rows_used, q + 1)

            def swiglu(h0, c0, nt, unit, sil, hid, e_hi, e_lo, after):
                for u in range(FFU):
                    unit(u)
                    if u % 4 == 1 and 5 <= u <= INU + 1:
                        j = (u - 5) // 4
                        dve.wait_ge(half_used, h0 + 2 * (4 * j + 4))
                        dve.wait_ge(silu_out, c0 + (j + 1))
                        dve.wait_ge(hidT_ps, c0 + j)
                        op = nc.vector.tensor_tensor(hid[:, 0:nt, :], ps[:, 2:2 + nt, :], sil[:, 0:nt, :], ALU.mult)
                        if nt == 1:
                            op = nc.vector.tensor_tensor(hidx[:, :], ps[:, 3, 0:P], silx[:, :], ALU.mult)
                        op.then_inc(hid_out, 1)
                    if u % 4 == 3 and 7 <= u <= INU + 3:
                        j = (u - 7) // 4
                        dve.wait_ge(hidT_hi, c0 + (j + 1))
                        for t in range(nt):
                            op = nc.vector.tensor_tensor(e_lo[:, 4 * j:4 * j + 4, tok(t)],
                                                         ps[:, 4 + t, :].rearrange("p (k n) -> p k n", k=4),
                                                         e_hi[:, 4 * j:4 * j + 4, tok(t)].bitcast(F32), ALU.subtract)
                        op.then_inc(hidT_lo, 1)
                    after(u)

            nc.vector.memset(ypad[:, :, 0:PADL], 0.0).then_inc(pad_zero, 1)
            dve.wait_ge(pool_step, 5)
            nc.vector.tensor_copy(iota[:, :], iota_i[:, :]).then_inc(iota_ready, 1)
            for r in range(0, P, 32):
                nc.vector.memset(sel4[r:r + 1, :], 1.0).then_inc(consts, 1)
            dve.wait_ge(vec_ps, 1)
            nc.vector.tensor_copy(vcols[:, :], ps[:, 6, 0:P]).then_inc(vec_out, 1)
            link(nc.vector.tensor_copy(lncols[:, :, :, :], ps[:, 6, P:P + 48].rearrange("p (v q k) -> p v q k", v=2, q=3)))
            dve.wait_ge(vec_ps, 2)
            nc.vector.tensor_copy(dwT[:, :, :], ps[:, 5, 0:KC * TAPS].rearrange("p (c k) -> p c k", c=KC))\
                .then_inc(vec_out, 1)
            nc.vector.tensor_copy(bsT[:, :], ps[:, 5, 256:256 + G]).then_inc(vec_out, 1)
            dve.wait_ge(vec_out, 3)
            link(nc.vector.tensor_copy(modb[:, :], vcols[:, 0:96]))
            for layer in range(2):
                for seg in (1, 4):
                    col = modb[:, 48 * layer + 8 * seg:48 * layer + 8 * seg + 8]
                    op = nc.vector.tensor_scalar(col, col, 1.0, None, ALU.add)
            link(op)
            for n in range(4):
                ada_take(n, 7)
            for t in range(NT):
                split_h(0, t)
            split_unit(0)
            split_unit(1)

            def glu(blk):
                dve.wait_ge(sig_out, blk + 1)
                dve.wait_ge(half_used, 8 * blk + 8)
                nc.vector.tensor_tensor(ypad[:, 4 * blk:4 * blk + 4, PADL:], ps[:, 4:8, 0:S], sig[:, :, :],
                                        ALU.mult).then_inc(glu_out, 1)

            def taps(channels, first, last):
                for k in range(first, last):
                    for ch in channels:
                        src, w = ypad[:, ch, k:k + S], dwT[:, ch, k:k + 1]
                        if k == 0:
                            op = nc.vector.tensor_scalar(ycv[:, ch, :], src, w, vcols[:, 104 + ch:105 + ch],
                                                         ALU.mult, ALU.add)
                        else:
                            dve.wait_ge(dve_step, tap_step[ch])
                            op = nc.vector.scalar_tensor_tensor(out=ycv[:, ch, :], in0=src, scalar=w,
                                                                in1=ycv[:, ch, :], op0=ALU.mult, op1=ALU.add)
                        steps[0] += 1
                        op.then_inc(dve_step, 1)
                        tap_step[ch] = steps[0]

            def taps_done(channels):
                dve.wait_ge(dve_step, max(tap_step[ch] for ch in channels))
                nc.vector.memset(cst[:, 3, 0:1], 0.0).then_inc(taps_out, len(channels))

            tap_step = {}
            for i in range(2, 6):
                split_unit(i)
            glu(0)
            dve.wait_ge(glu_out, 1)
            dve.wait_ge(pad_zero, 1)
            taps((0, 1), 0, 4)
            split_unit(6)
            taps((0, 1), 4, 8)
            split_unit(7)
            taps((0, 1), 8, 12)
            glu(1)
            dve.wait_ge(glu_out, 2)
            taps((0, 1), 12, 20)
            ada_take(4, 1 + 4 % 3)
            taps((0, 1), 20, TAPS)
            ada_take(5, 1 + 5 % 3)
            taps_done((0, 1))
            for n in range(6, ADB):
                k = TAPS * (n - 6) // 6
                taps((2, 3, 4), k, TAPS * (n - 5) // 6)
                ada_take(n, 1 + n % 3)
            taps_done((2, 3, 4))
            dve.wait_ge(ada_out, ADB)
            merge(0, 0, 3, 4)
            dve.wait_ge(mean_ps, 1)
            link(nc.vector.tensor_scalar(cst[:, 0, :], ps[:, 4, 0:S], 1.0 / D, None, ALU.mult))
            for hf in range(2):
                part = ycv[:, 4 * hf:4 * hf + 4, :]
                nc.vector.tensor_tensor(part, part, cst[:, 0:1, :].broadcast_to([P, 4, S]), ALU.subtract)\
                    .then_inc(centred, 1)
            dve.wait_ge(var_ps, 1)
            nc.vector.tensor_scalar(cst[:, 1, :], ps[:, 5, 0:S], 1.0 / D, 1e-5, ALU.mult, ALU.add).then_inc(cvar, 1)
            dve.wait_ge(cdev, 1)
            dve.wait_ge(centred, 2)
            link(nc.vector.reciprocal(cst[:, 3, :], cst[:, 2, :]))
            for hf in range(2):
                part = ycv[:, 4 * hf:4 * hf + 4, :]
                nc.vector.tensor_tensor(part, part, cst[:, 3:4, :].broadcast_to([P, 4, S]), ALU.mult)\
                    .then_inc(normed, 1)
            for i in range(2):
                split_unit(CONV_OUT + i)
            for hf in range(2):
                part = slice(4 * hf, 4 * hf + 4)
                dve.wait_ge(cact, hf + 1)
                link(nc.vector.tensor_copy(y_hi[:, part, :], ysq[:, part, :]))
                nc.vector.tensor_tensor(y_lo[:, part, :], ysq[:, part, :], y_hi[:, part, :].bitcast(F32),
                                        ALU.subtract).then_inc(y_ready, 1)
            for i in range(2, 4):
                split_unit(CONV_OUT + i)
            next_stage(0, g1row[:, :], FFN)

            def ffn_unit(u):
                if u >= 2:
                    split_unit(FFN + u)

            def ada_between(u):
                if u % 2 == 0 and u >= 4 and (u - 4) // 2 < ADB:
                    ada_take(ADB + (u - 4) // 2, 7)
                if u == 6:
                    gain_and_bias(0)
                if u == INU + 2:
                    dve.wait_ge(ada_out, 2 * ADB)
                    merge(1, 1, 0, 1)
                    merge(2, 1, 3, 4)

            swiglu(2 * FFN, 0, NT, ffn_unit, f_sil, f_hid, hid_hi, hid_lo, ada_between)
            next_stage(1, g2row[:, 0, :], SGU)

            def add_bias(q):
                dve.wait_ge(half_used, 2 * (SGU + 2 * q + 2))
                dve.wait_ge(brow_landed[q % 2], 16 * (q // 2 + 1))
                z = vv if q < 4 else uu
                for t in range(NT):
                    op = nc.vector.tensor_tensor(z[:, t, (q % 4) * BANK:(q % 4 + 1) * BANK],
                                                 ps[:, 2 * (q % 2) + t, :], brow[:, q % 2, :], ALU.add)
                op.then_inc(zb_out, 1)

            for i in range(2, 18):
                split_unit(SGU + i)
                if i == 6:
                    gain_and_bias(1)
                if i % 2:
                    add_bias((i - 3) // 2)
                if i in (10, 12):
                    t = (i - 10) // 2
                    dve.wait_ge(gelu_out, 4)
                    dve.wait_ge(sln_landed, 32)
                    variance(t, vv[:, t, :], HS, vvar)
                    link(standardise(t, vv[:, t, :], vv[:, t, :], vdev, t + 1))
                    link(nc.vector.tensor_tensor(vv[:, t, :], vv[:, t, :], s_lng[:, :], ALU.mult))
                    nc.vector.tensor_tensor(vv[:, t, :], vv[:, t, :], s_lnb[:, :], ALU.add).then_inc(v_ready, 1)
            for t in range(NT):
                dve.wait_ge(sv_ps, t + 1)
                dve.wait_ge(gelu_out, 8)
                for g in range(G):
                    u_g = uu[:, t, g * GW:(g + 1) * GW]
                    op = nc.vector.scalar_tensor_tensor(
                        out=u_g, in0=ps[:, (0 if t else 4) + g // 2, (g % 2) * GW:(g % 2 + 1) * GW],
                        scalar=bsT[:, g:g + 1], in1=u_g, op0=ALU.add, op1=ALU.mult)
                op.then_inc(gated, 1)
            for r in range(8):
                t, m = r % 2, r // 2
                dve.wait_ge(uT_hi_out, r + 1)
                nc.vector.tensor_tensor(uT_lo[:, 4 * m:4 * m + 4, tok(t)],
                                        ps[:, XB[t] + m % 2, :].rearrange("p (k n) -> p k n", k=4),
                                        uT_hi[:, 4 * m:4 * m + 4, tok(t)].bitcast(F32), ALU.subtract)\
                    .then_inc(uT_lo_out, 1)
            for m in range(2, HC // 2):
                split_unit(SGU_OUT + m)

            for t in range(NT):
                residual(2, t, g1row[:, :])
                standardise(t, xs[:, t, :], xs[:, t, :], dev_ready, 4 + t + 1).then_inc(x_ready, 1)

            for a, v in ((over, 0.0), (dest, -1.0), (gcol, 0.0)):
                nc.vector.memset(a[:, :, :], v)
            nc.vector.memset(meta[:, :], 0.0)
            nc.vector.memset(ye[:, :], 0.0)
            nc.vector.memset(yex[:, :], 0.0)
            for g in range(4):
                nc.vector.tensor_scalar(iotax[:, g * XS:(g + 1) * XS], iota[:, 0:XS], float(P), None, ALU.add)
            link(nc.vector.memset(ggT[:, :, :], 0.0))

            dve.wait_ge(logit_ps, 2)
            dve.wait_ge(iota_ready, 1)
            link(nc.vector.tensor_copy(lgt[:, :, :], ps[:, 6, 0:NT * E].rearrange("p (t e) -> p t e", t=NT)))
            for t in range(NT):
                op = nc.vector.max(top[:, t, :], lgt[:, t, :])
            link(op)
            nc.vector.tensor_tensor(tdif[:, :, :], top[:, :, 1:2], top[:, :, 0:1], ALU.subtract).then_inc(mdif, 1)
            for t in range(NT):
                op = nc.vector.max_index(topi[:, t, :], top[:, t, :], lgt[:, t, :])
            link(op)
            link(nc.vector.tensor_copy(topf[:, :, :], topi[:, :, :]))
            for t in range(NT):
                nc.vector.tensor_scalar(mask1[:, t, :], iota[:, 0:E], topf[:, t, 0:1], None, ALU.is_equal)
                op = nc.vector.tensor_scalar(mask2[:, t, :], iota[:, 0:E], topf[:, t, 1:2], None, ALU.is_equal)
            link(op)
            nc.vector.tensor_tensor(mask[:, :, :], mask1[:, :, :], mask2[:, :, :], ALU.add).then_inc(mask_ready, 1)
            dve.wait_ge(mgate, 2)
            for t in range(NT):
                op = nc.vector.tensor_scalar(gate1[:, t, :], mask1[:, t, :], tgate[:, t, 0:1], None, ALU.mult)
            link(op)
            for t in range(NT):
                op = nc.vector.scalar_tensor_tensor(out=gate[:, t, :], in0=mask2[:, t, :], scalar=tgate[:, t, 1:2],
                                                    in1=gate1[:, t, :], op0=ALU.mult, op1=ALU.add)
            dve.wait_ge(rank_ps, 1)
            dve.wait_ge(mask_ready, 1)
            for t in range(NT):
                op = nc.vector.scalar_tensor_tensor(out=rank1[:, t, :], in0=ps[:, 7, t * E:(t + 1) * E], scalar=1.0,
                                                    in1=mask[:, t, :], op0=ALU.add, op1=ALU.mult)
            link(op)
            nc.vector.tensor_scalar(dest[:, :, 0:E], rank1[:, :, :], 1.0, None, ALU.subtract)
            link(nc.vector.tensor_copy(gcol[:, :, 0:E], gate[:, :, :]))
            def choose(item):
                for t in range(NT):
                    d = dest[:, t, item]
                    nc.vector.tensor_scalar(oneh[:, t, 0:P], iota[:, :], d, None, ALU.is_equal)
                    op = nc.vector.tensor_scalar(ggate[:, t, :], iota[:, :], d, gcol[:, t, item],
                                                 ALU.is_equal, ALU.mult)
                    nc.vector.tensor_scalar(oneh[:, t, P:CAP], iotax[:, 0:XS], d, None, ALU.is_equal)
                    op = nc.vector.tensor_scalar(ggx[:, t, :], iotax[:, :], d, gcol[:, t, item],
                                                 ALU.is_equal, ALU.mult)
                op.then_inc(pick_ready, 1)

            def modulate_extra(step, n):
                dve.wait_ge(xe32_out, n)
                gain, shift = (ab[:, 2, v, :].unsqueeze(2).broadcast_to([P, KC, XS]) for v in range(2))
                for b in range(3):
                    k = slice(3 * b, min(3 * b + 3, KC))
                    picked = ps[:, PB[b], 0:(k.stop - k.start) * CAP].rearrange("p (k n) -> p k n", n=CAP)
                    op = nc.vector.tensor_tensor(xx[:, k, :], picked[:, :, P:CAP], gain[:, k, :], ALU.mult)
                step(op)
                nc.vector.tensor_tensor(xx[:, :, :], xx[:, :, :], shift, ALU.add)

            def split_item(step):
                step(nc.vector.tensor_copy(xe_hi[:, :, :], xe32[:, :, :]))
                nc.vector.tensor_tensor(xe_lo[:, :, :], xe32[:, :, :], xe_hi[:, :, :].bitcast(F32), ALU.subtract)\
                    .then_inc(xe_ready, 1)

            def take_rows():
                for g in range(4):
                    q, cols = slice(32 * g, 32 * g + 32), slice(g * (D // 4), (g + 1) * (D // 4))
                    nc.vector.tensor_tensor(yex[q, cols], ps[q, 1, 0:D // 4], g2row[q, 1, cols], ALU.mult)
                nc.vector.tensor_tensor(ye[:, :], ps[:, 6:8, :].rearrange("p a b -> p (a b)"), g2row[:, 1, :],
                                        ALU.mult).then_inc(ye_ready, 1)

            def add_rows():
                for t in range(NT):
                    for dh in range(2):
                        a = acc[:, t, dh * BANK:(dh + 1) * BANK]
                        op = nc.vector.tensor_tensor(a, ps[:, SB[t][dh], :], a, ALU.add)
                op.then_inc(acc_out, 1)

            choose(slice(0, 1))
            nc.vector.tensor_scalar(meta[:, XF + 1:XF + 1 + E], ps[:, 7, 2 * E:3 * E], float(P), None, ALU.is_gt)
            link(nc.vector.tensor_scalar(over[:, 0, E:], ps[:, 7, 2 * E:3 * E], float(CAP), None, ALU.is_gt))
            nc.vector.tensor_scalar(excess[:, :, :], rank1[:, :, :], float(CAP), 0.0, ALU.subtract, ALU.max)
            for s in range(3):
                link(nc.vector.tensor_tensor(over[:, s + 1, E:], over[:, s, E:], over[:, s, E - 2 ** s:2 * E - 2 ** s],
                                             ALU.add))
            nc.vector.tensor_scalar(meta[:, 4:5], over[:, 3, 2 * E - 1:2 * E], float(E), None, ALU.add)
            link(nc.vector.tensor_tensor(before[:, :], over[:, 3, E:], over[:, 0, E:], ALU.subtract))
            for m in range(3):
                op = nc.vector.scalar_tensor_tensor(out=oh[:, m, :], in0=before[:, :], scalar=float(m),
                                                    in1=over[:, 0, E:], op0=ALU.is_equal, op1=ALU.mult)
            link(op)
            for m in range(3):
                op = nc.vector.tensor_tensor_reduce(junk[:, 5 * m, :], oh[:, m, :], iota[:, 0:E], 1.0, 0.0, ALU.mult,
                                                    ALU.add, meta[:, m:m + 1])
            link(op)
            nc.vector.tensor_copy(metai[:, :], meta[:, :]).then_inc(meta_ready, 1)
            modulate_extra(link, 1)
            split_item(link)
            for m in range(3):
                for t in range(NT):
                    nc.vector.tensor_tensor_reduce(junk[:, 5 * m + 1 + 2 * t, :], oh[:, m, :], excess[:, t, :], 1.0,
                                                   -1.0, ALU.mult, ALU.add, dest[:, t, E + m:E + m + 1])
                    op = nc.vector.tensor_tensor_reduce(junk[:, 5 * m + 2 + 2 * t, :], oh[:, m, :], gate[:, t, :], 1.0,
                                                        0.0, ALU.mult, ALU.add, gcol[:, t, E + m:E + m + 1])
            link(op)
            dve.wait_ge(rows_landed, 96)
            for step_op in range(3):
                for t in range(NT):
                    a = acc[:, t, :]
                    if step_op == 0:
                        op = nc.vector.tensor_tensor(a, xs[:, t, :], lng[:, :], ALU.mult)
                    elif step_op == 1:
                        op = nc.vector.tensor_tensor(a, a, lnb[:, :], ALU.add)
                    else:
                        op = nc.vector.tensor_scalar(a, a, ALPHA, None, ALU.mult)
                link(op)
                if step_op == 1:
                    dve.sem_inc(rows_used, 1)
            dve.wait_ge(meta_ready, 1)
            items = dve.value_load(metai[0:1, 4:5], min_val=E, max_val=NCOL - 1)
            TURN = 2
            with dve.Fori(0, items) as i:
                turn = [0]

                def step(ins):
                    turn[0] += 1
                    ins.then_inc(dve_turn, 1)
                    dve.wait_ge(dve_turn, i * TURN + turn[0])

                def unit(u):
                    for s in range(2):
                        hb = (2 * u + s) % 4
                        dve.wait_ge(hi_ready, i * (2 * FFU) + (2 * (MOE + u) + s + 1))
                        dve.wait_ge(half_used, i * (2 * FFU) + (2 * (MOE + u) + s - 3))
                        nc.vector.tensor_tensor(w_lo[:, hb, :], ring[:, u % SLOTS, s * HALF:(s + 1) * HALF],
                                                w_hi[:, hb, :].bitcast(F32), ALU.subtract).then_inc(lo_ready, 1)

                def between(u):
                    if u == 0:
                        dve.wait_ge(half_used, i * (2 * FFU) + 2 * MOE)
                        take_rows()
                    if u == 3:
                        dve.wait_ge(spread_ps, i + 1)
                        add_rows()
                    if u == INU - 1:
                        dve.wait_ge(ggT_ps, i + 1)
                        choose(bass.ds(i + 1, 1))
                    if u == INU + 5:
                        modulate_extra(step, i + 2)
                        split_item(step)

                swiglu(i * (2 * FFU) + 2 * MOE, i * NJ + NJ, 1, unit, e_sil, e_hid, eh_hi, eh_lo, between)
                assert turn[0] == TURN
            dve.wait_ge(half_used, items * (2 * FFU) + 2 * MOE)
            take_rows()
            dve.wait_ge(spread_ps, items + 1)
            add_rows()
            dve.wait_ge(acc_out, items + 1)
            for t in range(NT):
                variance(t, acc[:, t, :], D, var_ready)
            dve.wait_ge(rows_landed, 128)
            for t in range(NT):
                link(standardise(t, acc[:, t, :], xs[:, t, :], dev_ready, 6 + t + 1))
                link(nc.vector.tensor_tensor(xs[:, t, :], xs[:, t, :], lng[:, :], ALU.mult))
                nc.vector.tensor_tensor(xs[:, t, :], xs[:, t, :], lnb[:, :], ALU.add).then_inc(x_ready, 1)


_INS = ["x", "c", "ada_w", "ada_b", "ln_g", "ln_b", "conv_w_in", "conv_dw", "conv_dw_b", "conv_ln_g", "conv_ln_b",
        "conv_w_out", "sgu_w_in", "sgu_b_in", "sgu_ln_g", "sgu_ln_b", "sgu_w_s", "sgu_b_s", "sgu_w_out",
        "ffn_w_in", "ffn_w_out", "moe_router", "moe_w_in", "moe_w_out"]


def kernel(**inputs):
    import numpy as _np
    import concourse.bacc as _bacc
    from concourse import mybir as _mybir
    from concourse.bass_utils import run_bass_kernel_spmd as _run

    nc = _bacc.Bacc("TRN2", target_bir_lowering=False, num_devices=1)
    arrays, args = {}, []
    for name in _INS:
        a = _np.ascontiguousarray(inputs[name])
        arrays[f"in_{name}"] = a
        args.append(nc.dram_tensor(f"in_{name}", a.shape, _mybir.dt.from_np(a.dtype), kind="ExternalInput").ap())
    shape = inputs["x"].shape
    out = nc.dram_tensor("out_x", shape, _mybir.dt.float32, kind="ExternalOutput").ap()
    hybrid_trunk(nc, *args, out)
    r = _run(nc, [arrays], core_ids=[0])
    return r.results[0]["out_x"]
```

```python
from contextlib import ExitStack

import concourse.bass as bass
from concourse import mybir

ALU = mybir.AluOpType
ACT = mybir.ActivationFunctionType
F32 = mybir.dt.float32
F32R = mybir.dt.float32r
I32 = mybir.dt.int32
U32 = mybir.dt.uint32

P = 128
BANK = 512
SLOTS = 7
UNIT = 2048
HALF = UNIT // 2


def hybrid_trunk(nc, x, c, ada_w, ada_b, ln_g, ln_b, conv_w_in, conv_dw, conv_dw_b, conv_ln_g,
                 conv_ln_b, conv_w_out, sgu_w_in, sgu_b_in, sgu_ln_g, sgu_ln_b, sgu_w_s, sgu_b_s,
                 sgu_w_out, ffn_w_in, ffn_w_out, moe_router, moe_w_in, moe_w_out, out):
    _, S, D = x.shape
    NT = S // P
    KC = D // P
    F = ffn_w_out.shape[1]
    NJ = F // BANK
    FC = F // P
    E = moe_router.shape[2]
    TAPS = conv_dw.shape[1]
    PADL = TAPS - 1
    HS = sgu_w_out.shape[1]
    HC = HS // P
    G = sgu_w_s.shape[1]
    GW = HS // G
    DEPTH = ada_w.shape[0]
    ALPHA = (2 * DEPTH) ** 0.25
    SEG = 6
    ADB = SEG * D // BANK
    XS = 32
    CAP = P + XS
    NCOL = E + 4
    INU = 4 * NJ
    OUTU = FC // 2
    FFU = INU + OUTU
    POOL_CH = (2, 3)
    PE_CH = 7
    assert S <= 2 * CAP and E * CAP >= S and 4 * (CAP + 1) > 2 * S
    assert NT == 2 and KC == 8 and FC % 4 == 0 and FFU % SLOTS == 0 and SEG * D // P == 48

    def in_unit(w, col, kh):
        return w.rearrange("(k p) n -> p k n", p=P)[:, 4 * kh:4 * kh + 4, col:col + BANK]

    def out_unit(w, m):
        return w.rearrange("(k p) n -> p k n", p=P)[:, 2 * m:2 * m + 2, :]

    units, ada_at, split_at = [], [], []

    def add_ada(layer, b):
        for kh in range(2):
            ada_at.append(len(units))
            units.append(("ada", len(ada_at) - 1, in_unit(ada_w[layer], b * BANK, kh)))

    def add_split(ap):
        split_at.append(len(units))
        units.append(("split", len(split_at) - 1, ap))

    for b in range(4):
        add_ada(0, b)
    for blk in range(2):
        for col in (D, 0):
            for kh in range(2):
                add_split(in_unit(conv_w_in[0], col + blk * BANK, kh))
    for b in range(4, ADB):
        add_ada(0, b)
    CONV_OUT = len(split_at)
    for m in range(KC // 2):
        add_split(out_unit(conv_w_out[0], m))
    FFN = len(split_at)
    for u in range(INU):
        j, part, kh = u // 4, (u % 4) // 2, u % 2
        add_split(in_unit(ffn_w_in[0], part * F + j * BANK, kh))
        if u % 2 and u // 2 < ADB:
            add_ada(1, u // 2)
    for m in range(OUTU):
        add_split(out_unit(ffn_w_out[0], m))
    SGU = len(split_at)
    for q in range(8):
        for kh in range(2):
            add_split(in_unit(sgu_w_in[0], (HS + q * BANK) if q < 4 else (q - 4) * BANK, kh))
    SGU_OUT = len(split_at)
    for m in range(HC // 2):
        add_split(out_unit(sgu_w_out[0], m))
    MOE = len(split_at)
    MOE_AT = len(units)
    assert MOE_AT % SLOTS == 0 and MOE % 2 == 0

    with ExitStack() as ctx:
        def sem(name):
            return ctx.enter_context(nc.semaphore(name))

        def sb(name, shape, dt=F32):
            return ctx.enter_context(nc.sbuf_tensor(name, shape, dt))

        ring = sb("ring", [P, SLOTS, UNIT])
        w_hi = sb("w_hi", [P, 4, HALF], F32R)
        w_lo = sb("w_lo", [P, 4, HALF], F32R)
        xs = sb("xs", [P, NT, D])
        g1row = sb("g1row", [P, D])
        g2row = sb("g2row", [P, 2, D])
        lng = sb("lng", [P, D])
        lnb = sb("lnb", [P, D])
        ident = sb("ident", [P, P])
        ones = sb("ones", [P, P])
        sel4 = sb("sel4", [P, P])
        tri = sb("tri", [P, P])
        iota = sb("iota", [P, CAP])
        vcols = sb("vcols", [P, P])
        modb = sb("modb", [P, 96])
        mods = sb("mods", [P, 2, SEG, KC])
        lncols = sb("lncols", [P, 2, 3, KC])
        ab = sb("ab", [P, 3, 2, KC])
        csil = sb("csil", [P, KC, 32])
        modrow = sb("modrow", [P, BANK])
        wsT = sb("wsT", [P, G, P])
        bsT = sb("bsT", [P, G])
        router = sb("router", [P, KC, E])
        stats = sb("stats", [P, NT, 4, 6])
        mv = sb("mv", [P, NT, 2])
        var = sb("var", [P, NT])
        dev = sb("dev", [P, NT])
        rstd = sb("rstd", [P, NT])
        ps = ctx.enter_context(nc.psum_tensor("ps", [P, 8, BANK], F32))

        ARENA = 80
        sb("arena", [P, ARENA * 256])
        base = nc.sbuf_base - ARENA * 1024

        def at(kib, name, shape, dt=F32):
            return nc.alloc_sbuf_tensor_at(name, shape, dt, offset=int(base + kib * 1024))

        hT_hi = at(0, "hT_hi", [P, KC, S], F32R)
        hT_lo = at(8, "hT_lo", [P, KC, S], F32R)
        ztmp_early = at(8, "ztmp_early", [P, NT, D])
        ztmp_late = at(24, "ztmp_late", [P, NT, D])
        h32 = at(16, "h32", [P, KC, S])
        ypad = at(24, "ypad", [P, KC, PADL + S])
        ycv = at(34, "ycv", [P, KC, S])
        ysq = at(42, "ysq", [P, KC, S])
        y_hi = at(50, "y_hi", [P, KC, S], F32R)
        y_lo = at(58, "y_lo", [P, KC, S], F32R)
        sig = at(66, "sig", [P, 4, S])
        dwT = at(70, "dwT", [P, KC, TAPS])
        diag = at(71, "diag", [P, 8, P])
        cst = at(75, "cst", [P, 4, S])
        prod = at(16, "prod", [P, 4, S])
        vecs = at(42, "vecs", [P, P])
        vecs2 = at(42.5, "vecs2", [48, P])
        iota_i = at(58, "iota_i", [P, CAP], I32)
        dwrow = at(43, "dwrow", [TAPS, D])
        bsrow = at(47, "bsrow", [G, P])
        wsr = at(50, "wsr", [P, G, P])
        wsm = at(54, "wsm", [P, G, P])
        f_sil = at(16, "f_sil", [P, NT, BANK])
        f_hid = at(20, "f_hid", [P, NT, BANK])
        hid_hi = at(24, "hid_hi", [P, FC, S], F32R)
        hid_lo = at(52, "hid_lo", [P, FC, S], F32R)
        vv = at(24, "vv", [P, NT, HS])
        uu = at(40, "uu", [P, NT, HS])
        s_lng = at(56, "s_lng", [P, HS])
        s_lnb = at(64, "s_lnb", [P, HS])
        brow = at(72, "brow", [P, 2, BANK])
        uT_hi = at(0, "uT_hi", [P, HC, S], F32R)
        uT_lo = at(56, "uT_lo", [P, HC, S], F32R)
        acc = at(0, "acc", [P, NT, D])
        oneh = at(22, "oneh", [P, NT, CAP])
        ggate = at(9, "ggate", [P, NT, P])
        ggT = at(10, "ggT", [P, 2 * NT, P])
        xe32 = at(24, "xe32", [P, KC, P])
        xe_hi = at(28, "xe_hi", [P, KC, P], F32R)
        xe_lo = at(32, "xe_lo", [P, KC, P], F32R)
        eh_hi = at(36, "eh_hi", [P, FC, P], F32R)
        eh_lo = at(50, "eh_lo", [P, FC, P], F32R)
        ye = at(64, "ye", [P, D])
        e_sil = at(68, "e_sil", [P, 1, BANK])
        e_hid = at(70, "e_hid", [P, 1, BANK])
        hidx_T = at(16, "hidx_T", [P, FC, XS])
        xx = at(20, "xx", [P, KC, XS])
        ggx = at(21, "ggx", [P, NT, P])
        yex = at(72, "yex", [P, D])
        silx = at(76, "silx", [P, P])
        hidx = at(76.5, "hidx", [P, P])
        small_at = [12 * 1024]

        def small(name, cols, dt=F32):
            t = nc.alloc_sbuf_tensor_at(name, [P, *cols], dt, offset=base + small_at[0])
            n = 4
            for d in cols:
                n *= d
            small_at[0] += (n + 31) // 32 * 32
            assert small_at[0] <= 16 * 1024
            return t

        lgt = small("lgt", [NT, E])
        top = small("top", [NT, 8])
        topi = small("topi", [NT, 8], U32)
        topf = small("topf", [NT, 8])
        tdif = small("tdif", [NT, 1])
        tgate = small("tgate", [NT, 2])
        mask1 = small("mask1", [NT, E])
        mask2 = small("mask2", [NT, E])
        mask = small("mask", [NT, E])
        gate1 = small("gate1", [NT, E])
        gate = small("gate", [NT, E])
        rank1 = small("rank1", [NT, E])
        excess = small("excess", [NT, E])
        over = small("over", [4, 2 * E])
        before = small("before", [E])
        oh = small("oh", [4, E])
        junk = small("junk", [15, E])
        dest = small("dest", [NT, NCOL])
        gcol = small("gcol", [NT, NCOL])
        XF = 8
        meta = small("meta", [XF + 1 + NCOL])
        metai = small("metai", [XF + 1 + NCOL], I32)

        landed = [sem(f"landed{i}") for i in range(SLOTS)]
        x_landed, vec_landed, misc_landed = sem("x_landed"), sem("vec_landed"), sem("misc_landed")
        rows_landed, gb_landed = sem("rows_landed"), sem("gb_landed")
        sln_landed = sem("sln_landed")
        brow_landed = [sem("brow_landed0"), sem("brow_landed1")]
        stored = sem("stored")
        lo_seen = sem("lo_seen")
        consts, pool_step, ws_masked = sem("consts"), sem("pool_step"), sem("ws_masked")
        hi_ready, lo_ready, half_used = sem("hi_ready"), sem("lo_ready"), sem("half_used")
        ada_used, ada_copied, ada_sums, ada_out = sem("ada_used"), sem("ada_copied"), sem("ada_sums"), sem("ada_out")
        vec_ps, vec_out, ws_ps, ws_out = sem("vec_ps"), sem("vec_out"), sem("ws_ps"), sem("ws_out")
        csil_ready, iota_ready = sem("csil_ready"), sem("iota_ready")
        pad_zero = sem("pad_zero")
        xT_ps, h32_out, h_ready = sem("xT_ps"), sem("h32_out"), sem("h_ready")
        h32_dve, xe32_dve = sem("h32_dve"), sem("xe32_dve")
        sig_out, glu_out, diag_ready, diag_used = sem("sig_out"), sem("glu_out"), sem("diag_ready"), sem("diag_used")
        taps_out, dconv_out = sem("taps_out"), sem("dconv_out")
        tap_product, tap_added = sem("tap_product"), sem("tap_added")
        mean_ps, centred, squared, var_ps, cvar, cdev, normed, cact, y_ready = (
            sem(n) for n in ("mean_ps", "centred", "squared", "var_ps", "cvar", "cdev", "normed", "cact", "y_ready"))
        var_ready, dev_ready, x_ready = sem("var_ready"), sem("dev_ready"), sem("x_ready")
        y_done, ab_ready, rows_used = sem("y_done"), sem("ab_ready"), sem("rows_used")
        silu_out, hid_out, hidT_ps, hidT_hi, hidT_lo = (
            sem(n) for n in ("silu_out", "hid_out", "hidT_ps", "hidT_hi", "hidT_lo"))
        zb_out, gelu_out, vvar, vdev, v_normed, v_scaled, v_ready, sv_ps, gated, uT_ps, uT_hi_out, \
            uT_lo_out = (
            sem(n) for n in ("zb_out", "gelu_out", "vvar", "vdev", "v_normed", "v_scaled", "v_ready", "sv_ps",
                             "gated", "uT_ps",
                             "uT_hi_out", "uT_lo_out"))
        logit_ps, mdif, mgate, mask_ready, rank_ps, meta_ready = (
            sem(n) for n in ("logit_ps", "mdif", "mgate", "mask_ready", "rank_ps", "meta_ready"))
        oneh_out, pick_ready, picked_ps, xe32_out, xe_hi_out, xe_ready = (
            sem(n) for n in ("oneh_out", "pick_ready", "picked_ps", "xe32_out", "xe_hi_out",
                             "xe_ready"))
        ggT_ps, ggT_out, ye_ready, spread_ps, acc_out = (
            sem(n) for n in ("ggT_ps", "ggT_out", "ye_ready", "spread_ps", "acc_out"))
        dve_step, dve_turn = sem("dve_step"), sem("dve_turn")

        SB = (6, 4)
        XB = (4, 2)
        PB = (0, 1, 2)
        YB = (6, 0)

        def tok(t):
            return slice(t * P, (t + 1) * P)

        def wait_landed(eng, pos):
            eng.wait_ge(landed[pos % SLOTS], 16 * (pos // SLOTS + 1))

        block = ctx.enter_context(nc.Block())

        @block.sync
        def _(sp):
            def load_vectors():
                for r0, n, vec in ((0, 48, ada_b[0]), (48, 48, ada_b[1]), (96, 8, c[0]), (104, 8, conv_dw_b[0]),
                                   (112, 8, conv_ln_g[0]), (120, 8, conv_ln_b[0])):
                    sp.dma_start(vecs[r0:r0 + n, :], vec.rearrange("(j p) -> j p", p=P)).then_inc(vec_landed, 16)
                sp.dma_start(vecs2[0:24, :], ln_g.rearrange("l n (j p) -> (l n j) p", p=P)[0:24, :]).then_inc(vec_landed, 16)
                sp.dma_start(vecs2[24:48, :], ln_b.rearrange("l n (j p) -> (l n j) p", p=P)[0:24, :]).then_inc(vec_landed, 16)

            for pos, (kind, n, src) in enumerate(units):
                if pos >= SLOTS:
                    k0, n0, _ = units[pos - SLOTS]
                    if k0 == "ada":
                        sp.wait_ge(ada_used, n0 + 1)
                    else:
                        sp.wait_ge(lo_ready, 2 * n0 + 2)
                dst = ring[:, pos % SLOTS, :].rearrange("p (k n) -> p k n", k=src.shape[1])
                sp.dma_start(dst, src).then_inc(landed[pos % SLOTS], 16)
                if pos == 0:
                    load_vectors()
                if pos == 1:
                    sp.dma_start(xs[:, :, :], x[0].rearrange("(t p) d -> p t d", p=P)).then_inc(x_landed, 16)

            w_in = moe_w_in[0].rearrange("e (k p) n -> e p k n", p=P)
            w_out = moe_w_out[0].rearrange("e (k p) n -> e p k n", p=P)

            def expert(e, i, wholly):
                for u in range(FFU):
                    h = 2 * (MOE + u - SLOTS) + 2
                    if wholly is None:
                        sp.wait_ge(half_used, i * (2 * FFU) + h)
                    else:
                        sp.wait_ge(lo_ready, i * (2 * FFU) + h)
                        sp.sem_inc(lo_seen, 1)
                        sp.wait_ge(half_used, (i * (2 * FFU) + wholly[u >= SLOTS]) + (h - 4))
                    if u < INU:
                        j, part, kh = u // 4, (u % 4) // 2, u % 2
                        src = w_in[bass.ds(e, 1), :, 4 * kh:4 * kh + 4, part * F + j * BANK:part * F + (j + 1) * BANK]
                    else:
                        src = w_out[bass.ds(e, 1), :, 2 * (u - INU):2 * (u - INU) + 2, :]
                    k = src.shape[2]
                    src = src.rearrange("e p k n -> (e p) k n")
                    dst = ring[:, u % SLOTS, :].rearrange("p (k n) -> p k n", k=k)
                    sp.dma_start(dst, src).then_inc(landed[u % SLOTS], 16)

            def freed(i):
                return [sp.value_load(metai[0:1, bass.ds(i + (XF + v), 1)], min_val=0, max_val=1) * 4
                        for v in range(2)]

            expert(0, 0, None)
            sp.wait_ge(meta_ready, 1)
            with sp.Fori(1, E) as i:
                expert(i, i, freed(i))
            items = sp.value_load(metai[0:1, 4:5], min_val=E, max_val=NCOL - 1)
            with sp.If(items > E):
                with sp.Fori(E, items) as i:
                    e = sp.value_load(metai[0:1, bass.ds(i - E, 1)], min_val=0, max_val=E - 1)
                    expert(e, i, freed(i))
                sp.nop()
            for t in range(NT):
                sp.wait_ge(x_ready, 2 * 3 + t + 1)
                sp.dma_start(out[0, tok(t), :], xs[:, t, :]).then_inc(stored, 16)
            sp.wait_ge(stored, 16 * NT)

        @block.gpsimd
        def _(pool):
            pool.memset(ident[:, :], 0.0).then_inc(pool_step, 1)
            pool.memset(ones[:, :], 1.0).then_inc(pool_step, 1)
            pool.memset(tri[:, :], 0.0).then_inc(pool_step, 1)
            pool.memset(sel4[:, :], 0.0).then_inc(pool_step, 1)
            pool.iota(iota_i[:, :], pattern=[[1, CAP]], base=0, channel_multiplier=0).then_inc(pool_step, 1)
            pool.wait_ge(pool_step, 5)
            pool.affine_select(out=ident[:, :], in_=ident[:, :], compare_op=ALU.not_equal, fill=1.0, base=0,
                               pattern=[[-1, P]], channel_multiplier=1).then_inc(consts, 1)
            pool.affine_select(out=tri[:, :], in_=tri[:, :], compare_op=ALU.is_ge, fill=1.0, base=0,
                               pattern=[[-1, P]], channel_multiplier=1).then_inc(consts, 1)
            pool.wait_ge(misc_landed, 64)
            pool.affine_select(out=wsm[:, :, :], in_=wsr[:, :, :], compare_op=ALU.is_ge, fill=0.0, base=0,
                               pattern=[[0, G], [-1, P]], channel_multiplier=1).then_inc(ws_masked, 1)
            pool.wait_ge(vec_out, 2)

            def diagonal(n):
                if n >= 8:
                    pool.wait_ge(diag_used, n - 7)
                pool.tensor_tensor(diag[:, n % 8, :], ident[:, :], dwT[:, PE_CH, n:n + 1].broadcast_to([P, P]),
                                   ALU.mult).then_inc(diag_ready, 1)

            for n in range(8):
                diagonal(n)
            pool.wait_ge(half_used, 4)
            for row, seg, layer in ((g1row[:, :], 2, 0), (g2row[:, 0, :], 5, 0), (g2row[:, 1, :], 5, 1)):
                pool.dma_start(row, ada_b[layer, seg * D:(seg + 1) * D].partition_broadcast(P)).then_inc(gb_landed, 16)
            pool.dma_start(lng[:, :], ln_g[0, 0].partition_broadcast(P)).then_inc(rows_landed, 16)
            pool.dma_start(lnb[:, :], ln_b[0, 0].partition_broadcast(P)).then_inc(rows_landed, 16)
            for n in range(2 * (TAPS - 1)):
                ch = POOL_CH[n % 2]
                pool.wait_ge(tap_product, n + 3)
                if n >= 2:
                    pool.wait_ge(tap_added, n - 1)
                pool.tensor_tensor(ycv[:, ch, :], ycv[:, ch, :], prod[:, n % 4, :], ALU.add).then_inc(tap_added, 1)
                if n % 2 and 8 + n // 2 < TAPS:
                    diagonal(8 + n // 2)

            def split_unit(n):
                for h in (2 * n, 2 * n + 1):
                    pool.wait_ge(hi_ready, h + 1)
                    pool.wait_ge(half_used, h - 3)
                    pool.wait_ge(lo_ready, h)
                    pool.tensor_tensor(w_lo[:, h % 4, :], ring[:, split_at[n] % SLOTS, (h % 2) * HALF:(h % 2 + 1) * HALF],
                                       w_hi[:, h % 4, :].bitcast(F32), ALU.subtract).then_inc(lo_ready, 1)

            def affine(q, dst):
                pool.wait_ge(rows_landed, 32 * (q + 1))
                pool.wait_ge(xT_ps, 2 * (q + 1) + 2)
                for t in range(NT):
                    pool.tensor_tensor(dst[:, t, :], xs[:, t, :], lng[:, :], ALU.mult).then_inc(pool_step, 1)
                pool.wait_ge(pool_step, 5 + NT * (q + 1))
                for t in range(NT):
                    pool.tensor_tensor(dst[:, t, :], dst[:, t, :], lnb[:, :], ALU.add).then_inc(rows_used, 1)

            def norm_rows(q):
                pool.wait_ge(rows_used, NT * q)
                pool.dma_start(lng[:, :], ln_g[q // 2, q % 2].partition_broadcast(P)).then_inc(rows_landed, 16)
                pool.dma_start(lnb[:, :], ln_b[q // 2, q % 2].partition_broadcast(P)).then_inc(rows_landed, 16)

            split_unit(FFN)
            affine(0, xs)
            norm_rows(1)
            pool.dma_start(g1row[:, :], ada_b[1, 2 * D:3 * D].partition_broadcast(P)).then_inc(gb_landed, 16)
            split_unit(SGU)
            pool.wait_ge(x_ready, 4)
            pool.dma_start(s_lng[:, :], sgu_ln_g[0].partition_broadcast(P)).then_inc(sln_landed, 16)
            pool.dma_start(s_lnb[:, :], sgu_ln_b[0].partition_broadcast(P)).then_inc(sln_landed, 16)
            for q in range(8):
                if q >= 2:
                    pool.wait_ge(zb_out, q - 1)
                col = HS + q * BANK if q < 4 else (q - 4) * BANK
                pool.dma_start(brow[:, q % 2, :], sgu_b_in[0, col:col + BANK].partition_broadcast(P))\
                    .then_inc(brow_landed[q % 2], 16)
                if q == 1:
                    affine(1, xs)
                    norm_rows(2)
                if q in (5, 6):
                    t = q - 5
                    pool.wait_ge(v_normed, t + 1)
                    pool.wait_ge(sln_landed, 32)
                    pool.tensor_tensor(vv[:, t, :], vv[:, t, :], s_lng[:, :], ALU.mult).then_inc(v_scaled, 1)
                    pool.wait_ge(v_scaled, t + 1)
                    pool.tensor_tensor(vv[:, t, :], vv[:, t, :], s_lnb[:, :], ALU.add).then_inc(v_ready, 1)
            affine(2, acc)
            norm_rows(3)

            def gate_slots(item, n):
                pool.wait_ge(oneh_out, n)
                pool.tensor_tensor(ggate[:, :, :], oneh[:, :, 0:P], gcol[:, :, item].broadcast_to([P, NT, P]), ALU.mult)
                for t in range(NT):
                    op = pool.tensor_tensor(ggx[:, t, :].rearrange("p (g n) -> p g n", g=4),
                                            oneh[:, t:t + 1, P:CAP].broadcast_to([P, 4, XS]),
                                            gcol[:, t:t + 1, item].broadcast_to([P, 4, XS]), ALU.mult)
                op.then_inc(pick_ready, 1)

            gate_slots(slice(0, 1), 1)
            pool.wait_ge(meta_ready, 1)
            items = pool.value_load(metai[0:1, 4:5], min_val=E, max_val=NCOL - 1)
            with pool.Fori(0, items) as i:
                gate_slots(bass.ds(i + 1, 1), i + 2)
                pool.wait_ge(xe_hi_out, i + 1)
                pool.tensor_tensor(xe_lo[:, :, :], xe32[:, :, :], xe_hi[:, :, :].bitcast(F32), ALU.subtract)\
                    .then_inc(xe_ready, 1)

        @block.tensor
        def _(pe):
            def three(o, a_hi, a_lo, b_hi, b_lo, start, stop):
                nc.tensor.matmul(o, a_hi, b_hi, start=start, stop=False)
                nc.tensor.matmul(o, a_hi, b_lo, start=False, stop=False)
                return nc.tensor.matmul(o, a_lo, b_hi, start=False, stop=stop)

            def ada_rows(n, bank):
                if n:
                    pe.wait_ge(ada_copied, n)
                for kh in range(2):
                    pos = ada_at[2 * n + kh]
                    wait_landed(pe, pos)
                    for g in range(4):
                        mm = nc.tensor.matmul(ps[32 * g:32 * g + 32, bank, :], csil[:, 4 * kh + g, :],
                                              ring[:, pos % SLOTS, g * BANK:(g + 1) * BANK],
                                              start=(kh == 0), stop=(kh == 1), skip_group_check=True)
                    mm.then_inc(ada_used, 1)

            def ada_finish(n, bank):
                b = n % ADB
                pe.wait_ge(ada_copied, n + 1)
                if b // 2 in (2, 5):
                    mm = nc.tensor.matmul(ps[:, bank, :], sel4[:, :], modrow[:, :], start=True, stop=True)
                else:
                    for j in range(4):
                        mm = nc.tensor.matmul(ps[:, bank, 4 * b + j:4 * b + j + 1], modrow[:, tok(j)],
                                              sel4[:, 0:1], start=True, stop=True)
                mm.then_inc(ada_sums, 1)

            def turn_x(q, t):
                if q:
                    pe.wait_ge(x_ready, 2 * (q - 1) + t + 1)
                for k in range(KC):
                    mm = nc.tensor.transpose(ps[:, XB[t] + k // 4, (k % 4) * P:(k % 4 + 1) * P],
                                             xs[:, t, tok(k)], ident[:, :])
                mm.then_inc(xT_ps, 1)

            def out_unit_rows(h, hb, a_hi, a_lo, kc, nt, first, last, extra=None):
                pe.wait_ge(lo_ready, h + 1)
                for t in range(nt):
                    for dh in range(2):
                        mm = three(ps[:, YB[t] + dh, :], a_hi[:, kc, tok(t)], a_lo[:, kc, tok(t)],
                                   w_hi[:, hb, dh * BANK:(dh + 1) * BANK], w_lo[:, hb, dh * BANK:(dh + 1) * BANK],
                                   first, last)
                if extra is not None:
                    mm = extra_out(extra, hb % 2, kc)
                mm.then_inc(half_used, 1)

            def in_half_rows(hb, a_hi, a_lo, k0, t, bank):
                for kk in range(2):
                    k = k0 + kk
                    mm = three(ps[:, bank + t, :], a_hi[:, k, tok(t)], a_lo[:, k, tok(t)],
                               w_hi[:, hb, kk * BANK:(kk + 1) * BANK], w_lo[:, hb, kk * BANK:(kk + 1) * BANK],
                               k == 0, k == KC - 1)
                return mm

            def in_unit_rows(h, hb, a_hi, a_lo, k0, nt, bank, extra=None):
                pe.wait_ge(lo_ready, h + 1)
                for t in range(nt):
                    mm = in_half_rows(hb, a_hi, a_lo, k0, t, bank)
                if extra is not None:
                    mm = extra_in(extra, hb % 2, k0, bank + 1)
                mm.then_inc(half_used, 1)

            def first_block(h0, q):
                for t in range(NT):
                    pe.wait_ge(h_ready, 2 * q + t + 1)
                    for s in range(4):
                        if t == 0:
                            pe.wait_ge(lo_ready, h0 + s + 1)
                        if t == 0 and s == 1:
                            turn_x(q, 1)
                        mm = in_half_rows((h0 + s) % 4, hT_hi, hT_lo, 2 * s, t, 0)
                        if t:
                            mm.then_inc(half_used, 1)

            def last_rows(h0, a_hi, a_lo, n):
                for t in range(NT):
                    for s in range(4):
                        kc = n - 4 + s
                        if t == 0:
                            pe.wait_ge(lo_ready, h0 + s + 1)
                        for dh in range(2):
                            mm = three(ps[:, YB[t] + dh, :], a_hi[:, kc, tok(t)], a_lo[:, kc, tok(t)],
                                       w_hi[:, (h0 + s) % 4, dh * BANK:(dh + 1) * BANK],
                                       w_lo[:, (h0 + s) % 4, dh * BANK:(dh + 1) * BANK], False, kc == n - 1)
                        if s == 3 and t == 0:
                            mm.then_inc(y_done, 1)
                        if t:
                            mm.then_inc(half_used, 1)

            def extra_in(slot, s, k0, bank):
                for kk in range(2):
                    for g in range(4):
                        w0 = s * HALF + kk * BANK + g * P
                        mm = nc.tensor.matmul(ps[32 * g:32 * g + 32, bank, 0:P], xx[:, k0 + kk, :],
                                              ring[:, slot, w0:w0 + P], start=(k0 + kk == 0),
                                              stop=(k0 + kk == KC - 1), skip_group_check=True)
                return mm

            def extra_out(slot, s, kc):
                for g in range(4):
                    w0 = s * HALF + g * (D // 4)
                    mm = nc.tensor.matmul(ps[32 * g:32 * g + 32, 3, 0:D // 4], hidx_T[:, kc, :],
                                          ring[:, slot, w0:w0 + D // 4], start=(kc == 0), stop=(kc == FC - 1),
                                          skip_group_check=True)
                return mm

            def swiglu(h0, c0, nt, a_hi, a_lo, hid, e_hi, e_lo, after, extra=False):
                for u in range(FFU):
                    j, b_part, kh = u // 4, (u % 4) // 2, u % 2
                    if nt == NT and u < 2:
                        if u == 0:
                            first_block(h0, 1)
                    elif nt == NT and u >= FFU - 2:
                        if u == FFU - 2:
                            last_rows(h0 + (2 * FFU - 4), e_hi, e_lo, FC)
                    elif u < INU:
                        if kh == 0:
                            pe.wait_ge(hid_out if b_part else silu_out, c0 + j)
                        for s in range(2):
                            in_unit_rows(h0 + (2 * u + s), (2 * u + s) % 4, a_hi, a_lo, 4 * kh + 2 * s, nt,
                                         2 * b_part, u % SLOTS if extra else None)
                    else:
                        for s in range(2):
                            kc = 2 * (u - INU) + s
                            if kc % 4 == 0:
                                pe.wait_ge(hidT_lo, c0 + (kc // 4 + 1))
                            if u == INU and s == 0:
                                pe.wait_ge(silu_out, c0 + NJ)
                            if u == INU and s == 0 and extra:
                                pe.wait_ge(hid_out, c0 + NJ)
                            out_unit_rows(h0 + (2 * u + s), (2 * u + s) % 4, e_hi, e_lo, kc, nt,
                                          kc == 0, kc == FC - 1, u % SLOTS if extra else None)
                    if u % 4 == 1 and 5 <= u <= INU + 1:
                        j = (u - 5) // 4
                        pe.wait_ge(hid_out, c0 + (j + 1))
                        pe.wait_ge(hidT_lo, c0 + j)
                        for t in range(nt):
                            for f in range(4):
                                mm = nc.tensor.transpose(ps[:, 4 + t, f * P:(f + 1) * P], hid[:, t, tok(f)],
                                                         ident[:, :])
                        if nt == 1:
                            mm = nc.tensor.transpose(ps[:, 5, 0:P], hidx[:, :], ident[:, :])
                        mm.then_inc(hidT_ps, 1)
                    after(u)

            pe.wait_ge(consts, 6)
            pe.wait_ge(vec_landed, 16 * 8)
            nc.tensor.transpose(ps[:, 6, 0:P], vecs[:, :], ident[:, :])
            nc.tensor.transpose(ps[:, 6, P:P + 48], vecs2[:, :], ident[0:48, 0:48]).then_inc(vec_ps, 1)
            pe.wait_ge(misc_landed, 64)
            for k in range(KC):
                nc.tensor.transpose(ps[:, 5, TAPS * k:TAPS * (k + 1)], dwrow[:, tok(k)], ident[0:TAPS, 0:TAPS])
            nc.tensor.transpose(ps[:, 5, 256:256 + G], bsrow[:, :], ident[0:G, 0:G]).then_inc(vec_ps, 1)
            pe.wait_ge(csil_ready, 1)
            pe.wait_ge(vec_out, 3)
            ada_rows(0, 6)
            pe.wait_ge(x_landed, 16)
            for t in range(NT):
                turn_x(0, t)
            for n in range(4):
                if n:
                    pe.wait_ge(ada_out, n)
                ada_finish(n, 7)
                if n < 3:
                    ada_rows(n + 1, 6)
                if n == 0:
                    pe.wait_ge(ws_masked, 1)
                    for g in range(G):
                        mm = nc.tensor.transpose(ps[:, g // 4, (g % 4) * P:(g % 4 + 1) * P], wsm[:, g, :], ident[:, :])
                    mm.then_inc(ws_ps, 1)

            pe.wait_ge(h_ready, 2)
            pe.wait_ge(ws_out, 1)
            pe.wait_ge(ada_out, 4)
            for i in range(8):
                blk, part, kh = i // 4, (i % 4) // 2, i % 2
                if blk and kh == 0:
                    pe.wait_ge(glu_out if part else sig_out, 1)
                for s in range(2):
                    h = 2 * i + s
                    pe.wait_ge(lo_ready, h + 1)
                    for ch in range(4):
                        for kk in range(2):
                            k = 4 * kh + 2 * s + kk
                            w = slice(kk * BANK + ch * P, kk * BANK + (ch + 1) * P)
                            mm = three(ps[:, 4 * part + ch, 0:S], w_hi[:, h % 4, w], w_lo[:, h % 4, w],
                                       hT_hi[:, k, :], hT_lo[:, k, :], k == 0, k == KC - 1)
                    mm.then_inc(half_used, 1)
            pe.wait_ge(glu_out, 2)
            for n in range(4, ADB):
                ada_rows(n, 0)
                for k in range(TAPS * (n - 4) // 8, TAPS * (n - 3) // 8):
                    pe.wait_ge(diag_ready, k + 1)
                    nc.tensor.matmul(ps[:, PE_CH, 0:S], diag[:, k % 8, :], ypad[:, PE_CH, k:k + S],
                                     start=(k == 0), stop=(k == TAPS - 1)).then_inc(diag_used, 1)
                pe.wait_ge(ada_out, n - 2)
                ada_finish(n, 1 + n % 3)
            for n, ch in enumerate((0, 1, PE_CH, *POOL_CH, 4, 5, 6)):
                if n in (0, 5):
                    pe.wait_ge(taps_out, 2 if n == 0 else 5)
                if n == 2:
                    pe.wait_ge(dconv_out, 1)
                if n == 3:
                    pe.wait_ge(tap_added, 2 * (TAPS - 1))
                mm = nc.tensor.matmul(ps[:, 4, 0:S], ones[:, :], ycv[:, ch, :], start=(n == 0), stop=(n == KC - 1))
            mm.then_inc(mean_ps, 1)
            for ch in range(KC):
                if ch % 4 == 0:
                    pe.wait_ge(squared, ch // 4 + 1)
                mm = nc.tensor.matmul(ps[:, 5, 0:S], ones[:, :], ysq[:, ch, :], start=(ch == 0), stop=(ch == KC - 1))
            mm.then_inc(var_ps, 1)
            pe.wait_ge(ada_out, ADB)
            pe.wait_ge(y_ready, 1)
            for kc in range(KC - 4):
                h = 2 * CONV_OUT + kc
                out_unit_rows(h, h % 4, y_hi, y_lo, kc, NT, kc == 0, False)
            pe.wait_ge(y_ready, 2)
            last_rows(2 * FFN - 4, y_hi, y_lo, KC)

            turn_x(1, 0)

            def ada_between(u):
                if u < INU and u % 2 and u // 2 < ADB:
                    ada_rows(ADB + u // 2, 6)
                if u < INU and u % 2 == 0 and 1 <= u // 2 <= ADB:
                    n = ADB + u // 2 - 1
                    pe.wait_ge(ada_out, n)
                    ada_finish(n, 7)
                if u == INU - 1:
                    pe.wait_ge(ada_out, 2 * ADB)

            swiglu(2 * FFN, 0, NT, hT_hi, hT_lo, f_hid, hid_hi, hid_lo, ada_between)

            turn_x(2, 0)
            first_block(2 * SGU, 2)
            for i in range(2, 16):
                q, kh = i // 2, i % 2
                if kh == 0 and q >= 2:
                    pe.wait_ge(zb_out, q - 1)
                for s in range(2):
                    h = 2 * (SGU + i) + s
                    in_unit_rows(h, h % 4, hT_hi, hT_lo, 4 * kh + 2 * s, NT, 2 * (q % 2))
            for t in range(NT):
                pe.wait_ge(v_ready, t + 1)
                if t:
                    pe.wait_ge(zb_out, 8)
                for g in range(G):
                    mm = nc.tensor.matmul(ps[:, (0 if t else 4) + g // 2, (g % 2) * GW:(g % 2 + 1) * GW],
                                          wsT[:, g, :], vv[:, t, g * GW:(g + 1) * GW], start=True, stop=True)
                mm.then_inc(sv_ps, 1)
            for r in range(2 * NT * 2):
                t, m = r % 2, r // 2
                pe.wait_ge(gated, NT if r else NT)
                if r >= 4:
                    pe.wait_ge(uT_lo_out, r - 3)
                for f in range(4):
                    mm = nc.tensor.transpose(ps[:, XB[t] + m % 2, f * P:(f + 1) * P],
                                             uu[:, t, tok(4 * m + f)], ident[:, :])
                mm.then_inc(uT_ps, 1)
            for m in range(HC // 2 - 2):
                for s in range(2):
                    kc = 2 * m + s
                    if kc % 4 == 0:
                        pe.wait_ge(uT_lo_out, 2 * (kc // 4 + 1))
                    h = 2 * (SGU_OUT + m) + s
                    out_unit_rows(h, h % 4, uT_hi, uT_lo, kc, NT, kc == 0, False)
            last_rows(2 * MOE - 4, uT_hi, uT_lo, HC)

            for t in range(NT):
                turn_x(3, t)
            for t in range(NT):
                pe.wait_ge(h32_out, 6 + t + 1)
                if t:
                    pe.wait_ge(h32_dve, NT + 1)
                for k in range(KC):
                    mm = nc.tensor.matmul(ps[:, 6, t * E:(t + 1) * E], h32[:, k, tok(t)], router[:, k, :],
                                          start=(k == 0), stop=(k == KC - 1))
                mm.then_inc(logit_ps, 1)
            pe.wait_ge(mask_ready, 1)
            nc.tensor.matmul(ps[:, 7, 0:E], tri[:, :], mask[:, 0, :], start=True, stop=True)
            nc.tensor.matmul(ps[:, 7, E:2 * E], ones[:, :], mask[:, 0, :], start=True, stop=False)
            nc.tensor.matmul(ps[:, 7, E:2 * E], tri[:, :], mask[:, 1, :], start=False, stop=True)
            nc.tensor.matmul(ps[:, 7, 2 * E:3 * E], ones[:, :], mask[:, 0, :], start=True, stop=False)
            nc.tensor.matmul(ps[:, 7, 2 * E:3 * E], ones[:, :], mask[:, 1, :], start=False, stop=True)\
                .then_inc(rank_ps, 1)

            def pick():
                for k in range(KC):
                    for t in range(NT):
                        mm = nc.tensor.matmul(ps[:, PB[k // 3], (k % 3) * CAP:(k % 3 + 1) * CAP],
                                              xs[:, t, tok(k)], oneh[:, t, :], start=(t == 0), stop=(t == NT - 1))
                mm.then_inc(picked_ps, 1)

            def spread(extra):
                for t in range(NT):
                    for dh in range(2):
                        cols = slice(dh * BANK, (dh + 1) * BANK)
                        mm = nc.tensor.matmul(ps[:, SB[t] + dh, :], ggT[:, t, :], ye[:, cols], start=True,
                                              stop=not extra)
                        if extra:
                            mm = nc.tensor.matmul(ps[:, SB[t] + dh, :], ggT[:, NT + t, :], yex[:, cols],
                                                  start=False, stop=True)
                    mm.then_inc(spread_ps, 1)

            def spread_last(flag):
                with pe.If(flag > 0):
                    spread(True)
                with pe.Else():
                    spread(False)
                pe.nop()

            pe.wait_ge(pick_ready, 1)
            pick()
            pe.wait_ge(meta_ready, 1)
            items = pe.value_load(metai[0:1, 4:5], min_val=E, max_val=NCOL - 1)
            with pe.Fori(0, items) as i:
                was_extra = pe.value_load(metai[0:1, bass.ds(i + XF, 1)], min_val=0, max_val=1)
                is_extra = pe.value_load(metai[0:1, bass.ds(i + (XF + 1), 1)], min_val=0, max_val=1)

                def between(u):
                    if u == 2:
                        pe.wait_ge(ye_ready, i + 1)
                        spread_last(was_extra)
                    if u == 4:
                        pe.wait_ge(acc_out, i * NT + NT)
                        for t in range(NT):
                            nc.tensor.transpose(ps[:, 6, tok(t)], ggate[:, t, :], ident[:, :])
                        for t in range(NT):
                            mm = nc.tensor.transpose(ps[:, 6, tok(NT + t)], ggx[:, t, :], ident[:, :])
                        mm.then_inc(ggT_ps, 1)
                    if u == INU + 3:
                        pe.wait_ge(pick_ready, i + 2)
                        pick()
                    if u == INU - 1:
                        pe.wait_ge(ggT_out, i + 1)

                def between_extra(u):
                    if u == 1:
                        pe.wait_ge(ye_ready, i + 1)
                    between(u)

                pe.wait_ge(xe_ready, i * 2 + 2)
                h0, c0 = i * (2 * FFU) + 2 * MOE, i * NJ + NJ
                with pe.If(is_extra > 0):
                    swiglu(h0, c0, 1, xe_hi, xe_lo, e_hid, eh_hi, eh_lo, between_extra, True)
                with pe.Else():
                    swiglu(h0, c0, 1, xe_hi, xe_lo, e_hid, eh_hi, eh_lo, between)
                pe.nop()
            pe.wait_ge(ye_ready, items + 1)
            spread_last(pe.value_load(metai[0:1, bass.ds(items + XF, 1)], min_val=0, max_val=1))

        @block.scalar
        def _(act):
            def split(pos_slot, landed_count, h, hb, first):
                if first:
                    act.wait_ge(landed[pos_slot], landed_count)
                return nc.scalar.activation(w_hi[:, hb, :], ring[:, pos_slot, (hb % 2) * HALF:(hb % 2 + 1) * HALF],
                                            ACT.Copy).then_inc(hi_ready, 1)

            def split_unit(n):
                pos = split_at[n]
                for s in range(2):
                    h = 2 * n + s
                    if h >= 4:
                        act.wait_ge(half_used, h - 3)
                    split(pos % SLOTS, 16 * (pos // SLOTS + 1), h, h % 4, s == 0)

            def ada_copy(n, bank):
                act.wait_ge(ada_used, 2 * n + 2)
                if n:
                    act.wait_ge(ada_sums, n)
                nc.scalar.activation(modrow[:, :], ps[:, bank, :], ACT.Copy).then_inc(ada_copied, 1)

            def modulate(q, gain, shift, tiles=(0, 1), chunks=KC):
                for t in tiles:
                    act.wait_ge(xT_ps, 2 * q + t + 1)
                    if t == 0 and q == 0:
                        act.wait_ge(ada_out, 4)
                    elif t == 0:
                        act.wait_ge(ab_ready, q)
                    for k in range(chunks):
                        op = nc.scalar.activation(h32[:, k, tok(t)], ps[:, XB[t] + k // 4, (k % 4) * P:(k % 4 + 1) * P],
                                                  ACT.Identity, bias=shift[:, k:k + 1], scale=gain[:, k:k + 1])
                    op.then_inc(h32_out, 1)

            def deviation(q, t):
                act.wait_ge(var_ready, 2 * q + t + 1)
                nc.scalar.activation(dev[:, t:t + 1], var[:, t:t + 1], ACT.Sqrt).then_inc(dev_ready, 1)

            def next_stage(q, n):
                split_unit(n)
                deviation(q, 0)
                split_unit(n + 1)
                modulate(q + 1, ab[:, q, 0, :], ab[:, q, 1, :], (0,))
                deviation(q, 1)
                modulate(q + 1, ab[:, q, 0, :], ab[:, q, 1, :], (1,))

            def swiglu(h0, c0, nt, unit, sil, e_hi, after):
                for u in range(FFU):
                    unit(u)
                    if u % 4 == 3 and u < INU:
                        j = (u - 3) // 4
                        act.wait_ge(half_used, h0 + 2 * (4 * j + 2))
                        act.wait_ge(hid_out, c0 + j)
                        op = nc.scalar.activation(sil[:, 0:nt, :], ps[:, 0:nt, :], ACT.Silu)
                        if nt == 1:
                            op = nc.scalar.activation(silx[:, :], ps[:, 1, 0:P], ACT.Silu)
                        op.then_inc(silu_out, 1)
                    if u % 4 == 3 and 7 <= u <= INU + 3:
                        j = (u - 7) // 4
                        act.wait_ge(hidT_ps, c0 + (j + 1))
                        if nt == 1:
                            nc.scalar.activation(hidx_T[:, 4 * j:4 * j + 4, :],
                                                 ps[:, 5, 0:P].rearrange("p (k n) -> p k n", k=4), ACT.Copy)
                        for t in range(nt):
                            op = nc.scalar.activation(e_hi[:, 4 * j:4 * j + 4, tok(t)],
                                                      ps[:, 4 + t, :].rearrange("p (k n) -> p k n", k=4), ACT.Copy)
                        op.then_inc(hidT_hi, 1)
                    after(u)

            act.dma_start(dwrow[:, :], conv_dw[0]).then_inc(misc_landed, 16)
            act.dma_start(bsrow[:, :], sgu_b_s[0]).then_inc(misc_landed, 16)
            act.dma_start(wsr[:, :, :], sgu_w_s[0].rearrange("g t s -> t g s")).then_inc(misc_landed, 16)
            act.dma_start(router[:, :, :], moe_router[0].rearrange("(k p) e -> p k e", p=P)).then_inc(misc_landed, 16)
            act.wait_ge(vec_out, 1)
            nc.scalar.activation(csil[:, :, :], vcols[:, 96:104].unsqueeze(2).broadcast_to([P, KC, 32]), ACT.Silu)\
                .then_inc(csil_ready, 1)
            for n in range(4):
                ada_copy(n, 6)
                if n == 1:
                    act.wait_ge(ws_ps, 1)
                    nc.scalar.activation(wsT[:, :, :], ps[:, 0:2, :].rearrange("p b (g n) -> p (b g) n", g=4), ACT.Copy)\
                        .then_inc(ws_out, 1)
            modulate(0, mods[:, 0, 1, :], mods[:, 0, 0, :], chunks=KC // 2)
            split_unit(0)
            split_unit(1)

            tap = [0]

            def tap_products(last):
                for k in range(tap[0], last):
                    for m, ch in enumerate(POOL_CH):
                        n = 2 * k + m - 2
                        if k == 0:
                            act.wait_ge(glu_out, 1)
                            act.wait_ge(pad_zero, 1)
                        elif n >= 4:
                            act.wait_ge(tap_added, n - 3)
                        dst = prod[:, n % 4, :] if k else ycv[:, ch, :]
                        bias = 0.0 if k else vcols[:, 104 + ch:105 + ch]
                        nc.scalar.activation(dst, ypad[:, ch, k:k + S], ACT.Identity, bias=bias,
                                             scale=dwT[:, ch, k:k + 1]).then_inc(tap_product, 1)
                tap[0] = max(tap[0], last)

            for i in range(2, 8):
                split_unit(i)
                if i % 4 == 3:
                    blk = i // 4
                    act.wait_ge(half_used, 8 * blk + 4)
                    if blk:
                        act.wait_ge(glu_out, 1)
                    nc.scalar.activation(sig[:, :, :], ps[:, 0:4, 0:S], ACT.Sigmoid).then_inc(sig_out, 1)
            for n in range(4, ADB + 1):
                if n < ADB:
                    ada_copy(n, 0)
                    tap_products(TAPS * (n - 3) // 8)
            act.wait_ge(diag_used, TAPS)
            nc.scalar.activation(ycv[:, PE_CH, :], ps[:, PE_CH, 0:S], ACT.Identity, bias=vcols[:, 104 + PE_CH:105 + PE_CH])\
                .then_inc(dconv_out, 1)
            for hf in range(2):
                act.wait_ge(centred, hf + 1)
                nc.scalar.activation(ysq[:, 4 * hf:4 * hf + 4, :], ycv[:, 4 * hf:4 * hf + 4, :], ACT.Square)\
                    .then_inc(squared, 1)
            for i in range(2):
                split_unit(CONV_OUT + i)
            act.wait_ge(cvar, 1)
            nc.scalar.activation(cst[:, 2, :], cst[:, 1, :], ACT.Sqrt).then_inc(cdev, 1)
            for hf in range(2):
                act.wait_ge(normed, hf + 1)
                for ch in range(4 * hf, 4 * hf + 4):
                    op = nc.scalar.activation(ysq[:, ch, :], ycv[:, ch, :], ACT.Silu,
                                              bias=vcols[:, 120 + ch:121 + ch], scale=vcols[:, 112 + ch:113 + ch])
                op.then_inc(cact, 1)
            for i in range(2, 4):
                split_unit(CONV_OUT + i)
            next_stage(0, FFN)

            def ffn_unit(u):
                if u >= 2:
                    split_unit(FFN + u)

            def ada_between(u):
                if u % 2 and 0 <= (u - 3) // 2 < ADB and u >= 3:
                    ada_copy(ADB + (u - 3) // 2, 6)

            swiglu(2 * FFN, 0, NT, ffn_unit, f_sil, hid_hi, ada_between)
            next_stage(1, SGU)

            def gelu(q):
                act.wait_ge(zb_out, q + 1)
                z = vv if q < 4 else uu
                nc.scalar.activation(z[:, :, (q % 4) * BANK:(q % 4 + 1) * BANK],
                                     z[:, :, (q % 4) * BANK:(q % 4 + 1) * BANK], ACT.Gelu).then_inc(gelu_out, 1)

            for i in range(2, 18):
                split_unit(SGU + i)
                if i % 2:
                    gelu((i - 3) // 2)
                if i in (10, 12):
                    t = (i - 10) // 2
                    act.wait_ge(vvar, t + 1)
                    nc.scalar.activation(dev[:, t:t + 1], var[:, t:t + 1], ACT.Sqrt).then_inc(vdev, 1)
            for r in range(8):
                t, m = r % 2, r // 2
                act.wait_ge(uT_ps, r + 1)
                nc.scalar.activation(uT_hi[:, 4 * m:4 * m + 4, tok(t)],
                                     ps[:, XB[t] + m % 2, :].rearrange("p (k n) -> p k n", k=4), ACT.Copy)\
                    .then_inc(uT_hi_out, 1)
            for m in range(2, HC // 2):
                split_unit(SGU_OUT + m)

            def split_moe(i, u):
                for s in range(2):
                    act.wait_ge(half_used, i * (2 * FFU) + (2 * (MOE + u) + s - 3))
                    split(u % SLOTS, i * (16 * FFU // SLOTS) + 16 * ((MOE_AT + u) // SLOTS + 1), None,
                          (2 * u + s) % 4, s == 0)

            split_moe(0, 0)
            deviation(2, 0)
            split_moe(0, 1)
            modulate(3, ab[:, 2, 0, :], ab[:, 2, 1, :], (0,))
            deviation(2, 1)
            modulate(3, ab[:, 2, 0, :], ab[:, 2, 1, :], (1,), KC // 2)
            act.wait_ge(mdif, 1)
            nc.scalar.activation(tgate[:, :, 0:1], tdif[:, :, :], ACT.Sigmoid, scale=-1.0).then_inc(mgate, 1)
            nc.scalar.activation(tgate[:, :, 1:2], tdif[:, :, :], ACT.Sigmoid).then_inc(mgate, 1)

            def modulate_item(chunks=KC):
                for k in range(chunks):
                    op = nc.scalar.activation(xe32[:, k, :], ps[:, PB[k // 3], (k % 3) * CAP:(k % 3) * CAP + P],
                                              ACT.Identity, bias=ab[:, 2, 1, k:k + 1], scale=ab[:, 2, 0, k:k + 1])
                op.then_inc(xe32_out, 1)

            act.wait_ge(picked_ps, 1)
            modulate_item(3)

            def expert(i, first):
                def unit(u):
                    if u >= first:
                        split_moe(i, u)

                def between(u):
                    if u == 6:
                        act.wait_ge(ggT_ps, i + 1)
                        nc.scalar.activation(ggT[:, :, :], ps[:, 6, :].rearrange("p (t n) -> p t n", t=2 * NT),
                                             ACT.Copy).then_inc(ggT_out, 1)
                    if u == INU + 5:
                        act.wait_ge(picked_ps, i + 2)
                        modulate_item()
                        act.wait_ge(xe32_out, i + 2)
                        nc.scalar.activation(xe_hi[:, :, :], xe32[:, :, :], ACT.Copy).then_inc(xe_hi_out, 1)

                swiglu(i * (2 * FFU) + 2 * MOE, i * NJ + NJ, 1, unit, e_sil, eh_hi, between)

            expert(0, 2)
            act.wait_ge(meta_ready, 1)
            items = act.value_load(metai[0:1, 4:5], min_val=E, max_val=NCOL - 1)
            with act.Fori(1, items) as i:
                expert(i, 0)
            act.wait_ge(var_ready, 7)
            nc.scalar.activation(dev[:, 0:1], var[:, 0:1], ACT.Sqrt).then_inc(dev_ready, 1)
            act.wait_ge(var_ready, 8)
            nc.scalar.activation(dev[:, 1:2], var[:, 1:2], ACT.Sqrt).then_inc(dev_ready, 1)

        @block.vector
        def _(dve):
            steps = [0]

            def link(ins):
                steps[0] += 1
                ins.then_inc(dve_step, 1)
                dve.wait_ge(dve_step, steps[0])

            def split_unit(n):
                for s in range(2):
                    h = 2 * n + s
                    dve.wait_ge(hi_ready, h + 1)
                    if h >= 4:
                        dve.wait_ge(half_used, h - 3)
                    nc.vector.tensor_tensor(w_lo[:, h % 4, :],
                                            ring[:, split_at[n] % SLOTS, s * HALF:(s + 1) * HALF],
                                            w_hi[:, h % 4, :].bitcast(F32), ALU.subtract).then_inc(lo_ready, 1)

            def ada_take(n, bank):
                layer, b = n // ADB, n % ADB
                dve.wait_ge(ada_sums, n + 1)
                if b // 2 in (2, 5):
                    row = g1row[:, :] if b // 2 == 2 else g2row[:, layer, :]
                    row = row[:, (b % 2) * BANK:(b % 2 + 1) * BANK]
                    dve.wait_ge(gb_landed, 64 if layer else 48)
                    op = nc.vector.scalar_tensor_tensor(out=row, in0=ps[:, bank, :], scalar=1.0, in1=row,
                                                        op0=ALU.add, op1=ALU.add)
                else:
                    op = nc.vector.tensor_tensor(mods[:, layer, b // 2, 4 * (b % 2):4 * (b % 2) + 4],
                                                 ps[:, bank, 4 * b:4 * b + 4],
                                                 modb[:, 48 * layer + 4 * b:48 * layer + 4 * b + 4], ALU.add)
                op.then_inc(ada_out, 1)

            def modulate(q, t, gain, shift):
                dve.wait_ge(xT_ps, 2 * q + t + 1)
                for k in range(KC // 2, KC):
                    op = nc.vector.tensor_scalar(h32[:, k, tok(t)], ps[:, XB[t] + 1, (k % 4) * P:(k % 4 + 1) * P],
                                                 gain[:, k:k + 1], shift[:, k:k + 1], ALU.mult, ALU.add)
                op.then_inc(h32_dve, 1)

            def split_h(q, t):
                dve.wait_ge(h32_out, 2 * q + t + 1)
                link(nc.vector.tensor_copy(hT_hi[:, :, tok(t)], h32[:, :, tok(t)]))
                nc.vector.tensor_tensor(hT_lo[:, :, tok(t)], h32[:, :, tok(t)],
                                        hT_hi[:, :, tok(t)].bitcast(F32), ALU.subtract).then_inc(h_ready, 1)

            def merge(q, layer, sh, sc):
                link(nc.vector.tensor_tensor(ab[:, q, 0, :], lncols[:, 0, q, :], mods[:, layer, sc, :], ALU.mult))
                link(nc.vector.tensor_tensor(ab[:, q, 1, :], lncols[:, 1, q, :], mods[:, layer, sc, :], ALU.mult))
                nc.vector.tensor_tensor(ab[:, q, 1, :], ab[:, q, 1, :], mods[:, layer, sh, :], ALU.add)\
                    .then_inc(ab_ready, 1)

            def variance(t, row, width, ready):
                n = width // BANK
                for k in range(n):
                    op = nc.vector.bn_stats(stats[:, t, k, :], row[:, k * BANK:(k + 1) * BANK])
                link(op)
                link(nc.vector.bn_aggr(mv[:, t, :], stats[:, t, 0:n, :].rearrange("p a b -> p (a b)")))
                nc.vector.tensor_scalar(var[:, t:t + 1], mv[:, t, 1:2], 1e-5, None, ALU.add).then_inc(ready, 1)

            def standardise(t, row, out_row, ready, count):
                dve.wait_ge(ready, count)
                link(nc.vector.reciprocal(rstd[:, t:t + 1], dev[:, t:t + 1]))
                return nc.vector.tensor_scalar(out_row, row, mv[:, t, 0:1], rstd[:, t:t + 1], ALU.subtract, ALU.mult)

            def residual(q, t, grow):
                if t == 0:
                    dve.wait_ge(y_done, q + 1)
                else:
                    dve.wait_ge(half_used, 2 * (FFN, SGU, MOE)[q])
                ztmp = ztmp_late if q == 2 else ztmp_early
                y = ps[:, YB[t]:YB[t] + 2, :].rearrange("p a b -> p (a b)")
                link(nc.vector.tensor_tensor(ztmp[:, t, :], y, grow, ALU.mult))
                if q:
                    dve.wait_ge(rows_used, NT * (q - 1) + t + 1)
                link(nc.vector.scalar_tensor_tensor(out=xs[:, t, :], in0=xs[:, t, :], scalar=ALPHA,
                                                    in1=ztmp[:, t, :], op0=ALU.mult, op1=ALU.add))
                variance(t, xs[:, t, :], D, var_ready)

            def next_stage(q, grow, n):
                residual(q, 0, grow)
                standardise(0, xs[:, 0, :], xs[:, 0, :], dev_ready, 2 * q + 1).then_inc(x_ready, 1)
                residual(q, 1, grow)
                split_h(q + 1, 0)
                standardise(1, xs[:, 1, :], xs[:, 1, :], dev_ready, 2 * q + 2).then_inc(x_ready, 1)
                dve.wait_ge(lo_ready, 2 * n + 2)
                split_unit(n + 1)
                split_h(q + 1, 1)

            def swiglu(h0, c0, nt, unit, sil, hid, e_hi, e_lo, after):
                for u in range(FFU):
                    unit(u)
                    if u % 4 == 1 and 5 <= u <= INU + 1:
                        j = (u - 5) // 4
                        dve.wait_ge(half_used, h0 + 2 * (4 * j + 4))
                        dve.wait_ge(silu_out, c0 + (j + 1))
                        dve.wait_ge(hidT_ps, c0 + j)
                        op = nc.vector.tensor_tensor(hid[:, 0:nt, :], ps[:, 2:2 + nt, :], sil[:, 0:nt, :], ALU.mult)
                        if nt == 1:
                            op = nc.vector.tensor_tensor(hidx[:, :], ps[:, 3, 0:P], silx[:, :], ALU.mult)
                        op.then_inc(hid_out, 1)
                    if u % 4 == 3 and 7 <= u <= INU + 3:
                        j = (u - 7) // 4
                        dve.wait_ge(hidT_hi, c0 + (j + 1))
                        for t in range(nt):
                            op = nc.vector.tensor_tensor(e_lo[:, 4 * j:4 * j + 4, tok(t)],
                                                         ps[:, 4 + t, :].rearrange("p (k n) -> p k n", k=4),
                                                         e_hi[:, 4 * j:4 * j + 4, tok(t)].bitcast(F32), ALU.subtract)
                        op.then_inc(hidT_lo, 1)
                    after(u)

            nc.vector.memset(ypad[:, :, 0:PADL], 0.0).then_inc(pad_zero, 1)
            dve.wait_ge(pool_step, 5)
            nc.vector.tensor_copy(iota[:, :], iota_i[:, :]).then_inc(iota_ready, 1)
            for r in range(0, P, 32):
                nc.vector.memset(sel4[r:r + 1, :], 1.0).then_inc(consts, 1)
            dve.wait_ge(vec_ps, 1)
            nc.vector.tensor_copy(vcols[:, :], ps[:, 6, 0:P]).then_inc(vec_out, 1)
            link(nc.vector.tensor_copy(lncols[:, :, :, :], ps[:, 6, P:P + 48].rearrange("p (v q k) -> p v q k", v=2, q=3)))
            dve.wait_ge(vec_ps, 2)
            nc.vector.tensor_copy(dwT[:, :, :], ps[:, 5, 0:KC * TAPS].rearrange("p (c k) -> p c k", c=KC))\
                .then_inc(vec_out, 1)
            nc.vector.tensor_copy(bsT[:, :], ps[:, 5, 256:256 + G]).then_inc(vec_out, 1)
            dve.wait_ge(vec_out, 3)
            link(nc.vector.tensor_copy(modb[:, :], vcols[:, 0:96]))
            for layer in range(2):
                for seg in (1, 4):
                    col = modb[:, 48 * layer + 8 * seg:48 * layer + 8 * seg + 8]
                    op = nc.vector.tensor_scalar(col, col, 1.0, None, ALU.add)
            link(op)
            for n in range(4):
                ada_take(n, 7)
            dve.wait_ge(ada_out, 4)
            for t in range(NT):
                modulate(0, t, mods[:, 0, 1, :], mods[:, 0, 0, :])
            for t in range(NT):
                dve.wait_ge(h32_dve, t + 1)
                split_h(0, t)
            split_unit(0)
            split_unit(1)

            def glu(blk):
                dve.wait_ge(sig_out, blk + 1)
                dve.wait_ge(half_used, 8 * blk + 8)
                nc.vector.tensor_tensor(ypad[:, 4 * blk:4 * blk + 4, PADL:], ps[:, 4:8, 0:S], sig[:, :, :],
                                        ALU.mult).then_inc(glu_out, 1)

            def taps(channels, first, last):
                for k in range(first, last):
                    for ch in channels:
                        src, w = ypad[:, ch, k:k + S], dwT[:, ch, k:k + 1]
                        if k == 0:
                            op = nc.vector.tensor_scalar(ycv[:, ch, :], src, w, vcols[:, 104 + ch:105 + ch],
                                                         ALU.mult, ALU.add)
                        else:
                            dve.wait_ge(dve_step, tap_step[ch])
                            op = nc.vector.scalar_tensor_tensor(out=ycv[:, ch, :], in0=src, scalar=w,
                                                                in1=ycv[:, ch, :], op0=ALU.mult, op1=ALU.add)
                        steps[0] += 1
                        op.then_inc(dve_step, 1)
                        tap_step[ch] = steps[0]

            def taps_done(channels):
                dve.wait_ge(dve_step, max(tap_step[ch] for ch in channels))
                nc.vector.memset(cst[:, 3, 0:1], 0.0).then_inc(taps_out, len(channels))

            tap_step = {}
            for i in range(2, 6):
                split_unit(i)
            glu(0)
            dve.wait_ge(glu_out, 1)
            dve.wait_ge(pad_zero, 1)
            taps((0, 1), 0, 4)
            split_unit(6)
            taps((0, 1), 4, 8)
            split_unit(7)
            taps((0, 1), 8, 12)
            glu(1)
            dve.wait_ge(glu_out, 2)
            taps((0, 1), 12, 20)
            ada_take(4, 1 + 4 % 3)
            taps((0, 1), 20, TAPS)
            ada_take(5, 1 + 5 % 3)
            taps_done((0, 1))
            for n in range(6, ADB):
                k = TAPS * (n - 6) // 6
                taps((4, 5, 6), k, TAPS * (n - 5) // 6)
                ada_take(n, 1 + n % 3)
            taps_done((4, 5, 6))
            dve.wait_ge(ada_out, ADB)
            merge(0, 0, 3, 4)
            dve.wait_ge(mean_ps, 1)
            link(nc.vector.tensor_scalar(cst[:, 0, :], ps[:, 4, 0:S], 1.0 / D, None, ALU.mult))
            for hf in range(2):
                part = ycv[:, 4 * hf:4 * hf + 4, :]
                nc.vector.tensor_tensor(part, part, cst[:, 0:1, :].broadcast_to([P, 4, S]), ALU.subtract)\
                    .then_inc(centred, 1)
            for i in range(2):
                split_unit(CONV_OUT + i)
            dve.wait_ge(var_ps, 1)
            nc.vector.tensor_scalar(cst[:, 1, :], ps[:, 5, 0:S], 1.0 / D, 1e-5, ALU.mult, ALU.add).then_inc(cvar, 1)
            dve.wait_ge(cdev, 1)
            dve.wait_ge(centred, 2)
            link(nc.vector.reciprocal(cst[:, 3, :], cst[:, 2, :]))
            for hf in range(2):
                part = ycv[:, 4 * hf:4 * hf + 4, :]
                nc.vector.tensor_tensor(part, part, cst[:, 3:4, :].broadcast_to([P, 4, S]), ALU.mult)\
                    .then_inc(normed, 1)
            for hf in range(2):
                part = slice(4 * hf, 4 * hf + 4)
                dve.wait_ge(cact, hf + 1)
                link(nc.vector.tensor_copy(y_hi[:, part, :], ysq[:, part, :]))
                nc.vector.tensor_tensor(y_lo[:, part, :], ysq[:, part, :], y_hi[:, part, :].bitcast(F32),
                                        ALU.subtract).then_inc(y_ready, 1)
            for i in range(2, 4):
                split_unit(CONV_OUT + i)
            next_stage(0, g1row[:, :], FFN)

            def ffn_unit(u):
                if u >= 2:
                    split_unit(FFN + u)

            def ada_between(u):
                if u % 2 == 0 and u >= 4 and (u - 4) // 2 < ADB:
                    ada_take(ADB + (u - 4) // 2, 7)
                if u == INU + 2:
                    dve.wait_ge(ada_out, 2 * ADB)
                    merge(1, 1, 0, 1)
                    merge(2, 1, 3, 4)

            swiglu(2 * FFN, 0, NT, ffn_unit, f_sil, f_hid, hid_hi, hid_lo, ada_between)
            next_stage(1, g2row[:, 0, :], SGU)

            def add_bias(q):
                dve.wait_ge(half_used, 2 * (SGU + 2 * q + 2))
                dve.wait_ge(brow_landed[q % 2], 16 * (q // 2 + 1))
                z = vv if q < 4 else uu
                for t in range(NT):
                    op = nc.vector.tensor_tensor(z[:, t, (q % 4) * BANK:(q % 4 + 1) * BANK],
                                                 ps[:, 2 * (q % 2) + t, :], brow[:, q % 2, :], ALU.add)
                op.then_inc(zb_out, 1)

            for i in range(2, 18):
                split_unit(SGU + i)
                if i % 2:
                    add_bias((i - 3) // 2)
                if i in (10, 12):
                    t = (i - 10) // 2
                    dve.wait_ge(gelu_out, 4)
                    variance(t, vv[:, t, :], HS, vvar)
                    standardise(t, vv[:, t, :], vv[:, t, :], vdev, t + 1).then_inc(v_normed, 1)
            for t in range(NT):
                dve.wait_ge(sv_ps, t + 1)
                dve.wait_ge(gelu_out, 8)
                for g in range(G):
                    u_g = uu[:, t, g * GW:(g + 1) * GW]
                    op = nc.vector.scalar_tensor_tensor(
                        out=u_g, in0=ps[:, (0 if t else 4) + g // 2, (g % 2) * GW:(g % 2 + 1) * GW],
                        scalar=bsT[:, g:g + 1], in1=u_g, op0=ALU.add, op1=ALU.mult)
                op.then_inc(gated, 1)
            for r in range(8):
                t, m = r % 2, r // 2
                dve.wait_ge(uT_hi_out, r + 1)
                nc.vector.tensor_tensor(uT_lo[:, 4 * m:4 * m + 4, tok(t)],
                                        ps[:, XB[t] + m % 2, :].rearrange("p (k n) -> p k n", k=4),
                                        uT_hi[:, 4 * m:4 * m + 4, tok(t)].bitcast(F32), ALU.subtract)\
                    .then_inc(uT_lo_out, 1)
            for m in range(2, HC // 2):
                split_unit(SGU_OUT + m)

            def split_moe(i, u):
                for s in range(2):
                    hb = (2 * u + s) % 4
                    dve.wait_ge(hi_ready, i * (2 * FFU) + (2 * (MOE + u) + s + 1))
                    dve.wait_ge(half_used, i * (2 * FFU) + (2 * (MOE + u) + s - 3))
                    nc.vector.tensor_tensor(w_lo[:, hb, :], ring[:, u % SLOTS, s * HALF:(s + 1) * HALF],
                                            w_hi[:, hb, :].bitcast(F32), ALU.subtract).then_inc(lo_ready, 1)

            for t in range(NT):
                residual(2, t, g1row[:, :])
                standardise(t, xs[:, t, :], xs[:, t, :], dev_ready, 4 + t + 1).then_inc(x_ready, 1)
            dve.wait_ge(ab_ready, 3)
            modulate(3, 1, ab[:, 2, 0, :], ab[:, 2, 1, :])
            for u in range(2):
                split_moe(0, u)
            for a, v in ((over, 0.0), (dest, -1.0), (gcol, 0.0)):
                nc.vector.memset(a[:, :, :], v)
            nc.vector.memset(meta[:, :], 0.0)
            nc.vector.memset(ye[:, :], 0.0)
            nc.vector.memset(yex[:, :], 0.0)
            link(nc.vector.memset(ggT[:, :, :], 0.0))

            dve.wait_ge(logit_ps, 2)
            dve.wait_ge(iota_ready, 1)
            link(nc.vector.tensor_copy(lgt[:, :, :], ps[:, 6, 0:NT * E].rearrange("p (t e) -> p t e", t=NT)))
            for t in range(NT):
                op = nc.vector.max(top[:, t, :], lgt[:, t, :])
            link(op)
            nc.vector.tensor_tensor(tdif[:, :, :], top[:, :, 1:2], top[:, :, 0:1], ALU.subtract).then_inc(mdif, 1)
            for t in range(NT):
                op = nc.vector.max_index(topi[:, t, :], top[:, t, :], lgt[:, t, :])
            link(op)
            link(nc.vector.tensor_copy(topf[:, :, :], topi[:, :, :]))
            for t in range(NT):
                nc.vector.tensor_scalar(mask1[:, t, :], iota[:, 0:E], topf[:, t, 0:1], None, ALU.is_equal)
                op = nc.vector.tensor_scalar(mask2[:, t, :], iota[:, 0:E], topf[:, t, 1:2], None, ALU.is_equal)
            link(op)
            nc.vector.tensor_tensor(mask[:, :, :], mask1[:, :, :], mask2[:, :, :], ALU.add).then_inc(mask_ready, 1)
            dve.wait_ge(mgate, 2)
            for t in range(NT):
                op = nc.vector.tensor_scalar(gate1[:, t, :], mask1[:, t, :], tgate[:, t, 0:1], None, ALU.mult)
            link(op)
            for t in range(NT):
                op = nc.vector.scalar_tensor_tensor(out=gate[:, t, :], in0=mask2[:, t, :], scalar=tgate[:, t, 1:2],
                                                    in1=gate1[:, t, :], op0=ALU.mult, op1=ALU.add)
            dve.wait_ge(rank_ps, 1)
            dve.wait_ge(mask_ready, 1)
            for t in range(NT):
                op = nc.vector.scalar_tensor_tensor(out=rank1[:, t, :], in0=ps[:, 7, t * E:(t + 1) * E], scalar=1.0,
                                                    in1=mask[:, t, :], op0=ALU.add, op1=ALU.mult)
            link(op)
            nc.vector.tensor_scalar(dest[:, :, 0:E], rank1[:, :, :], 1.0, None, ALU.subtract)
            link(nc.vector.tensor_copy(gcol[:, :, 0:E], gate[:, :, :]))
            def choose(item):
                line = iota[:, :].unsqueeze(1).broadcast_to([P, NT, CAP])
                nc.vector.tensor_tensor(oneh[:, :, :], line, dest[:, :, item].broadcast_to([P, NT, CAP]),
                                        ALU.is_equal).then_inc(oneh_out, 1)

            def modulate_extra(step, n):
                dve.wait_ge(xe32_out, n)
                gain, shift = (ab[:, 2, v, :].unsqueeze(2).broadcast_to([P, KC, XS]) for v in range(2))
                for b in range(3):
                    k = slice(3 * b, min(3 * b + 3, KC))
                    picked = ps[:, PB[b], 0:(k.stop - k.start) * CAP].rearrange("p (k n) -> p k n", n=CAP)
                    op = nc.vector.tensor_tensor(xx[:, k, :], picked[:, :, P:CAP], gain[:, k, :], ALU.mult)
                step(op)
                nc.vector.tensor_tensor(xx[:, :, :], xx[:, :, :], shift, ALU.add).then_inc(xe_ready, 1)

            def take_rows():
                for g in range(4):
                    q, cols = slice(32 * g, 32 * g + 32), slice(g * (D // 4), (g + 1) * (D // 4))
                    nc.vector.tensor_tensor(yex[q, cols], ps[q, 3, 0:D // 4], g2row[q, 1, cols], ALU.mult)
                nc.vector.tensor_tensor(ye[:, :], ps[:, 6:8, :].rearrange("p a b -> p (a b)"), g2row[:, 1, :],
                                        ALU.mult).then_inc(ye_ready, 1)

            def add_rows(t):
                a = acc[:, t, :]
                nc.vector.tensor_tensor(a, ps[:, SB[t]:SB[t] + 2, :].rearrange("p a b -> p (a b)"), a, ALU.add)\
                    .then_inc(acc_out, 1)

            choose(slice(0, 1))
            nc.vector.tensor_scalar(meta[:, XF + 1:XF + 1 + E], ps[:, 7, 2 * E:3 * E], float(P), None, ALU.is_gt)
            link(nc.vector.tensor_scalar(over[:, 0, E:], ps[:, 7, 2 * E:3 * E], float(CAP), None, ALU.is_gt))
            nc.vector.tensor_scalar(excess[:, :, :], rank1[:, :, :], float(CAP), 0.0, ALU.subtract, ALU.max)
            for s in range(3):
                link(nc.vector.tensor_tensor(over[:, s + 1, E:], over[:, s, E:], over[:, s, E - 2 ** s:2 * E - 2 ** s],
                                             ALU.add))
            nc.vector.tensor_scalar(meta[:, 4:5], over[:, 3, 2 * E - 1:2 * E], float(E), None, ALU.add)
            link(nc.vector.tensor_tensor(before[:, :], over[:, 3, E:], over[:, 0, E:], ALU.subtract))
            for m in range(3):
                op = nc.vector.scalar_tensor_tensor(out=oh[:, m, :], in0=before[:, :], scalar=float(m),
                                                    in1=over[:, 0, E:], op0=ALU.is_equal, op1=ALU.mult)
            link(op)
            for m in range(3):
                op = nc.vector.tensor_tensor_reduce(junk[:, 5 * m, :], oh[:, m, :], iota[:, 0:E], 1.0, 0.0, ALU.mult,
                                                    ALU.add, meta[:, m:m + 1])
            link(op)
            nc.vector.tensor_copy(metai[:, :], meta[:, :]).then_inc(meta_ready, 1)
            dve.wait_ge(picked_ps, 1)
            for k in range(3, KC):
                nc.vector.tensor_scalar(xe32[:, k, :], ps[:, PB[k // 3], (k % 3) * CAP:(k % 3) * CAP + P],
                                        ab[:, 2, 0, k:k + 1], ab[:, 2, 1, k:k + 1], ALU.mult, ALU.add)\
                    .then_inc(xe32_dve, 1)
            modulate_extra(link, 1)
            dve.wait_ge(xe32_dve, KC - 3)
            link(nc.vector.tensor_copy(xe_hi[:, :, :], xe32[:, :, :]))
            nc.vector.tensor_tensor(xe_lo[:, :, :], xe32[:, :, :], xe_hi[:, :, :].bitcast(F32), ALU.subtract)\
                .then_inc(xe_ready, 1)
            for m in range(3):
                for t in range(NT):
                    nc.vector.tensor_tensor_reduce(junk[:, 5 * m + 1 + 2 * t, :], oh[:, m, :], excess[:, t, :], 1.0,
                                                   -1.0, ALU.mult, ALU.add, dest[:, t, E + m:E + m + 1])
                    op = nc.vector.tensor_tensor_reduce(junk[:, 5 * m + 2 + 2 * t, :], oh[:, m, :], gate[:, t, :], 1.0,
                                                        0.0, ALU.mult, ALU.add, gcol[:, t, E + m:E + m + 1])
            link(op)
            dve.wait_ge(rows_used, 3 * NT)
            link(nc.vector.tensor_scalar(acc[:, :, :], acc[:, :, :], ALPHA, None, ALU.mult))
            TURN = 1

            def expert(i, first):
                turn = [0]

                def step(ins):
                    turn[0] += 1
                    ins.then_inc(dve_turn, 1)
                    dve.wait_ge(dve_turn, i * TURN + turn[0])

                def unit(u):
                    if u >= first:
                        split_moe(i, u)

                def between(u):
                    if u == 1:
                        dve.wait_ge(half_used, i * (2 * FFU) + 2 * MOE)
                        take_rows()
                    if u == 3:
                        dve.wait_ge(spread_ps, i * NT + NT)
                        for t in range(NT):
                            add_rows(t)
                    if u == INU - 1:
                        dve.wait_ge(ggT_ps, i + 1)
                        choose(bass.ds(i + 1, 1))
                    if u == INU + 5:
                        modulate_extra(step, i + 2)

                swiglu(i * (2 * FFU) + 2 * MOE, i * NJ + NJ, 1, unit, e_sil, e_hid, eh_hi, eh_lo, between)
                assert turn[0] == TURN

            expert(0, 2)
            dve.wait_ge(meta_ready, 1)
            items = dve.value_load(metai[0:1, 4:5], min_val=E, max_val=NCOL - 1)
            with dve.Fori(1, items) as i:
                expert(i, 0)
            dve.wait_ge(half_used, items * (2 * FFU) + 2 * MOE)
            take_rows()
            for t in range(NT):
                dve.wait_ge(spread_ps, items * NT + (t + 1))
                add_rows(t)
                dve.wait_ge(acc_out, items * NT + (t + 1))
                variance(t, acc[:, t, :], D, var_ready)
            dve.wait_ge(rows_landed, 128)
            for t in range(NT):
                link(nc.vector.scalar_tensor_tensor(out=xs[:, t, :], in0=acc[:, t, :], scalar=mv[:, t, 0:1],
                                                    in1=lng[:, :], op0=ALU.subtract, op1=ALU.mult))
                dve.wait_ge(dev_ready, 6 + t + 1)
                link(nc.vector.reciprocal(rstd[:, t:t + 1], dev[:, t:t + 1]))
                nc.vector.scalar_tensor_tensor(out=xs[:, t, :], in0=xs[:, t, :], scalar=rstd[:, t:t + 1],
                                               in1=lnb[:, :], op0=ALU.mult, op1=ALU.add).then_inc(x_ready, 1)


_INS = ["x", "c", "ada_w", "ada_b", "ln_g", "ln_b", "conv_w_in", "conv_dw", "conv_dw_b", "conv_ln_g", "conv_ln_b",
        "conv_w_out", "sgu_w_in", "sgu_b_in", "sgu_ln_g", "sgu_ln_b", "sgu_w_s", "sgu_b_s", "sgu_w_out",
        "ffn_w_in", "ffn_w_out", "moe_router", "moe_w_in", "moe_w_out"]


def kernel(**inputs):
    import numpy as _np
    import concourse.bacc as _bacc
    from concourse import mybir as _mybir
    from concourse.bass_utils import run_bass_kernel_spmd as _run

    nc = _bacc.Bacc("TRN2", target_bir_lowering=False, num_devices=1)
    arrays, args = {}, []
    for name in _INS:
        a = _np.ascontiguousarray(inputs[name])
        arrays[f"in_{name}"] = a
        args.append(nc.dram_tensor(f"in_{name}", a.shape, _mybir.dt.from_np(a.dtype), kind="ExternalInput").ap())
    shape = inputs["x"].shape
    out = nc.dram_tensor("out_x", shape, _mybir.dt.float32, kind="ExternalOutput").ap()
    hybrid_trunk(nc, *args, out)
    r = _run(nc, [arrays], core_ids=[0])
    return r.results[0]["out_x"]
```
